# Optimizing a Trainium2 kernel written in Bass

```python
import math
import jax, jax.numpy as jnp
from jax import lax
import numpy as np

D_MODEL = 1024
BATCH = 1
SEQ = 256
DEPTH = 4

N_MIXERS = 3
HEAD_DIM = 64
ROT_DIM = HEAD_DIM // 4
ROPE_THETA = 500000.0
NORM_EPS = 1e-6
D_FF = 4 * D_MODEL

DIFF_HEADS = D_MODEL // (2 * HEAD_DIM)
DIFF_QK_WIDTH = DIFF_HEADS * 2 * HEAD_DIM
DIFF_V_DIM = 2 * HEAD_DIM
DIFF_IN = 2 * DIFF_QK_WIDTH + DIFF_HEADS * DIFF_V_DIM
DENSE_Q_BLOCK = 128

MOBA_HEADS = D_MODEL // HEAD_DIM
MOBA_BLOCK = 256
MOBA_TOPK = 3
MOBA_Q_CHUNK = 32
MOBA_IN = 3 * MOBA_HEADS * HEAD_DIM

SWA_HEADS = D_MODEL // HEAD_DIM
SWA_KV_HEADS = SWA_HEADS // 8
SWA_WINDOW = 128
SWA_Q_BLOCK = SWA_WINDOW
SWA_IN = (SWA_HEADS + 2 * SWA_KV_HEADS) * HEAD_DIM

N_DIFF = (DEPTH + 2) // 3
N_MOBA = (DEPTH + 1) // 3
N_SWA = DEPTH // 3


def rms_norm(x, g):
    xf = x.astype(jnp.float32)
    y = xf * lax.rsqrt(jnp.mean(xf * xf, axis=-1, keepdims=True) + NORM_EPS)
    return (y * g.astype(jnp.float32)).astype(x.dtype)

def rope_tables(positions):
    inv = ROPE_THETA ** (-jnp.arange(0, ROT_DIM, 2, dtype=jnp.float32) / ROT_DIM)
    ang = positions.astype(jnp.float32)[..., None] * inv
    return jnp.cos(ang), jnp.sin(ang)

def apply_partial_rope(x, cos, sin):
    half = ROT_DIM // 2
    c = cos[:, :, None, :].astype(x.dtype)
    s = sin[:, :, None, :].astype(x.dtype)
    x1 = x[..., :half]
    x2 = x[..., half:ROT_DIM]
    return jnp.concatenate([x1 * c - x2 * s, x2 * c + x1 * s, x[..., ROT_DIM:]], axis=-1)

def diff_attention(h, w_in, w_out, lam_q1, lam_k1, lam_q2, lam_k2, sub_g, cos, sin, lambda_init):
    B, S, _ = h.shape
    H = DIFF_HEADS
    qkv = h @ w_in
    q, k, v = jnp.split(qkv, [DIFF_QK_WIDTH, 2 * DIFF_QK_WIDTH], axis=-1)
    q = apply_partial_rope(q.reshape(B, S, 2 * H, HEAD_DIM), cos, sin) * (HEAD_DIM ** -0.5)
    k = apply_partial_rope(k.reshape(B, S, 2 * H, HEAD_DIM), cos, sin)
    q = q.reshape(B, S, H, 2, HEAD_DIM)
    k = k.reshape(B, S, H, 2, HEAD_DIM)
    v = v.reshape(B, S, H, DIFF_V_DIM)
    f32 = jnp.float32
    lam = (jnp.exp(jnp.sum(lam_q1.astype(f32) * lam_k1.astype(f32)))
           - jnp.exp(jnp.sum(lam_q2.astype(f32) * lam_k2.astype(f32))) + lambda_init)
    nqb = S // DENSE_Q_BLOCK
    qb = q.reshape(B, nqb, DENSE_Q_BLOCK, H, 2, HEAD_DIM).transpose(1, 0, 2, 3, 4, 5)
    key_pos = jnp.arange(S)

    def block(args):
        qi, blk = args
        q_pos = blk * DENSE_Q_BLOCK + jnp.arange(DENSE_Q_BLOCK)
        s = jnp.einsum('bqhcd,bkhcd->bhcqk', qi, k).astype(f32)
        causal = key_pos[None, :] <= q_pos[:, None]
        s = jnp.where(causal, s, -jnp.inf)
        p = jax.nn.softmax(s, axis=-1)
        p = p[:, :, 0] - lam * p[:, :, 1]
        return jnp.einsum('bhqk,bkhe->bqhe', p.astype(v.dtype), v)

    o = lax.map(block, (qb, jnp.arange(nqb)))
    o = o.transpose(1, 0, 2, 3, 4).reshape(B, S, H, DIFF_V_DIM)
    o = rms_norm(o, sub_g) * (1.0 - lambda_init)
    return o.reshape(B, S, H * DIFF_V_DIM) @ w_out

def moba_attention(h, w_in, w_out, cos, sin):
    B, S, _ = h.shape
    H, D, Bk = MOBA_HEADS, HEAD_DIM, MOBA_BLOCK
    f32 = jnp.float32
    q, k, v = jnp.split(h @ w_in, 3, axis=-1)
    q = apply_partial_rope(q.reshape(B, S, H, D), cos, sin) * (D ** -0.5)
    k = apply_partial_rope(k.reshape(B, S, H, D), cos, sin)
    v = v.reshape(B, S, H, D)
    nb = -(-S // Bk)
    pad = nb * Bk - S
    k = jnp.pad(k, ((0, 0), (0, pad), (0, 0), (0, 0)))
    v = jnp.pad(v, ((0, 0), (0, pad), (0, 0), (0, 0)))
    K = min(MOBA_TOPK, nb)
    kb = k.reshape(B, nb, Bk, H, D).transpose(0, 3, 1, 2, 4)
    vb = v.reshape(B, nb, Bk, H, D).transpose(0, 3, 1, 2, 4)
    k_mean = jnp.mean(kb.astype(f32), axis=3).astype(k.dtype)
    nqc = S // MOBA_Q_CHUNK
    qc = q.reshape(B, nqc, MOBA_Q_CHUNK, H, D).transpose(1, 0, 3, 2, 4)
    b_idx = jnp.arange(B)[:, None, None, None]
    h_idx = jnp.arange(H)[None, :, None, None]
    blk_ids = jnp.arange(nb)
    in_blk = jnp.arange(Bk)

    def chunk(args):
        qi, ci = args
        q_pos = ci * MOBA_Q_CHUNK + jnp.arange(MOBA_Q_CHUNK)
        own = (ci * MOBA_Q_CHUNK) // Bk
        gate = jnp.einsum('bhqd,bhnd->bhqn', qi, k_mean).astype(f32)
        gate = jnp.where(blk_ids < own, gate, -jnp.inf)
        _, sel = lax.top_k(gate, K)
        valid = jnp.arange(K) < own
        ks = kb[b_idx, h_idx, sel]
        vs = vb[b_idx, h_idx, sel]
        s_sel = jnp.einsum('bhqd,bhqnkd->bhqnk', qi, ks).astype(f32)
        s_sel = jnp.where(valid[:, None], s_sel, -jnp.inf).reshape(B, H, MOBA_Q_CHUNK, K * Bk)
        k_own = lax.dynamic_index_in_dim(kb, own, axis=2, keepdims=False)
        v_own = lax.dynamic_index_in_dim(vb, own, axis=2, keepdims=False)
        s_own = jnp.einsum('bhqd,bhkd->bhqk', qi, k_own).astype(f32)
        own_pos = own * Bk + in_blk
        s_own = jnp.where(own_pos[None, :] <= q_pos[:, None], s_own, -jnp.inf)
        p = jax.nn.softmax(jnp.concatenate([s_sel, s_own], axis=-1), axis=-1).astype(v.dtype)
        p_sel = p[..., :K * Bk].reshape(B, H, MOBA_Q_CHUNK, K, Bk)
        p_own = p[..., K * Bk:]
        return (jnp.einsum('bhqnk,bhqnkd->bhqd', p_sel, vs)
                + jnp.einsum('bhqk,bhkd->bhqd', p_own, v_own))

    o = lax.map(chunk, (qc, jnp.arange(nqc)))
    o = o.transpose(1, 0, 3, 2, 4).reshape(B, S, H * D)
    return o @ w_out

def swa_sink_attention(h, w_in, b_in, sinks, w_out, cos, sin):
    B, S, _ = h.shape
    KV, D, Qb = SWA_KV_HEADS, HEAD_DIM, SWA_Q_BLOCK
    G = SWA_HEADS // KV
    f32 = jnp.float32
    qkv = h @ w_in + b_in
    q, k, v = jnp.split(qkv, [SWA_HEADS * D, (SWA_HEADS + KV) * D], axis=-1)
    q = apply_partial_rope(q.reshape(B, S, SWA_HEADS, D), cos, sin) * (D ** -0.5)
    k = apply_partial_rope(k.reshape(B, S, KV, D), cos, sin)
    v = v.reshape(B, S, KV, D)
    nb = S // Qb
    qb = q.reshape(B, nb, Qb, KV, G, D)
    kb = k.reshape(B, nb, Qb, KV, D)
    vb = v.reshape(B, nb, Qb, KV, D)
    pad_k = jnp.zeros_like(kb[:, :1])
    pad_v = jnp.zeros_like(vb[:, :1])
    k2 = jnp.concatenate([jnp.concatenate([pad_k, kb[:, :-1]], axis=1), kb], axis=2)
    v2 = jnp.concatenate([jnp.concatenate([pad_v, vb[:, :-1]], axis=1), vb], axis=2)
    s = jnp.einsum('bnqkgd,bnjkd->bnkgqj', qb, k2).astype(f32)
    qi = jnp.arange(Qb)[:, None] + Qb
    kj = jnp.arange(2 * Qb)[None, :]
    dist = qi - kj
    band = (dist >= 0) & (dist < SWA_WINDOW)
    prev_ok = (jnp.arange(nb)[:, None] > 0) | (jnp.arange(2 * Qb)[None, :] >= Qb)
    mask = band[None, :, :] & prev_ok[:, None, :]
    s = jnp.where(mask[None, :, None, None], s, -jnp.inf)
    sink = sinks.astype(f32).reshape(KV, G)[None, None, :, :, None, None]
    m = jnp.maximum(jnp.max(s, axis=-1, keepdims=True), sink)
    e = jnp.exp(s - m)
    p = (e / (jnp.sum(e, axis=-1, keepdims=True) + jnp.exp(sink - m))).astype(v.dtype)
    o = jnp.einsum('bnkgqj,bnjkd->bnqkgd', p, v2).reshape(B, S, SWA_HEADS * D)
    return o @ w_out

def sqrelu_mlp(h, w_up, w_down):
    a = jnp.maximum(h @ w_up, 0)
    return (a * a) @ w_down

def first_inputs(seed: int = 0) -> dict:
    key = jax.random.key(seed)
    ks = jax.random.split(key, 24)
    f32 = jnp.float32
    nrm = lambda k, shape, scale: jax.random.normal(k, shape, f32) * scale
    x = jax.random.normal(ks[0], (BATCH, SEQ, D_MODEL), f32)
    positions = jnp.broadcast_to(jnp.arange(SEQ, dtype=jnp.int32)[None, :], (BATCH, SEQ))
    return {
        "x": x,
        "positions": positions,
        "attn_norm_g": 1.0 + nrm(ks[1], (DEPTH, D_MODEL), 0.02),
        "mlp_norm_g": 1.0 + nrm(ks[2], (DEPTH, D_MODEL), 0.02),
        "diff_w_in": nrm(ks[3], (N_DIFF, D_MODEL, DIFF_IN), D_MODEL ** -0.5),
        "diff_w_out": nrm(ks[4], (N_DIFF, DIFF_HEADS * DIFF_V_DIM, D_MODEL), (DIFF_HEADS * DIFF_V_DIM) ** -0.5),
        "diff_lam_q1": nrm(ks[5], (N_DIFF, HEAD_DIM), 0.1),
        "diff_lam_k1": nrm(ks[6], (N_DIFF, HEAD_DIM), 0.1),
        "diff_lam_q2": nrm(ks[7], (N_DIFF, HEAD_DIM), 0.1),
        "diff_lam_k2": nrm(ks[8], (N_DIFF, HEAD_DIM), 0.1),
        "diff_subln_g": 1.0 + nrm(ks[9], (N_DIFF, DIFF_V_DIM), 0.02),
        "moba_w_in": nrm(ks[10], (N_MOBA, D_MODEL, MOBA_IN), D_MODEL ** -0.5),
        "moba_w_out": nrm(ks[11], (N_MOBA, MOBA_HEADS * HEAD_DIM, D_MODEL), (MOBA_HEADS * HEAD_DIM) ** -0.5),
        "swa_w_in": nrm(ks[12], (N_SWA, D_MODEL, SWA_IN), D_MODEL ** -0.5),
        "swa_b_in": nrm(ks[13], (N_SWA, SWA_IN), 0.02),
        "swa_sinks": nrm(ks[14], (N_SWA, SWA_HEADS), 0.5),
        "swa_w_out": nrm(ks[15], (N_SWA, SWA_HEADS * HEAD_DIM, D_MODEL), (SWA_HEADS * HEAD_DIM) ** -0.5),
        "mlp_w_up": nrm(ks[16], (DEPTH, D_MODEL, D_FF), D_MODEL ** -0.5),
        "mlp_w_down": nrm(ks[17], (DEPTH, D_FF, D_MODEL), 0.5 * D_FF ** -0.5),
        "final_norm_g": 1.0 + nrm(ks[18], (D_MODEL,), 0.02),
    }

def first_block(x, positions, attn_norm_g, mlp_norm_g, diff_w_in, diff_w_out, diff_lam_q1, diff_lam_k1,
              diff_lam_q2, diff_lam_k2, diff_subln_g, moba_w_in, moba_w_out, swa_w_in, swa_b_in,
              swa_sinks, swa_w_out, mlp_w_up, mlp_w_down, final_norm_g):
    cos, sin = rope_tables(positions)
    h = x
    for i in range(DEPTH):
        mixer = i % N_MIXERS
        slot = i // N_MIXERS
        a = rms_norm(h, attn_norm_g[i])
        if mixer == 0:
            lambda_init = 0.8 - 0.6 * math.exp(-0.3 * i)
            y = diff_attention(a, diff_w_in[slot], diff_w_out[slot], diff_lam_q1[slot], diff_lam_k1[slot],
                               diff_lam_q2[slot], diff_lam_k2[slot], diff_subln_g[slot], cos, sin, lambda_init)
        elif mixer == 1:
            y = moba_attention(a, moba_w_in[slot], moba_w_out[slot], cos, sin)
        else:
            y = swa_sink_attention(a, swa_w_in[slot], swa_b_in[slot], swa_sinks[slot], swa_w_out[slot], cos, sin)
        h = h + y
        h = h + sqrelu_mlp(rms_norm(h, mlp_norm_g[i]), mlp_w_up[i], mlp_w_down[i])
    return rms_norm(h, final_norm_g)


DEPTH_2 = 2

D_MIX = D_MODEL
CONV_WIDTH = D_MIX // 4
CONV_GROUPS = 4
CONV_K = 31
MLA_HEADS = 8
MLA_NOPE = 64
MLA_ROPE = 32
MLA_QK = MLA_NOPE + MLA_ROPE
MLA_V = 64
MLA_WIDTH = MLA_HEADS * MLA_V
Q_LORA = 768
KV_LORA = 256
ROPE_THETA_2 = 10000.0
Q_BLOCK = 128
SG_WIDTH = D_MIX - CONV_WIDTH - MLA_WIDTH
SG_HEADS = 4
SG_HEAD_DIM = SG_WIDTH // SG_HEADS
SG_CHUNK = 128
IN_SIZES = (CONV_WIDTH, CONV_WIDTH, CONV_WIDTH,
            Q_LORA, KV_LORA, MLA_ROPE, MLA_WIDTH,
            SG_WIDTH, SG_WIDTH, SG_WIDTH)
IN_COLS = 3 * CONV_WIDTH + Q_LORA + KV_LORA + MLA_ROPE + MLA_WIDTH + 3 * SG_WIDTH
EPS = 1e-6


def _rms_norm(x, g):
    xf = x.astype(jnp.float32)
    y = xf * lax.rsqrt(jnp.mean(xf * xf, axis=-1, keepdims=True) + EPS)
    return (y * g.astype(jnp.float32)).astype(x.dtype)

def _layer_norm(x, g, b):
    xf = x.astype(jnp.float32)
    mu = jnp.mean(xf, axis=-1, keepdims=True)
    var = jnp.mean(jnp.square(xf - mu), axis=-1, keepdims=True)
    y = (xf - mu) * lax.rsqrt(var + EPS) * g.astype(jnp.float32) + b.astype(jnp.float32)
    return y.astype(x.dtype)

def _rope_tables(seq):
    half = MLA_ROPE // 2
    inv_freq = ROPE_THETA_2 ** (-jnp.arange(half, dtype=jnp.float32) / half)
    ang = jnp.arange(seq, dtype=jnp.float32)[:, None] * inv_freq[None, :]
    return jnp.cos(ang), jnp.sin(ang)

def _apply_rope(x, cos, sin):
    half = MLA_ROPE // 2
    c = cos[None, :, None, :].astype(x.dtype)
    s = sin[None, :, None, :].astype(x.dtype)
    x1, x2 = x[..., :half], x[..., half:]
    return jnp.concatenate([x1 * c - x2 * s, x1 * s + x2 * c], axis=-1)

def _conv_branch(a, a_glu, conv_w, conv_b, ln_g, ln_b, pw_w, pw_b):
    y = a * jax.nn.sigmoid(a_glu)
    y = lax.conv_general_dilated(
        y, conv_w[:, None, :], window_strides=(1,),
        padding=[(CONV_K - 1, 0)],
        dimension_numbers=('NWC', 'WIO', 'NWC'),
        feature_group_count=CONV_WIDTH) + conv_b
    y = jax.nn.silu(_layer_norm(y, ln_g, ln_b))
    return y @ pw_w + pw_b

def _causal_attention(q, k, v):
    B, S, H, Dq = q.shape
    nb = S // Q_BLOCK
    scale = Dq ** -0.5
    q_blocks = jnp.moveaxis(q.reshape(B, nb, Q_BLOCK, H, Dq), 1, 0)
    k_pos = jnp.arange(S)

    def block(args):
        qb, i = args
        q_pos = i * Q_BLOCK + jnp.arange(Q_BLOCK)
        s = jnp.einsum('bqhd,bkhd->bhqk', qb, k).astype(jnp.float32) * scale
        s = jnp.where(k_pos[None, :] <= q_pos[:, None], s, -jnp.inf)
        p = jax.nn.softmax(s, axis=-1).astype(v.dtype)
        return jnp.einsum('bhqk,bkhd->bqhd', p, v)

    out = lax.map(block, (q_blocks, jnp.arange(nb)))
    return jnp.moveaxis(out, 0, 1).reshape(B, S, H * v.shape[-1])

def _mla_branch(c_q, c_kv, k_rope, q_norm_g, w_uq, kv_norm_g, w_ukv,
                qk_q_g, qk_k_g, cos, sin):
    B, S, _ = c_q.shape
    q = (_rms_norm(c_q, q_norm_g) @ w_uq).reshape(B, S, MLA_HEADS, MLA_QK)
    kv = (_rms_norm(c_kv, kv_norm_g) @ w_ukv).reshape(B, S, MLA_HEADS, MLA_NOPE + MLA_V)
    k_nope, v = kv[..., :MLA_NOPE], kv[..., MLA_NOPE:]
    k_r = jnp.broadcast_to(k_rope[:, :, None, :], (B, S, MLA_HEADS, MLA_ROPE))
    k = jnp.concatenate([k_nope, k_r], axis=-1)
    q = _rms_norm(q, qk_q_g)
    k = _rms_norm(k, qk_k_g)
    q = jnp.concatenate([q[..., :MLA_NOPE], _apply_rope(q[..., MLA_NOPE:], cos, sin)], axis=-1)
    k = jnp.concatenate([k[..., :MLA_NOPE], _apply_rope(k[..., MLA_NOPE:], cos, sin)], axis=-1)
    return _causal_attention(q, k, v)

def _sgu_branch(u, v, ln_g, ln_b, sg_w, sg_b):
    B, S, _ = u.shape
    nc = S // SG_CHUNK
    u = jax.nn.gelu(u)
    v = _layer_norm(jax.nn.gelu(v), ln_g, ln_b)
    v = v.reshape(B, nc, SG_CHUNK, SG_HEADS, SG_HEAD_DIM)
    mask = jnp.tril(jnp.ones((SG_CHUNK, SG_CHUNK), dtype=bool))
    w = jnp.where(mask[None], sg_w, jnp.zeros_like(sg_w))
    mixed = jnp.einsum('gts,bcsgd->bctgd', w, v) + sg_b.T[None, None, :, :, None]
    return u * mixed.reshape(B, S, SG_WIDTH)

def _layer(x, cos, sin, norm_g, w_in, conv_w, conv_b, conv_ln_g, conv_ln_b,
           conv_pw_w, conv_pw_b, q_norm_g, w_uq, kv_norm_g, w_ukv, qk_q_g, qk_k_g,
           sg_ln_g, sg_ln_b, sg_w, sg_b, branch_norm_g, w_out):
    h = _rms_norm(x, norm_g)
    proj = h @ w_in
    idx = np.cumsum(IN_SIZES)[:-1].tolist()
    (a, a_glu, z_conv, c_q, c_kv, k_rope, z_mla,
     u_sg, v_sg, z_sg) = jnp.split(proj, idx, axis=-1)

    y_conv = _conv_branch(a, a_glu, conv_w, conv_b, conv_ln_g, conv_ln_b,
                          conv_pw_w, conv_pw_b) * jax.nn.silu(z_conv)
    y_mla = _mla_branch(c_q, c_kv, k_rope, q_norm_g, w_uq, kv_norm_g, w_ukv,
                        qk_q_g, qk_k_g, cos, sin) * jax.nn.silu(z_mla)
    y_sg = _sgu_branch(u_sg, v_sg, sg_ln_g, sg_ln_b, sg_w, sg_b) * jax.nn.silu(z_sg)

    g_conv = branch_norm_g[:CONV_WIDTH]
    g_mla = branch_norm_g[CONV_WIDTH:CONV_WIDTH + MLA_WIDTH]
    g_sg = branch_norm_g[CONV_WIDTH + MLA_WIDTH:]
    y = jnp.concatenate([_rms_norm(y_conv, g_conv),
                         _rms_norm(y_mla, g_mla),
                         _rms_norm(y_sg, g_sg)], axis=-1)
    return x + y @ w_out

def second_inputs(seed: int = 0) -> dict:
    key = jax.random.key(seed)
    ks = jax.random.split(key, 24)
    f32 = jnp.float32

    def nrm(k, shape, scale):
        return jax.random.normal(k, shape, f32) * scale

    def gain(k, shape):
        return 1.0 + 0.02 * jax.random.normal(k, shape, f32)

    L = DEPTH_2
    return {
        'x': jax.random.normal(ks[0], (BATCH, SEQ, D_MODEL), f32),
        'norm_g': gain(ks[1], (L, D_MODEL)),
        'w_in': nrm(ks[2], (L, D_MODEL, IN_COLS), D_MODEL ** -0.5),
        'conv_w': nrm(ks[3], (L, CONV_K, CONV_WIDTH), CONV_K ** -0.5),
        'conv_b': nrm(ks[4], (L, CONV_WIDTH), 0.01),
        'conv_ln_g': gain(ks[5], (L, CONV_WIDTH)),
        'conv_ln_b': nrm(ks[6], (L, CONV_WIDTH), 0.01),
        'conv_pw_w': nrm(ks[7], (L, CONV_WIDTH, CONV_WIDTH), CONV_WIDTH ** -0.5),
        'conv_pw_b': nrm(ks[8], (L, CONV_WIDTH), 0.01),
        'q_norm_g': gain(ks[9], (L, Q_LORA)),
        'w_uq': nrm(ks[10], (L, Q_LORA, MLA_HEADS * MLA_QK), Q_LORA ** -0.5),
        'kv_norm_g': gain(ks[11], (L, KV_LORA)),
        'w_ukv': nrm(ks[12], (L, KV_LORA, MLA_HEADS * (MLA_NOPE + MLA_V)), KV_LORA ** -0.5),
        'qk_q_g': gain(ks[13], (L, MLA_QK)),
        'qk_k_g': gain(ks[14], (L, MLA_QK)),
        'sg_ln_g': gain(ks[15], (L, SG_WIDTH)),
        'sg_ln_b': nrm(ks[16], (L, SG_WIDTH), 0.01),
        'sg_w': nrm(ks[17], (L, SG_HEADS, SG_CHUNK, SG_CHUNK), SG_CHUNK ** -0.5),
        'sg_b': 1.0 + nrm(ks[18], (L, SG_HEADS, SG_CHUNK), 0.1),
        'branch_norm_g': gain(ks[19], (L, D_MIX)),
        'w_out': nrm(ks[20], (L, D_MIX, D_MODEL), D_MIX ** -0.5),
    }

def second_block(x, norm_g, w_in, conv_w, conv_b, conv_ln_g, conv_ln_b, conv_pw_w,
              conv_pw_b, q_norm_g, w_uq, kv_norm_g, w_ukv, qk_q_g, qk_k_g,
              sg_ln_g, sg_ln_b, sg_w, sg_b, branch_norm_g, w_out):
    cos, sin = _rope_tables(x.shape[1])
    for l in range(DEPTH_2):
        x = _layer(x, cos, sin, norm_g[l], w_in[l], conv_w[l], conv_b[l],
                   conv_ln_g[l], conv_ln_b[l], conv_pw_w[l], conv_pw_b[l],
                   q_norm_g[l], w_uq[l], kv_norm_g[l], w_ukv[l], qk_q_g[l], qk_k_g[l],
                   sg_ln_g[l], sg_ln_b[l], sg_w[l], sg_b[l], branch_norm_g[l], w_out[l])
    return x


def setup_inputs(seed=0):
    out = dict(first_inputs(seed))
    for name, value in second_inputs(seed + 1).items():
        if name != "x":
            out[name + "_2"] = value
    return out


def reference(
    x, positions, attn_norm_g, mlp_norm_g, diff_w_in, diff_w_out, diff_lam_q1, diff_lam_k1,
    diff_lam_q2, diff_lam_k2, diff_subln_g, moba_w_in, moba_w_out, swa_w_in, swa_b_in,
    swa_sinks, swa_w_out, mlp_w_up, mlp_w_down, final_norm_g, norm_g_2, w_in_2, conv_w_2,
    conv_b_2, conv_ln_g_2, conv_ln_b_2, conv_pw_w_2, conv_pw_b_2, q_norm_g_2, w_uq_2,
    kv_norm_g_2, w_ukv_2, qk_q_g_2, qk_k_g_2, sg_ln_g_2, sg_ln_b_2, sg_w_2, sg_b_2,
    branch_norm_g_2, w_out_2,
):
    x = first_block(
        x, positions, attn_norm_g, mlp_norm_g, diff_w_in, diff_w_out, diff_lam_q1, diff_lam_k1,
        diff_lam_q2, diff_lam_k2, diff_subln_g, moba_w_in, moba_w_out, swa_w_in, swa_b_in,
        swa_sinks, swa_w_out, mlp_w_up, mlp_w_down, final_norm_g,
    )
    return second_block(
        x, norm_g_2, w_in_2, conv_w_2, conv_b_2, conv_ln_g_2, conv_ln_b_2, conv_pw_w_2,
        conv_pw_b_2, q_norm_g_2, w_uq_2, kv_norm_g_2, w_ukv_2, qk_q_g_2, qk_k_g_2, sg_ln_g_2,
        sg_ln_b_2, sg_w_2, sg_b_2, branch_norm_g_2, w_out_2,
    )


_drawn_inputs = setup_inputs


def setup_inputs(seed=0):
    import zlib

    import numpy as np

    out = dict(_drawn_inputs(seed))
    spreads = {}
    factors = {'conv_b_2': 4.944,
     'conv_ln_g_2': 4.622,
     'conv_ln_b_2': 8.0,
     'conv_pw_b_2': 6.974,
     'q_norm_g_2': 8.0,
     'kv_norm_g_2': 3.597,
     'qk_q_g_2': 8.0,
     'qk_k_g_2': 8.0,
     'sg_ln_g_2': 8.0,
     'sg_ln_b_2': 8.0,
     'branch_norm_g_2': 2.853}
    for name, (base, spread) in spreads.items():
        noise = np.random.default_rng([zlib.crc32(name.encode()), seed]).standard_normal(out[name].shape)
        drawn = base * np.exp(spread * noise) if base else spread * noise
        out[name] = __import__('jax').numpy.asarray(drawn.astype(out[name].dtype))
    for name, factor in factors.items():
        out[name] = (out[name] * factor).astype(out[name].dtype)
    return out
```

```python
import math
from contextlib import ExitStack

import concourse.bass as bass
import numpy as np
from concourse import mybir

FP32 = mybir.dt.float32
FP32R = mybir.dt.float32r
INT32 = mybir.dt.int32
ALU = mybir.AluOpType
ACT = mybir.ActivationFunctionType
AXIS = mybir.AxisListType

P = 128
SEQ, D = 256, 1024
TT = SEQ // P
KT = D // P
FF = 4 * D
DEPTH, DEPTH_2 = 4, 2
HEAD = 64
EPS = 1e-6
HALF = 8
ROPE_THETA = 500000.0
NEG = -1.0e30
BANK = 512
SLOT = 4096
CONV_K = 31
ROUND = 1.5 * 2.0 ** 23
TURN_PARTS = [6.28125, 0.0019350051879882812, 3.019916050e-07]
PI_BELOW = 3.1415925
PARAMS = 10
CW, SGW, MLAW = 256, 256, 512
NOPE, ROPE2, QK2, V2, H2 = 64, 32, 96, 64, 8
HALF2 = ROPE2 // 2
QL, KVL = 768, 256
IN_COLS = 3104
A0, GLU0, ZC0, CQ0, CKV0, KR0, ZM0, U0, V0, ZS0 = 0, 256, 512, 768, 1536, 1792, 1824, 2336, 2592, 2848
W_IN_2_BLOCKS = [(0, 512), (2336, 512), (512, 512), (1024, 512), (1536, 288), (1824, 512), (2848, 256)]
MIXERS = ["diff", "moba", "swa", "diff"]
QKV_COLS = {"diff": 3072, "moba": 3072, "swa": 1280}
LAMBDAS = ["diff_lam_q1", "diff_lam_k1", "diff_lam_q2", "diff_lam_k2"]
LAMBDA_INIT = {0: 0.8 - 0.6 * math.exp(-0.3 * 0), 3: 0.8 - 0.6 * math.exp(-0.3 * 3)}

ROWS_A = [("conv_w_2", DEPTH_2 * CONV_K * 2), ("conv_b_2", DEPTH_2 * 2)]
ROWS_B = [("attn_norm_g", DEPTH * KT), ("mlp_norm_g", DEPTH * KT), ("diff_subln_g", 2), ("norm_g_2", DEPTH_2 * KT),
          ("q_norm_g_2", DEPTH_2 * 6), ("kv_norm_g_2", DEPTH_2 * 2), ("branch_norm_g_2", DEPTH_2 * KT),
          ("sg_b_2", DEPTH_2 * 4)]
N_ROWS_A = sum(n for _, n in ROWS_A)
N_ROWS_B = sum(n for _, n in ROWS_B)
ROW_AT = {}
for _rows in (ROWS_A, ROWS_B):
    _at = 0
    for _name, _n in _rows:
        ROW_AT[_name] = _at
        _at += _n
SPREAD_2 = [("conv_ln_g_2", CW), ("conv_ln_b_2", CW), ("conv_pw_b_2", CW), ("sg_ln_g_2", SGW), ("sg_ln_b_2", SGW),
            ("qk_q_g_2", QK2), ("qk_k_g_2", QK2)]
SPREAD_AT = {}
_at = 0
for _name, _n in SPREAD_2:
    SPREAD_AT[_name] = (_at, _n)
    _at += _n
SPREAD_COLS = _at


class Tally:

    def __init__(self, sem):
        self.sem, self.n, self.turn = sem, 0, 0

    def one(self, k=1):
        self.n += k
        return self.sem, k

    def after(self, k=1):
        self.n += k
        return self.sem, self.n + self.turn

    def now(self, back=0):
        return self.sem, self.n - back + self.turn


class Tallies:

    def __init__(self, sems):
        self.of = {name: Tally(s) for name, s in sems.items()}
        self.loaded = [self.of[f"raw_loaded{s}"] for s in range(2)]
        self.filled = [self.of[f"filled{p}"] for p in range(4)]
        self.emptied = [self.of[f"emptied{p}"] for p in range(4)]
        self.block = 0
        self.lam = 0

    def __getitem__(self, name):
        return self.of[name]


def build(nc, a, out):
    ctx = ExitStack()
    with ctx:
        def sb(name, shape, dt=FP32):
            return ctx.enter_context(nc.sbuf_tensor(name, shape, dt))

        raw = sb("raw", [P, 2, SLOT])
        whi = sb("whi", [P, 2, SLOT], FP32R)
        wlo = sb("wlo", [P, 2, SLOT], FP32R)
        h = sb("h", [P, TT, D])
        xhi = sb("xhi", [P, KT, SEQ], FP32R)
        xlo = sb("xlo", [P, KT, SEQ], FP32R)
        qkv = sb("qkv", [P, TT, IN_COLS])
        qT = sb("qT", [P, 8, SEQ])
        kT = sb("kT", [P, 8, SEQ])
        sm = sb("sm", [P, 2, 2, 384])
        pT = sb("pT", [P, 2, 2, 384])
        ident = sb("ident", [P, P])
        causal = sb("causal", [P, 384])
        band = sb("band", [P, 384])
        colsA = sb("colsA", [P, N_ROWS_A])
        colsB = sb("colsB", [P, N_ROWS_B])
        subg = sb("subg", [P, 2])
        sinks = sb("sinks", [P, 16])
        sinks8 = sb("sinks8", [P, 16])
        wsg = sb("wsg", [P, DEPTH_2, 4, P])
        pos_i = sb("pos_i", [P, TT], INT32)
        pos = sb("pos", [P, TT])
        inv = sb("inv", [P, HALF])
        cos1 = sb("cos1", [P, TT, HALF])
        sin1 = sb("sin1", [P, TT, HALF])
        cs2 = sb("cs2", [P, 2, TT, HALF2])
        ang = sb("ang", [P, TT, HALF])
        turns_of = sb("turns_of", [P, TT, HALF])
        lams = sb("lams", [P, 4])
        neglam = sb("neglam", [P, 2])
        ss = sb("ss", [P, 8])
        var = sb("var", [P, 8])
        std = sb("std", [P, 8])
        rstd = sb("rstd", [P, 8])
        ss16 = sb("ss16", [P, 32])
        std16 = sb("std16", [P, 32])
        rstd16 = sb("rstd16", [P, 32])
        mx = sb("mx", [P, 2, 2, 2])
        negm = sb("negm", [P, 2, 2, 2])
        snk = sb("snk", [P, 2, 2, 2])
        sums = sb("sums", [P, 2, 2, 2])
        rinv = sb("rinv", [P, 2, 2, 2])
        bn6 = sb("bn6", [P, TT, 6])
        bn2 = sb("bn2", [P, TT, 2])

        first = ExitStack()
        ahi = first.enter_context(nc.sbuf_tensor("ahi", [P, 2, 4, SEQ], FP32R))
        alo = first.enter_context(nc.sbuf_tensor("alo", [P, 2, 4, SEQ], FP32R))
        swab = first.enter_context(nc.sbuf_tensor("swab", [P, QKV_COLS["swa"]], FP32))
        fing = swab[:, 0:D]
        first.close()
        qbuf = sb("qbuf", [P, TT, H2 * QK2])
        kfull = sb("kfull", [P, TT, H2 * QK2])
        kvbuf = qkv[:, :, CQ0:CQ0 + H2 * (NOPE + V2)]
        ypad = sb("ypad", [P, 2, CONV_K - 1 + SEQ])
        yacc = sb("yacc", [P, 2, SEQ])
        spread = sb("spread", [P, SPREAD_COLS])

        relu_at = [qkv[:, 0, j * 1024:(j + 1) * 1024] for j in range(2)]
        square_at = qkv[:, 1, 0:1024]
        lamv = qT[:, 0:2, :].rearrange("p a (b n) -> p (a b) n", b=2)

        pair = [ctx.enter_context(nc.psum_tensor(f"pair{i}", [P, 2, BANK], FP32)) for i in range(4)]

        sem_names = ["raw_loaded0", "raw_loaded1", "hi_split", "lo_split", "block_used",
                     "filled0", "filled1", "filled2", "filled3", "emptied0", "emptied1", "emptied2", "emptied3",
                     "x_loaded", "params_loaded", "rows_loaded", "mixing_loaded", "gains_loaded", "spread_loaded",
                     "pool_step", "consts_made", "mixing_masked", "dve_step", "angles_ready", "sines_ready", "params_ready",
                     "xhi_written", "squares_summed", "var_ready", "std_ready", "rstd_ready", "sum16_ready", "std16_ready",
                     "ahi_written", "alo_written", "roped", "shift_ready", "exp_done", "p_ready", "o_normed", "h_ready",
                     "sig_ready", "glu_ready", "conv_ready", "ln_ready", "silu_ready", "zsilu_ready", "qk_ready", "gelu_ready",
                     "vln_ready", "branches_ready", "y_ready", "stored"]
        sems = {n: ctx.enter_context(nc.semaphore(n)) for n in sem_names}

        def tallies():
            return Tallies(sems)

        def turns(t, i, per):
            for name, k in per.items():
                t[name].turn = i * k

        def after_turns(t, per, count, blocks):
            for name, k in per.items():
                t[name].turn = 0
                t[name].n += (count - 1) * k
            t.block += (count - 1) * blocks

        IN_TURN = {"raw_loaded0": 16, "raw_loaded1": 16, "hi_split": 4, "lo_split": 4, "block_used": 2,
                   "emptied2": 1, "emptied3": 1}
        MLP_TURN = {"raw_loaded0": 32, "raw_loaded1": 32, "hi_split": 8, "lo_split": 8, "block_used": 4,
                    "emptied0": 1, "emptied1": 1, "ahi_written": 2, "alo_written": 2}

        def slot(buf, s, T, w):
            return buf[:, s, 0:T * w].rearrange("p (t n) -> p t n", t=T)

        def halves(n):
            return [slice(0, n // 2), slice(n // 2, n)]

        def block_plan():
            full, plan = KT * BANK, []
            for mixer in MIXERS:
                plan += [KT * w for _, w in in_blocks(mixer)] + [full] * (2 + 2 * (FF // BANK))
            for _ in range(DEPTH_2):
                plan += [KT * w for _, w in W_IN_2_BLOCKS] + [6 * 384] * 2 + [2 * BANK] * 2 + [2 * CW] + [full] * 2
            return plan

        def gain(name, layer, n=KT):
            at = ROW_AT[name] + layer * n
            return lambda kt: colsB[:, at + kt:at + kt + 1]

        def gain_latent(layer):
            q, kv = gain("q_norm_g_2", layer, 6), gain("kv_norm_g_2", layer, 2)
            return lambda kt: q(kt) if kt < 6 else kv(kt - 6)

        def gain_sub(which):
            return lambda kt: subg[:, which:which + 1]

        def param2(name):
            at, n = SPREAD_AT[name]
            return spread[:, at:at + n]

        def lanes(ap, shape):
            return ap.to_broadcast(shape)

        def in_blocks(mixer):
            cols = QKV_COLS[mixer]
            return [(n, min(BANK, cols - n)) for n in range(0, cols, BANK)]

        PBLOCKS = [(0, 0, 0), (P, 1, 0), (2 * P, 1, 1)]
        PAIRS = {"diff": 8, "moba": 8, "swa": 8, "mla": 4}
        SCALE = {"diff": HEAD ** -0.5, "moba": HEAD ** -0.5, "swa": HEAD ** -0.5, "mla": QK2 ** -0.5}

        def heads(mixer, hp, c):
            if mixer == "mla":
                return qT[0:QK2, 2 * hp + c, :], kT[0:QK2, 2 * hp + c, :]
            rows = slice(c * HEAD, (c + 1) * HEAD)
            return qT[rows, hp, :], kT[rows, hp // 4 if mixer == "swa" else hp, :]

        def values(mixer, hp, c, kt):
            if mixer == "diff":
                return qkv[:, kt, 2048 + hp * P:2048 + (hp + 1) * P]
            if mixer == "moba":
                return qkv[:, kt, 2048 + (2 * hp + c) * HEAD:2048 + (2 * hp + c + 1) * HEAD]
            if mixer == "swa":
                return qkv[:, kt, 1152 + (hp // 4) * HEAD:1152 + (hp // 4 + 1) * HEAD]
            v = (2 * hp + c) * (NOPE + V2) + NOPE
            return kvbuf[:, kt, v:v + V2]

        def q_tile(mixer, n, tt):
            return qbuf[:, tt, n * QK2:(n + 1) * QK2] if mixer == "mla" else qkv[:, tt, n * P:(n + 1) * P]

        def k_tile(mixer, n, tt):
            if mixer == "mla":
                return kfull[:, tt, n * QK2:(n + 1) * QK2]
            at = (1280 if mixer == "swa" else 1024) + n * P
            return qkv[:, tt, at:at + P]

        def k_tiles(mixer):
            return 2 if mixer == "swa" else 8

        def o_at(mixer, g):
            return qkv[:, :, g * 512:(g + 1) * 512] if mixer == "diff" else qbuf[:, :, 0:MLAW]

        def y_tile(kt):
            if kt < 2:
                return lambda tt: qkv[:, tt, ZC0 + kt * P:ZC0 + (kt + 1) * P]
            if kt < 6:
                return lambda tt: qbuf[:, tt, (kt - 2) * P:(kt - 1) * P]
            return lambda tt: qkv[:, tt, U0 + (kt - 6) * P:U0 + (kt - 5) * P]

        def branch(n):
            return [qkv[:, :, ZC0:ZC0 + CW], qbuf[:, :, 0:MLAW], qkv[:, :, U0:U0 + SGW]][n]

        def h_tile(kt):
            return lambda tt: h[:, tt, kt * P:(kt + 1) * P]

        def o_tile(kt):
            return lambda tt: qkv[:, tt, kt * P:(kt + 1) * P]

        def latent_tile(kt):
            return lambda tt: qkv[:, tt, CQ0 + kt * P:CQ0 + (kt + 1) * P]

        def conv_tile(kt):
            return lambda tt: qkv[:, tt, kt * P:(kt + 1) * P]

        def pair_tile(kt, width=SEQ):
            return pair[kt // 4][:, (kt % 4) // 2, (kt % 2) * SEQ:(kt % 2) * SEQ + width]

        block = ctx.enter_context(nc.Block())
        emptied_by_layer = []

        @block.scalar
        def _(act):
            t = tallies()

            plan = block_plan()

            def split():
                if not plan:
                    return
                s = t.block % 2
                act.wait_ge(*t.loaded[s].after(16))
                for cols in halves(plan.pop(0)):
                    act.activation(whi[:, s, cols], raw[:, s, cols], ACT.Copy).then_inc(*t["hi_split"].one())
                t.block += 1

            def used():
                act.wait_ge(*t["block_used"].after())

            def turn_split(n, scale_of, per_pair=4):
                for kt in range(n):
                    if kt % 4 == 0:
                        act.wait_ge(*t.filled[kt // 4].after())
                    g = scale_of(kt) if scale_of else 1.0
                    act.activation(xhi[:, kt, :], pair_tile(kt), ACT.Copy, scale=g).then_inc(*t["xhi_written"].one())
                for p in range((n + 3) // 4):
                    t.emptied[p].n += 1

            def sum_squares(parts):
                for n, src in enumerate(parts):
                    w = src.shape[-1]
                    junk = kT[:, :, :].rearrange("p a b -> p (a b)")[:, (n % 2) * 1024:(n % 2) * 1024 + w]
                    if n >= 2:
                        act.wait_ge(*t["squares_summed"].now())
                    act.activation(junk, src, ACT.Square, accum_out=ss[:, n:n + 1]).then_inc(*t["squares_summed"].one())

            def roots(n):
                act.wait_ge(*t["var_ready"].after())
                act.activation(std[:, 0:n], var[:, 0:n], ACT.Sqrt).then_inc(*t["std_ready"].one())

            def norm(g, root=True):
                turn_split(KT, g)
                sum_squares([h[:, tt, :] for tt in range(TT)])
                if root:
                    roots(TT)

            def project_even(dst, w, p, scale):
                for tt in range(TT):
                    m = act.activation(dst(tt), pair[p][:, tt, 0:w], ACT.Copy, scale=scale(tt))
                m.then_inc(*t.emptied[p].one())

            def project_in(mixer):
                if mixer == "swa":
                    for n, w in in_blocks(mixer):
                        used()
                        t.emptied[2 + (n // BANK) % 2].n += 1
                        split()
                    return
                act.wait_ge(*t["rstd_ready"].after())
                with act.Fori(0, 3) as i:
                    turns(t, i, IN_TURN)
                    used()
                    project_even(lambda tt: qkv[:, tt, bass.ds(i * 1024, BANK)], BANK, 2, lambda tt: rstd[:, tt:tt + 1])
                    split()
                    used()
                    t.emptied[3].n += 1
                    split()
                after_turns(t, IN_TURN, 3, 2)
                del plan[:4]

            def queries_out(mixer):
                rows = QK2 if mixer == "mla" else P
                for p in range(2):
                    act.wait_ge(*t.filled[p].after())
                    act.activation(qT[0:rows, 4 * p:4 * p + 4, :],
                                   pair[p][0:rows, :, :].rearrange("p b (j n) -> p (b j) n", j=2), ACT.Copy)\
                        .then_inc(*t.emptied[p].one())
                for p in range(2, 2 + (k_tiles(mixer) + 3) // 4):
                    t.filled[p].n += 1
                    t.emptied[p].n += 1

            def exps(mixer, hp):
                b = hp % 2
                t.filled[b].n += 1
                t.emptied[b].n += 1
                act.wait_ge(*t["shift_ready"].after())
                if mixer == "swa":
                    act.activation(snk[:, b, :, :], snk[:, b, :, :], ACT.Exp)
                for c in range(2):
                    for tt, cols in ((0, slice(0, P)), (1, slice(P, 3 * P))):
                        m = act.activation(sm[:, b, c, cols], sm[:, b, c, cols], ACT.Exp, scale=SCALE[mixer],
                                           bias=negm[:, b, c, tt:tt + 1], accum_out=sums[:, b, c, tt:tt + 1])
                m.then_inc(*t["exp_done"].one())

            def probs_out(mixer, hp):
                nb = 1 if mixer == "diff" else 2
                act.wait_ge(*t.filled[2].after())
                act.activation(pT[:, hp % 2, 0:nb, :], pair[2][:, 0:nb, 0:384], ACT.Copy).then_inc(*t.emptied[2].one())

            def outputs(mixer, g):
                act.wait_ge(*t.filled[3].after())
                if mixer in ("moba", "swa"):
                    act.activation(xhi[:, 4 * g:4 * g + 4, :], pair[3][:, :, :].rearrange("p b (j n) -> p (b j) n", j=2),
                                   ACT.Copy).then_inc(*t["xhi_written"].one())
                    t.emptied[3].n += 1
                else:
                    src = pair[3][:, :, :].rearrange("p b (j t e) -> p (b j) t e", j=2, t=TT)
                    act.activation(o_at(mixer, g).rearrange("p t (j e) -> p j t e", j=4), src, ACT.Copy)\
                        .then_inc(*t.emptied[3].one())

            def attend(mixer):
                queries_out(mixer)
                n = PAIRS[mixer]
                exps(mixer, 0)
                for hp in range(n):
                    if hp + 1 < n:
                        exps(mixer, hp + 1)
                    probs_out(mixer, hp)
                    if hp and (hp - 1) % 4 == 3:
                        outputs(mixer, (hp - 1) // 4)
                outputs(mixer, (n - 1) // 4)

            def roots16(n):
                act.wait_ge(*t["sum16_ready"].after())
                act.activation(std16[:, 0:n], ss16[:, 0:n], ACT.Sqrt).then_inc(*t["std16_ready"].one())

            def project_out():
                for n in range(2):
                    used()
                    t.emptied[2 + n].n += 1
                    split()

            def mlp():
                def up(j):
                    b = j % 2
                    used()
                    act.activation(relu_at[b], pair[b][:, :, :].rearrange("p b n -> p (b n)"), ACT.Relu)\
                        .then_inc(*t.emptied[b].one())
                    act.wait_ge(*t.emptied[b].now())
                    act.activation(ahi[:, b, :, :].rearrange("p f n -> p (f n)"), relu_at[b], ACT.Square)\
                        .then_inc(*t["ahi_written"].one())
                    split()

                def down():
                    used()
                    split()

                up(0)
                up(1)
                down()
                with act.Fori(0, 3) as i:
                    turns(t, i, MLP_TURN)
                    up(0)
                    down()
                    up(1)
                    down()
                after_turns(t, MLP_TURN, 3, 4)
                del plan[:8]
                down()
                t.emptied[2].n += 1
                t.emptied[3].n += 1

            def second(layer):
                norm(gain("norm_g_2", layer))
                for n, (c0, w) in enumerate(W_IN_2_BLOCKS):
                    used()
                    if n % 2 == 0:
                        if n == 0:
                            act.wait_ge(*t["rstd_ready"].after())
                        project_even(lambda tt: qkv[:, tt, c0:c0 + w], w, 2, lambda tt: rstd[:, tt:tt + 1])
                    else:
                        t.emptied[3].n += 1
                    split()
                act.wait_ge(*t.emptied[2].now())
                act.wait_ge(*t.emptied[3].now())
                turn_split(8, gain_latent(layer))
                sum_squares([qkv[:, tt, c:c + w] for c, w in ((CQ0, QL), (CKV0, KVL)) for tt in range(TT)])
                roots(4)
                act.wait_ge(*t["rstd_ready"].after())
                for n in range(2):
                    used()
                    if n == 0:
                        project_even(lambda tt: qbuf[:, tt, 0:384], 384, 2, lambda tt: rstd[:, tt:tt + 1])
                    else:
                        t.emptied[3].n += 1
                    split()
                for n in range(2):
                    used()
                    if n == 0:
                        project_even(lambda tt: kvbuf[:, tt, 0:BANK], BANK, 2, lambda tt: rstd[:, 2 + tt:3 + tt])
                    else:
                        t.emptied[3].n += 1
                    split()
                act.activation(qkv[:, :, GLU0:GLU0 + CW], qkv[:, :, GLU0:GLU0 + CW], ACT.Sigmoid).then_inc(*t["sig_ready"].one())
                act.wait_ge(*t.filled[0].after())
                act.activation(ypad[:, :, CONV_K - 1:], pair[0][:, 0, :].rearrange("p (c n) -> p c n", c=2), ACT.Copy)\
                    .then_inc(*t.emptied[0].one())
                t.filled[1].n += 1
                roots(TT)
                t.emptied[1].n += 1
                act.wait_ge(*t["ln_ready"].after())
                act.activation(qkv[:, :, 0:CW], qkv[:, :, 0:CW], ACT.Silu).then_inc(*t["silu_ready"].one())
                turn_split(2, None)
                act.activation(qkv[:, :, ZC0:ZC0 + CW], qkv[:, :, ZC0:ZC0 + CW], ACT.Silu).then_inc(*t["zsilu_ready"].one())
                used()
                t.emptied[2].n += 1
                split()
                roots16(32)
                attend("mla")
                act.activation(qkv[:, :, V0:V0 + SGW], qkv[:, :, V0:V0 + SGW], ACT.Gelu_apprx_tanh).then_inc(*t["gelu_ready"].one())
                act.activation(qkv[:, :, U0:U0 + SGW], qkv[:, :, U0:U0 + SGW], ACT.Gelu_apprx_tanh).then_inc(*t["gelu_ready"].one())
                roots(TT)
                act.activation(qkv[:, :, ZM0:ZM0 + MLAW], qkv[:, :, ZM0:ZM0 + MLAW], ACT.Silu).then_inc(*t["zsilu_ready"].one())
                act.activation(qkv[:, :, ZS0:ZS0 + SGW], qkv[:, :, ZS0:ZS0 + SGW], ACT.Silu).then_inc(*t["zsilu_ready"].one())
                t.filled[1].n += 1
                t.emptied[1].n += 1
                act.wait_ge(*t["branches_ready"].after())
                sum_squares([branch(n)[:, tt, :] for n in range(3) for tt in range(TT)])
                roots(6)
                t["rstd_ready"].n += 1
                turn_split(KT, gain("branch_norm_g_2", layer))
                project_out()

            rows_a = sm[:, 0, 0, 0:P]
            rows_b = sm[0:N_ROWS_B, 0, 1, 0:P]
            for tile_at, rows in ((rows_a, ROWS_A), (rows_b, ROWS_B)):
                for name, n in rows:
                    v = a[name]
                    flat = v.rearrange("a b c -> (a b c)") if len(v.shape) == 3 else v.rearrange("a b -> (a b)")
                    act.dma_start(tile_at[ROW_AT[name]:ROW_AT[name] + n, :], flat.rearrange("(r p) -> r p", p=P))\
                        .then_inc(*t["rows_loaded"].one(16))
            split()
            split()
            act.wait_ge(*t.filled[2].after())
            act.activation(colsA[:, :], pair[2][:, 0, 0:N_ROWS_A], ACT.Copy)
            act.activation(colsB[:, :], pair[2][:, 1, 0:N_ROWS_B], ACT.Copy).then_inc(*t.emptied[2].one())
            act.wait_ge(*t.filled[3].after())
            act.activation(wsg[:, :, :, :].rearrange("p l g t -> p l (g t)"), pair[3][:, :, :], ACT.Copy)\
                .then_inc(*t.emptied[3].one())
            act.wait_ge(*t.emptied[2].now())
            act.wait_ge(*t["angles_ready"].after())
            act.activation(sin1[:, :, :], sin1[:, :, :], ACT.Sin).then_inc(*t["sines_ready"].one())
            act.activation(cos1[:, :, :], cos1[:, :, :], ACT.Sin).then_inc(*t["sines_ready"].one())
            act.activation(lams[:, :], lams[:, :], ACT.Exp).then_inc(*t["sines_ready"].one())

            for layer, mixer in enumerate(MIXERS):
                norm(gain("attn_norm_g", layer))
                if mixer == "swa":
                    t["rstd_ready"].n += 1
                project_in(mixer)
                attend(mixer)
                if mixer == "diff":
                    roots16(16)
                    turn_split(KT, gain_sub(layer // 3))
                project_out()
                norm(gain("mlp_norm_g", layer), root=False)
                mlp()
            act.wait_ge(*t.emptied[2].now())
            act.wait_ge(*t.emptied[3].now())
            sum_squares([h[:, tt, :] for tt in range(TT)])
            roots(TT)
            t["rstd_ready"].n += 1
            for layer in range(DEPTH_2):
                second(layer)

        @block.tensor
        def _(pe):
            t = tallies()

            def free(p):
                if t.emptied[p].n:
                    pe.wait_ge(*t.emptied[p].now())
                t.emptied[p].n += 1

            def products(dst, x, w, first, last):
                (x_hi, x_lo), (w_hi, w_lo) = x, w
                pe.matmul(dst, x_hi, w_hi, start=first, stop=False)
                pe.matmul(dst, x_hi, w_lo, start=False, stop=False)
                return pe.matmul(dst, x_lo, w_hi, start=False, stop=last)

            def weights(T, w):
                pe.wait_ge(*t["lo_split"].after(2))
                s = t.block % 2
                t.block += 1
                return slot(whi, s, T, w), slot(wlo, s, T, w)

            def token_major(p, T, w, k0=0):
                w_hi, w_lo = weights(T, w)
                free(p)
                for tt in range(TT):
                    tok = slice(tt * P, (tt + 1) * P)
                    for k in range(T):
                        m = products(pair[p][:, tt, 0:w], (xhi[:, k0 + k, tok], xlo[:, k0 + k, tok]),
                                     (w_hi[:, k, :], w_lo[:, k, :]), k == 0, k == T - 1)
                m.then_inc(*t["block_used"].one())

            def turn(n, tile):
                for kt in range(n):
                    p = kt // 4
                    if kt % 4 == 0:
                        free(p)
                    for tt in range(TT):
                        m = pe.transpose(pair_tile(kt)[:, tt * P:(tt + 1) * P], tile(kt)(tt), ident[:, :])
                    if kt % 4 == 3 or kt == n - 1:
                        m.then_inc(*t.filled[p].one())

            def turned(n):
                for p in range((n + 3) // 4):
                    pe.wait_ge(*t.emptied[p].now())

            def project_in(mixer):
                turned(KT)
                if mixer == "swa":
                    for n, w in in_blocks(mixer):
                        token_major(2 + (n // BANK) % 2, KT, w)
                    return
                with pe.Fori(0, 3) as i:
                    turns(t, i, IN_TURN)
                    for b in range(2):
                        token_major(2 + b, KT, BANK)
                after_turns(t, IN_TURN, 3, 2)

            def turn_heads(mixer):
                rows = QK2 if mixer == "mla" else P
                for n in range(8):
                    if n % 4 == 0:
                        free(n // 4)
                    for tt in range(TT):
                        m = pe.transpose(pair_tile(n)[0:rows, tt * P:(tt + 1) * P], q_tile(mixer, n, tt), ident[:, :])
                    if n % 4 == 3:
                        m.then_inc(*t.filled[n // 4].one())
                for n in range(k_tiles(mixer)):
                    p = 2 + n // 4
                    if n % 4 == 0:
                        free(p)
                    for tt in range(TT):
                        dst = pair[p][0:rows, (n % 4) // 2, (n % 2) * SEQ + tt * P:(n % 2) * SEQ + (tt + 1) * P]
                        m = pe.transpose(dst, k_tile(mixer, n, tt), ident[:, :])
                    if n % 4 == 3 or n == k_tiles(mixer) - 1:
                        m.then_inc(*t.filled[p].one())

            def scores(mixer, hp):
                b = hp % 2
                free(b)
                for c in range(2):
                    q, k = heads(mixer, hp, c)
                    pe.matmul(pair[b][:, c, 0:P], q[:, 0:P], k[:, 0:P], start=True, stop=True)
                    m = pe.matmul(pair[b][:, c, P:3 * P], q[:, P:2 * P], k[:, :], start=True, stop=True)
                m.then_inc(*t.filled[b].one())

            def turn_probs(mixer, hp):
                pe.wait_ge(*t["p_ready"].after())
                free(2)
                for c in range(1 if mixer == "diff" else 2):
                    for at, _, _ in PBLOCKS:
                        m = pe.transpose(pair[2][:, c, at:at + P], sm[:, hp % 2, c, at:at + P], ident[:, :])
                m.then_inc(*t.filled[2].one())

            def mix_values(mixer, hp, evac_back):
                pe.wait_ge(*t.emptied[2].now(evac_back))
                j = hp % 4
                if j == 0:
                    free(3)
                at = (j % 2) * SEQ
                b = hp % 2
                if mixer in ("moba", "swa"):
                    for c in range(2):
                        rows = slice(c * HEAD, (c + 1) * HEAD)
                        pe.matmul(pair[3][rows, j // 2, at:at + SEQ], values(mixer, hp, c, 0), pT[:, b, c, 0:SEQ],
                                  start=True, stop=False)
                        m = pe.matmul(pair[3][rows, j // 2, at + P:at + SEQ], values(mixer, hp, c, 1),
                                      pT[:, b, c, SEQ:SEQ + P], start=False, stop=True)
                else:
                    for c in range(1 if mixer == "diff" else 2):
                        w = P if mixer == "diff" else V2
                        for qt in range(TT):
                            dst = pair[3][:, j // 2, at + qt * P + c * V2:at + qt * P + c * V2 + w]
                            parts = [x for x in PBLOCKS if x[1] == qt]
                            for col, _, kt in parts:
                                m = pe.matmul(dst, pT[:, b, c, col:col + P], values(mixer, hp, c, kt),
                                              start=kt == 0, stop=kt == qt)
                if j == 3:
                    m.then_inc(*t.filled[3].one())

            def attend(mixer):
                turn_heads(mixer)
                for p in range(2 + (k_tiles(mixer) + 3) // 4):
                    pe.wait_ge(*t.emptied[p].now())
                n = PAIRS[mixer]
                scores(mixer, 0)
                for hp in range(n):
                    if hp + 1 < n:
                        scores(mixer, hp + 1)
                    turn_probs(mixer, hp)
                    if hp:
                        mix_values(mixer, hp - 1, 1)
                mix_values(mixer, n - 1, 0)

            def project_out():
                for n in range(2):
                    token_major(2 + n, KT, BANK)

            def mlp():
                def up(j):
                    w_hi, w_lo = weights(KT, BANK)
                    free(j % 2)
                    for f in range(4):
                        cols = slice(f * P, (f + 1) * P)
                        dst = pair[j % 2][:, f // 2, (f % 2) * SEQ:(f % 2 + 1) * SEQ]
                        for k in range(KT):
                            m = products(dst, (w_hi[:, k, cols], w_lo[:, k, cols]), (xhi[:, k, :], xlo[:, k, :]),
                                         k == 0, k == KT - 1)
                    m.then_inc(*t["block_used"].one())

                def down(j, first=False, last=False):
                    w_hi, w_lo = weights(4, D)
                    if first:
                        free(2)
                        free(3)
                    pe.wait_ge(*t["alo_written"].after())
                    for n in range(2):
                        cols = slice(n * BANK, (n + 1) * BANK)
                        for tt in range(TT):
                            tok = slice(tt * P, (tt + 1) * P)
                            for f in range(4):
                                m = products(pair[2 + n][:, tt, :], (ahi[:, j % 2, f, tok], alo[:, j % 2, f, tok]),
                                             (w_hi[:, f, cols], w_lo[:, f, cols]), first and f == 0, last and f == 3)
                    m.then_inc(*t["block_used"].one())

                turned(KT)
                up(0)
                up(1)
                down(0, first=True)
                with pe.Fori(0, 3) as i:
                    turns(t, i, MLP_TURN)
                    up(0)
                    down(1)
                    up(1)
                    down(0)
                after_turns(t, MLP_TURN, 3, 4)
                down(1, last=True)

            def normed():
                pe.wait_ge(*t.emptied[2].now())
                pe.wait_ge(*t.emptied[3].now())

            def second(layer):
                turn(KT, h_tile)
                turned(KT)
                for n, (_, w) in enumerate(W_IN_2_BLOCKS):
                    token_major(2 + n % 2, KT, w)
                normed()
                turn(8, latent_tile)
                turned(8)
                for n in range(2):
                    token_major(2 + n, 6, 384)
                for n in range(2):
                    token_major(2 + n, 2, BANK, 6)
                pe.wait_ge(*t["glu_ready"].after())
                free(0)
                for ct in range(2):
                    for tt in range(TT):
                        m = pe.transpose(pair[0][:, 0, ct * SEQ + tt * P:ct * SEQ + (tt + 1) * P], conv_tile(ct)(tt), ident[:, :])
                m.then_inc(*t.filled[0].one())
                pe.wait_ge(*t["conv_ready"].after())
                free(1)
                for ct in range(2):
                    for tt in range(TT):
                        m = pe.transpose(pair[1][:, 0, tt * CW + ct * P:tt * CW + (ct + 1) * P],
                                         yacc[:, ct, tt * P:(tt + 1) * P], ident[:, :])
                m.then_inc(*t.filled[1].one())
                pe.wait_ge(*t["silu_ready"].after())
                turn(2, conv_tile)
                turned(2)
                token_major(2, 2, CW)
                pe.wait_ge(*t["qk_ready"].after())
                attend("mla")
                pe.wait_ge(*t["vln_ready"].after())
                free(1)
                for tt in range(TT):
                    for g in range(4):
                        m = pe.matmul(pair[1][:, tt, g * 64:(g + 1) * 64], wsg[:, layer, g, :],
                                      qkv[:, tt, V0 + g * 64:V0 + (g + 1) * 64], start=True, stop=True)
                m.then_inc(*t.filled[1].one())
                pe.wait_ge(*t["y_ready"].after())
                turn(KT, y_tile)
                turned(KT)
                project_out()

            pe.wait_ge(sems["consts_made"], 6)
            pe.wait_ge(sems["rows_loaded"], 16 * (len(ROWS_A) + len(ROWS_B)))
            free(2)
            pe.transpose(pair[2][:, 0, 0:N_ROWS_A], sm[:, 0, 0, 0:P], ident[:, :])
            pe.transpose(pair[2][:, 1, 0:N_ROWS_B], sm[0:N_ROWS_B, 0, 1, 0:P], ident[0:N_ROWS_B, 0:N_ROWS_B])\
                .then_inc(*t.filled[2].one())
            pe.wait_ge(sems["mixing_masked"], 1)
            free(3)
            for layer in range(DEPTH_2):
                for g in range(4):
                    m = pe.transpose(pair[3][:, layer, g * P:(g + 1) * P], wsg[:, layer, g, :], ident[:, :])
            m.then_inc(*t.filled[3].one())
            pe.wait_ge(sems["x_loaded"], 16)
            for layer, mixer in enumerate(MIXERS):
                if layer:
                    normed()
                turn(KT, h_tile)
                project_in(mixer)
                pe.wait_ge(*t["roped"].after())
                attend(mixer)
                if mixer == "diff":
                    pe.wait_ge(*t["o_normed"].after())
                    turn(KT, o_tile)
                    turned(KT)
                else:
                    pe.wait_ge(*t.emptied[3].now())
                project_out()
                normed()
                turn(KT, h_tile)
                mlp()
            pe.wait_ge(sems["h_ready"], 1)
            for layer in range(DEPTH_2):
                if layer:
                    normed()
                second(layer)
                emptied_by_layer.append({p: t.emptied[p].n for p in (2, 3)})

        @block.vector
        def _(dve):
            t = tallies()
            plan = block_plan()

            def step():
                dve.wait_ge(*t["dve_step"].now())

            def split():
                if not plan:
                    return
                s = t.block % 2
                for cols in halves(plan.pop(0)):
                    dve.wait_ge(*t["hi_split"].after())
                    dve.tensor_tensor(wlo[:, s, cols], raw[:, s, cols], whi[:, s, cols].bitcast(FP32), ALU.subtract)\
                        .then_inc(*t["lo_split"].one())
                t.block += 1

            def used():
                dve.wait_ge(*t["block_used"].after())

            def turn_split(n, scale_of):
                for kt in range(n):
                    p = kt // 4
                    if kt % 4 == 0:
                        t.filled[p].n += 1
                    if kt % 2 == 0:
                        dve.wait_ge(*t["xhi_written"].after(2))
                    g = scale_of(kt) if scale_of else 1.0
                    m = dve.scalar_tensor_tensor(out=xlo[:, kt, :], in0=pair_tile(kt), scalar=g,
                                                 in1=xhi[:, kt, :].bitcast(FP32), op0=ALU.mult, op1=ALU.subtract)
                    if kt % 4 == 3 or kt == n - 1:
                        m.then_inc(*t.emptied[p].one())

            def variances(parts, widths, root=True):
                dve.wait_ge(*t["squares_summed"].after(parts))
                at = 0
                for n, w in widths:
                    m = dve.tensor_scalar(var[:, at:at + n], ss[:, at:at + n], 1.0 / w, EPS, ALU.mult, ALU.add)
                    at += n
                if root:
                    m.then_inc(*t["var_ready"].one())
                    dve.wait_ge(*t["std_ready"].after())
                    dve.reciprocal(rstd[:, 0:at], std[:, 0:at]).then_inc(*t["rstd_ready"].one())
                    dve.wait_ge(*t["rstd_ready"].now())
                else:
                    m.then_inc(*t["dve_step"].one())
                    step()
                    dve.reciprocal(rstd[:, 0:at], var[:, 0:at]).then_inc(*t["dve_step"].one())
                    step()

            def norm(g, root=True):
                turn_split(KT, g)
                variances(TT, [(TT, D)], root)

            def project_odd(dst, w, p, scale):
                for tt in range(TT):
                    m = dve.tensor_scalar(dst(tt), pair[p][:, tt, 0:w], scale(tt), None, ALU.mult)
                m.then_inc(*t.emptied[p].one())

            def project_in(mixer):
                if mixer == "swa":
                    for n, w in in_blocks(mixer):
                        p = 2 + (n // BANK) % 2
                        used()
                        for tt in range(TT):
                            m = dve.scalar_tensor_tensor(out=qkv[:, tt, n:n + w], in0=pair[p][:, tt, 0:w],
                                                         scalar=rstd[:, tt:tt + 1], in1=swab[:, n:n + w],
                                                         op0=ALU.mult, op1=ALU.add)
                        m.then_inc(*t.emptied[p].one())
                        split()
                    return
                with dve.Fori(0, 3) as i:
                    turns(t, i, IN_TURN)
                    used()
                    t.emptied[2].n += 1
                    split()
                    used()
                    project_odd(lambda tt: qkv[:, tt, bass.ds(i * 1024 + BANK, BANK)], BANK, 3, lambda tt: rstd[:, tt:tt + 1])
                    split()
                after_turns(t, IN_TURN, 3, 2)
                del plan[:4]

            def rope(view, n, half, cos, sin):
                shape = [P, TT, n, half]
                x1, x2 = view(0, half), view(half, 2 * half)
                c = lanes(cos.unsqueeze(2), shape)
                s = lanes(sin.unsqueeze(2), shape)
                size = TT * n * half
                tmp = [qT[:, :, :].rearrange("p a b -> p (a b)")[:, k * size:(k + 1) * size]
                       .rearrange("p (t n f) -> p t n f", t=TT, n=n) for k in range(4)]
                for dst, x, y in ((tmp[0], x1, c), (tmp[1], x2, s), (tmp[2], x2, c), (tmp[3], x1, s)):
                    dve.tensor_tensor(dst, x, y, ALU.mult).then_inc(*t["dve_step"].one())
                step()
                dve.tensor_tensor(x1, tmp[0], tmp[1], ALU.subtract).then_inc(*t["dve_step"].one())
                return dve.tensor_tensor(x2, tmp[2], tmp[3], ALU.add)

            def prepare(mixer):
                dve.wait_ge(*t.emptied[2].now())
                dve.wait_ge(*t.emptied[3].now())
                n = 18 if mixer == "swa" else 32
                x = qkv[:, :, 0:n * HEAD].rearrange("p t (h d) -> p t h d", d=HEAD)
                m = rope(lambda lo, hi: x[:, :, :, lo:hi], n, HALF, cos1[:, :, :], sin1[:, :, :])
                if mixer == "swa":
                    m.then_inc(*t["dve_step"].one())
                    step()
                    k = qkv[:, :, 1024:1152].rearrange("p t (g d) -> p t g d", g=2)
                    both = qkv[:, :, 1280:1536].rearrange("p t (g r d) -> p t g r d", g=2, r=2)
                    for r in range(2):
                        m = dve.tensor_copy(both[:, :, :, r, :], k)
                m.then_inc(*t["roped"].one())

            def keys_out(mixer):
                rows = QK2 if mixer == "mla" else P
                for p in range(2):
                    t.filled[p].n += 1
                    t.emptied[p].n += 1
                for g in range((k_tiles(mixer) + 3) // 4):
                    p, n = 2 + g, min(4, k_tiles(mixer))
                    dve.wait_ge(*t.filled[p].after())
                    dve.tensor_copy(kT[0:rows, 4 * g:4 * g + n, :].rearrange("p j n -> p (j n)"),
                                    pair[p][0:rows, :, :].rearrange("p b n -> p (b n)")[:, 0:n * SEQ])\
                        .then_inc(*t.emptied[p].one())

            def shifts(mixer, hp):
                b = hp % 2
                dve.wait_ge(*t.filled[b].after())
                mask = band if mixer == "swa" else causal
                dve.tensor_tensor(sm[:, b, :, :], pair[b][:, :, 0:384], lanes(mask[:, :].unsqueeze(1), [P, 2, 384]), ALU.add)\
                    .then_inc(*t.emptied[b].one())
                dve.wait_ge(*t.emptied[b].now())
                for tt, cols in ((0, slice(0, P)), (1, slice(P, 3 * P))):
                    dve.tensor_reduce(mx[:, b, :, tt], sm[:, b, :, cols], AXIS.X, ALU.max).then_inc(*t["dve_step"].one())
                step()
                m = mx[:, b, :, :]
                if mixer == "swa":
                    dve.tensor_tensor(m, m, lanes(sinks8[:, 2 * hp:2 * hp + 2].unsqueeze(2), [P, 2, 2]), ALU.max)\
                        .then_inc(*t["dve_step"].one())
                    step()
                ins = dve.tensor_scalar(negm[:, b, :, :], m, -SCALE[mixer], None, ALU.mult)
                if mixer == "swa":
                    ins.then_inc(*t["dve_step"].one())
                    step()
                    ins = dve.tensor_tensor(snk[:, b, :, :], negm[:, b, :, :],
                                            lanes(sinks[:, 2 * hp:2 * hp + 2].unsqueeze(2), [P, 2, 2]), ALU.add)
                ins.then_inc(*t["shift_ready"].one())

            def probs(mixer, hp):
                b = hp % 2
                dve.wait_ge(*t["exp_done"].after())
                if mixer == "swa":
                    dve.tensor_tensor(sums[:, b, :, :], sums[:, b, :, :], snk[:, b, :, :], ALU.add).then_inc(*t["dve_step"].one())
                    step()
                dve.reciprocal(rinv[:, b, :, :], sums[:, b, :, :]).then_inc(*t["dve_step"].one())
                step()
                if mixer == "diff":
                    dve.tensor_scalar(rinv[:, b, 1, :], rinv[:, b, 1, :], neglam[:, t.lam:t.lam + 1], None, ALU.mult)\
                        .then_inc(*t["dve_step"].one())
                    step()
                    for tt, cols in ((0, slice(0, P)), (1, slice(P, 3 * P))):
                        dve.tensor_scalar(pT[:, b, 1, cols], sm[:, b, 1, cols], rinv[:, b, 1, tt:tt + 1], None, ALU.mult)\
                            .then_inc(*t["dve_step"].one())
                    step()
                    for tt, cols in ((0, slice(0, P)), (1, slice(P, 3 * P))):
                        m = dve.scalar_tensor_tensor(out=sm[:, b, 0, cols], in0=sm[:, b, 0, cols], scalar=rinv[:, b, 0, tt:tt + 1],
                                                     in1=pT[:, b, 1, cols], op0=ALU.mult, op1=ALU.add)
                else:
                    for tt, cols in ((0, slice(0, P)), (1, slice(P, 3 * P))):
                        w = cols.stop - cols.start
                        m = dve.tensor_tensor(sm[:, b, :, cols], sm[:, b, :, cols],
                                              lanes(rinv[:, b, :, tt:tt + 1], [P, 2, w]), ALU.mult)
                m.then_inc(*t["p_ready"].one())
                dve.wait_ge(*t["p_ready"].now())
                t.filled[2].n += 1
                t.emptied[2].n += 1

            def outputs(mixer, g):
                t.filled[3].n += 1
                if mixer in ("moba", "swa"):
                    dve.wait_ge(*t["xhi_written"].after())
                    dve.tensor_tensor(xlo[:, 4 * g:4 * g + 4, :], pair[3][:, :, :].rearrange("p b (j n) -> p (b j) n", j=2),
                                      xhi[:, 4 * g:4 * g + 4, :].bitcast(FP32), ALU.subtract).then_inc(*t.emptied[3].one())
                else:
                    t.emptied[3].n += 1

            def attend(mixer):
                keys_out(mixer)
                n = PAIRS[mixer]
                shifts(mixer, 0)
                for hp in range(n):
                    if hp + 1 < n:
                        shifts(mixer, hp + 1)
                    probs(mixer, hp)
                    if hp and (hp - 1) % 4 == 3:
                        outputs(mixer, (hp - 1) // 4)
                outputs(mixer, (n - 1) // 4)

            def roots16(n, w):
                dve.tensor_scalar(ss16[:, 0:n], ss16[:, 0:n], 1.0 / w, EPS, ALU.mult, ALU.add).then_inc(*t["sum16_ready"].one())
                dve.wait_ge(*t["std16_ready"].after())
                dve.reciprocal(rstd16[:, 0:n], std16[:, 0:n]).then_inc(*t["dve_step"].one())
                step()

            def sub_norm():
                dve.wait_ge(*t.emptied[3].now())
                o = qkv[:, :, 0:D]
                squares = qkv[:, :, D:2 * D]
                dve.tensor_tensor(squares, o, o, ALU.mult).then_inc(*t["dve_step"].one())
                step()
                dve.tensor_reduce(ss16[:, 0:16].rearrange("p (t h) -> p t h", t=TT),
                                  squares.rearrange("p t (h e) -> p t h e", e=P), AXIS.X, ALU.add).then_inc(*t["dve_step"].one())
                step()
                roots16(16, P)
                ov = o.rearrange("p t (h e) -> p t h e", e=P)
                r = rstd16[:, 0:16].rearrange("p (t h) -> p t h", t=TT).unsqueeze(3)
                dve.tensor_tensor(ov, ov, lanes(r, [P, TT, 8, P]), ALU.mult).then_inc(*t["o_normed"].one())

            def project_out():
                for n in range(2):
                    used()
                    cols = slice(n * BANK, (n + 1) * BANK)
                    dve.tensor_tensor(h[:, :, cols], pair[2 + n][:, :, :], h[:, :, cols], ALU.add)\
                        .then_inc(*t.emptied[2 + n].one())
                    split()

            def mlp():
                def up(j):
                    b = j % 2
                    used()
                    dve.wait_ge(*t.emptied[b].after())
                    if t["alo_written"].n:
                        dve.wait_ge(*t["alo_written"].now())
                    dve.tensor_tensor(square_at, relu_at[b], relu_at[b], ALU.mult).then_inc(*t["dve_step"].one())
                    dve.wait_ge(*t["ahi_written"].after())
                    step()
                    dve.tensor_tensor(alo[:, b, :, :].rearrange("p f n -> p (f n)"), square_at,
                                      ahi[:, b, :, :].rearrange("p f n -> p (f n)").bitcast(FP32), ALU.subtract)\
                        .then_inc(*t["alo_written"].one())
                    split()

                def down():
                    used()
                    split()

                up(0)
                up(1)
                down()
                per = dict(MLP_TURN, dve_step=2)
                with dve.Fori(0, 3) as i:
                    turns(t, i, per)
                    up(0)
                    down()
                    up(1)
                    down()
                after_turns(t, per, 3, 4)
                del plan[:8]
                used()
                for n in range(2):
                    cols = slice(n * BANK, (n + 1) * BANK)
                    for tt in range(TT):
                        m = dve.scalar_tensor_tensor(out=h[:, tt, cols], in0=pair[2 + n][:, tt, :], scalar=rstd[:, tt:tt + 1],
                                                     in1=h[:, tt, cols], op0=ALU.mult, op1=ALU.add)
                    m.then_inc(*t.emptied[2 + n].one())
                split()

            def chain(m):
                m.then_inc(*t["dve_step"].one())
                step()

            def layer_norm(src, dst, g, b, centred):
                for tt in range(TT):
                    m = dve.bn_stats(bn6[:, tt, :], src(tt))
                chain(m)
                for tt in range(TT):
                    m = dve.bn_aggr(bn2[:, tt, :], bn6[:, tt, :])
                chain(m)
                dve.tensor_scalar(var[:, 0:TT], bn2[:, :, 1], EPS, None, ALU.add).then_inc(*t["var_ready"].one())
                dve.wait_ge(*t["std_ready"].after())
                chain(dve.reciprocal(rstd[:, 0:TT], std[:, 0:TT]))
                for tt in range(TT):
                    m = dve.tensor_scalar(dst[:, tt, :], src(tt), bn2[:, tt, 0:1], rstd[:, tt:tt + 1], ALU.subtract, ALU.mult)
                m.then_inc(*centred.one())
                dve.wait_ge(*centred.now())
                chain(dve.tensor_tensor(dst, dst, lanes(g.unsqueeze(1), [P, TT, 256]), ALU.mult))
                return dve.tensor_tensor(dst, dst, lanes(b.unsqueeze(1), [P, TT, 256]), ALU.add)

            def second(layer):
                norm(gain("norm_g_2", layer))
                for n, (c0, w) in enumerate(W_IN_2_BLOCKS):
                    used()
                    if n % 2:
                        project_odd(lambda tt: qkv[:, tt, c0:c0 + w], w, 3, lambda tt: rstd[:, tt:tt + 1])
                    else:
                        t.emptied[2].n += 1
                    split()
                turn_split(8, gain_latent(layer))
                variances(4, [(2, QL), (2, KVL)])
                for n in range(2):
                    used()
                    if n:
                        project_odd(lambda tt: qbuf[:, tt, 384:768], 384, 3, lambda tt: rstd[:, tt:tt + 1])
                    else:
                        t.emptied[2].n += 1
                    split()
                for n in range(2):
                    used()
                    if n:
                        project_odd(lambda tt: kvbuf[:, tt, BANK:2 * BANK], BANK, 3, lambda tt: rstd[:, 2 + tt:3 + tt])
                    else:
                        t.emptied[2].n += 1
                    split()
                dve.wait_ge(*t.emptied[2].now())
                dve.wait_ge(*t.emptied[3].now())
                dve.wait_ge(*t["spread_loaded"].after(16 * len(SPREAD_2)))
                if layer == 0:
                    chain(dve.memset(ypad[:, :, 0:CONV_K - 1], 0.0))
                dve.wait_ge(*t["sig_ready"].after())
                dve.tensor_tensor(qkv[:, :, A0:A0 + CW], qkv[:, :, A0:A0 + CW], qkv[:, :, GLU0:GLU0 + CW], ALU.mult)\
                    .then_inc(*t["glu_ready"].one())
                t.filled[0].n += 1
                dve.wait_ge(*t.emptied[0].after())
                at = layer * CONV_K * 2
                for k in range(CONV_K):
                    for ct in range(2):
                        w = colsA[:, at + 2 * k + ct:at + 2 * k + ct + 1]
                        bias = colsA[:, ROW_AT["conv_b_2"] + 2 * layer + ct:ROW_AT["conv_b_2"] + 2 * layer + ct + 1]
                        y = ypad[:, ct, k:k + SEQ]
                        if k == 0:
                            m = dve.tensor_scalar(yacc[:, ct, :], y, w, bias, ALU.mult, ALU.add)
                        else:
                            dve.wait_ge(*t["dve_step"].now(1))
                            m = dve.scalar_tensor_tensor(out=yacc[:, ct, :], in0=y, scalar=w, in1=yacc[:, ct, :],
                                                         op0=ALU.mult, op1=ALU.add)
                        if (k, ct) != (CONV_K - 1, 1):
                            m.then_inc(*t["dve_step"].one())
                m.then_inc(*t["conv_ready"].one())
                dve.wait_ge(*t.filled[1].after())
                m = layer_norm(lambda tt: pair[1][:, 0, tt * CW:(tt + 1) * CW], qkv[:, :, 0:CW], param2("conv_ln_g_2"),
                               param2("conv_ln_b_2"), t.emptied[1])
                m.then_inc(*t["ln_ready"].one())
                turn_split(2, None)
                q = qbuf[:, :, :].rearrange("p t (h d) -> p t h d", d=QK2)
                k = kfull[:, :, :].rearrange("p t (h d) -> p t h d", d=QK2)
                kv = kvbuf[:, :, :].rearrange("p t (h d) -> p t h d", d=NOPE + V2)
                dve.tensor_copy(k[:, :, :, 0:NOPE], kv[:, :, :, 0:NOPE]).then_inc(*t["dve_step"].one())
                kr = qkv[:, :, KR0:KR0 + ROPE2].unsqueeze(2)
                dve.tensor_copy(k[:, :, :, NOPE:QK2], lanes(kr, [P, TT, H2, ROPE2])).then_inc(*t["dve_step"].one())
                step()
                squares = kT[:, :, :].rearrange("p a b -> p (a b)")[:, 0:TT * H2 * QK2].rearrange("p (t h d) -> p t h d", t=TT, d=QK2)
                for n, x in enumerate((q, k)):
                    chain(dve.tensor_tensor(squares, x, x, ALU.mult))
                    chain(dve.tensor_reduce(ss16[:, 16 * n:16 * n + 16].rearrange("p (t h) -> p t h", t=TT), squares,
                                            AXIS.X, ALU.add))
                used()
                for tt in range(TT):
                    m = dve.tensor_tensor(yacc[:, tt, :], pair[2][:, tt, 0:CW], param2("conv_pw_b_2"), ALU.add)
                m.then_inc(*t.emptied[2].one())
                dve.wait_ge(*t.emptied[2].now())
                dve.wait_ge(*t["zsilu_ready"].after())
                chain(dve.tensor_tensor(qkv[:, :, ZC0:ZC0 + CW], qkv[:, :, ZC0:ZC0 + CW], yacc[:, :, :], ALU.mult))
                split()
                roots16(32, QK2)
                for n, (x, g) in enumerate(((q, "qk_q_g_2"), (k, "qk_k_g_2"))):
                    r = rstd16[:, 16 * n:16 * n + 16].rearrange("p (t h) -> p t h", t=TT).unsqueeze(3)
                    chain(dve.tensor_tensor(x, x, lanes(r, [P, TT, H2, QK2]), ALU.mult))
                    for tt in range(TT):
                        m = dve.tensor_tensor(x[:, tt], x[:, tt], lanes(param2(g).unsqueeze(1), [P, H2, QK2]), ALU.mult)
                    chain(m)
                    m = rope(lambda lo, hi: x[:, :, :, NOPE + lo:NOPE + hi], H2, HALF2, cs2[:, 0, :, :], cs2[:, 1, :, :])
                    if n == 0:
                        chain(m)
                m.then_inc(*t["qk_ready"].one())
                attend("mla")
                v = qkv[:, :, V0:V0 + SGW]
                dve.wait_ge(*t["gelu_ready"].after())
                layer_norm(lambda tt: v[:, tt, :], v, param2("sg_ln_g_2"), param2("sg_ln_b_2"), t["dve_step"])\
                    .then_inc(*t["vln_ready"].one())
                dve.wait_ge(*t["zsilu_ready"].after())
                dve.wait_ge(*t.emptied[3].now())
                chain(dve.tensor_tensor(qbuf[:, :, 0:MLAW], qbuf[:, :, 0:MLAW], qkv[:, :, ZM0:ZM0 + MLAW], ALU.mult))
                dve.wait_ge(*t["gelu_ready"].after())
                dve.wait_ge(*t.filled[1].after())
                for g in range(4):
                    u = qkv[:, :, U0 + g * 64:U0 + (g + 1) * 64]
                    at = ROW_AT["sg_b_2"] + layer * 4 + g
                    m = dve.scalar_tensor_tensor(out=u, in0=pair[1][:, :, g * 64:(g + 1) * 64], scalar=colsB[:, at:at + 1], in1=u,
                                                 op0=ALU.add, op1=ALU.mult)
                m.then_inc(*t.emptied[1].one())
                dve.wait_ge(*t.emptied[1].now())
                dve.wait_ge(*t["zsilu_ready"].after())
                dve.tensor_tensor(qkv[:, :, U0:U0 + SGW], qkv[:, :, U0:U0 + SGW], qkv[:, :, ZS0:ZS0 + SGW], ALU.mult)\
                    .then_inc(*t["branches_ready"].one())
                variances(6, [(2, CW), (2, MLAW), (2, SGW)])
                for n in range(3):
                    for tt in range(TT):
                        m = dve.tensor_scalar(branch(n)[:, tt, :], branch(n)[:, tt, :], rstd[:, 2 * n + tt:2 * n + tt + 1], None,
                                              ALU.mult)
                m.then_inc(*t["y_ready"].one())
                turn_split(KT, gain("branch_norm_g_2", layer))
                project_out()

            dve.wait_ge(sems["params_loaded"], 16 * PARAMS)
            for n in range(2):
                m = dve.tensor_tensor(lamv[:, 2 * n, :], lamv[:, 2 * n, :], lamv[:, 2 * n + 1, :], ALU.mult)
            chain(m)
            for n in range(2):
                m = dve.tensor_reduce(lams[:, 2 * n:2 * n + 2], lamv[:, 2 * n, :].rearrange("p (s d) -> p s d", d=HEAD),
                                      AXIS.X, ALU.add)
            chain(m)
            chain(dve.tensor_copy(pos[:, :], pos_i[:, :]))
            for tt in range(TT):
                m = dve.tensor_scalar(ang[:, tt, :], inv[:, :], pos[:, tt:tt + 1], None, ALU.mult)
            chain(m)
            chain(dve.tensor_scalar(turns_of[:, :, :], ang[:, :, :], 1.0 / (2 * math.pi), ROUND, ALU.mult, ALU.add))
            chain(dve.tensor_scalar(turns_of[:, :, :], turns_of[:, :, :], -ROUND, None, ALU.add))
            for part in TURN_PARTS:
                chain(dve.scalar_tensor_tensor(out=ang[:, :, :], in0=turns_of[:, :, :], scalar=-part, in1=ang[:, :, :],
                                               op0=ALU.mult, op1=ALU.add))
            chain(dve.tensor_scalar(cos1[:, :, :], ang[:, :, :], math.pi / 2, None, ALU.add))
            chain(dve.tensor_scalar(turns_of[:, :, :], cos1[:, :, :], math.pi, -2 * math.pi, ALU.is_gt, ALU.mult))
            chain(dve.tensor_tensor(cos1[:, :, :], cos1[:, :, :], turns_of[:, :, :], ALU.add))
            dve.tensor_scalar(sin1[:, :, :], ang[:, :, :], PI_BELOW, -PI_BELOW, ALU.min, ALU.max).then_inc(*t["dve_step"].one())
            dve.tensor_scalar(cos1[:, :, :], cos1[:, :, :], PI_BELOW, -PI_BELOW, ALU.min, ALU.max).then_inc(*t["angles_ready"].one())
            dve.tensor_scalar(sinks8[:, :], sinks[:, :], 1.0 / SCALE["swa"], None, ALU.mult).then_inc(*t["dve_step"].one())
            split()
            split()
            t.filled[2].n += 1
            t.filled[3].n += 1
            dve.wait_ge(*t.emptied[2].after())
            dve.wait_ge(*t.emptied[3].after())
            dve.wait_ge(*t["sines_ready"].after(3))
            chain(dve.tensor_tensor(neglam[:, :], lams[:, 2:4], lams[:, 0:2], ALU.subtract))
            for n, layer in enumerate(LAMBDA_INIT):
                at = ROW_AT["diff_subln_g"] + n
                dve.tensor_scalar(neglam[:, n:n + 1], neglam[:, n:n + 1], -LAMBDA_INIT[layer], None, ALU.add)\
                    .then_inc(*t["dve_step"].one())
                dve.tensor_scalar(subg[:, n:n + 1], colsB[:, at:at + 1], 1.0 - LAMBDA_INIT[layer], None, ALU.mult)\
                    .then_inc(*t["params_ready"].one())
            step()

            for layer, mixer in enumerate(MIXERS):
                t.lam = layer // 3
                norm(gain("attn_norm_g", layer))
                project_in(mixer)
                prepare(mixer)
                attend(mixer)
                if mixer == "diff":
                    sub_norm()
                    turn_split(KT, gain_sub(t.lam))
                project_out()
                norm(gain("mlp_norm_g", layer), root=False)
                mlp()
            variances(TT, [(TT, D)])
            dve.wait_ge(sems["gains_loaded"], 16)
            for tt in range(TT):
                m = dve.scalar_tensor_tensor(out=h[:, tt, :], in0=h[:, tt, :], scalar=rstd[:, tt:tt + 1], in1=fing,
                                             op0=ALU.mult, op1=ALU.mult)
            m.then_inc(*t["h_ready"].one())
            dve.wait_ge(*t["h_ready"].now())
            for layer in range(DEPTH_2):
                second(layer)

        @block.sync
        def _(sp):
            t = tallies()

            def load(src, T, w):
                s = t.block % 2
                if t.block >= 2:
                    sp.wait_ge(*t["lo_split"].now(2))
                sp.dma_start(slot(raw, s, T, w), src).then_inc(*t.loaded[s].one(16))
                t["lo_split"].n += 2
                t.block += 1

            def tiles(w):
                return w.rearrange("(t p) n -> p t n", p=P)

            def loads(mixer, w_in, w_out):
                if mixer == "swa":
                    for n, w in in_blocks(mixer):
                        load(tiles(w_in[:, n:n + w]), KT, w)
                else:
                    first = 0 if t.block else 1
                    for b in range(2 * first):
                        load(tiles(w_in[:, b * BANK:(b + 1) * BANK]), KT, BANK)
                    with sp.Fori(0, 3 - first) as i:
                        turns(t, i, IN_TURN)
                        for b in range(2):
                            load(tiles(w_in[:, bass.ds(i * 1024 + (2 * first + b) * BANK, BANK)]), KT, BANK)
                    after_turns(t, IN_TURN, 3 - first, 2)
                out_loads(w_out)

            def out_loads(w_out):
                for n in range(2):
                    load(tiles(w_out[:, n * BANK:(n + 1) * BANK]), KT, BANK)

            def mlp_loads(w_up, w_down):
                def up(j):
                    load(tiles(w_up[:, bass.ds(j * BANK, BANK)]), KT, BANK)

                def down(j):
                    load(tiles(w_down[bass.ds(j * BANK, BANK), :]), 4, D)

                up(0)
                up(1)
                down(0)
                with sp.Fori(0, 3) as i:
                    turns(t, i, MLP_TURN)
                    for b in range(2):
                        up(2 * i + 2 + b)
                        down(2 * i + 1 + b)
                after_turns(t, MLP_TURN, 3, 4)
                down(7)

            sp.dma_start(h[:, :, :], a["x"][0].rearrange("(t p) n -> p t n", p=P)).then_inc(*t["x_loaded"].one(16))
            for layer, mixer in enumerate(MIXERS):
                which = layer // 3
                name = {"diff": "diff", "moba": "moba", "swa": "swa"}[mixer]
                loads(mixer, a[f"{name}_w_in"][which], a[f"{name}_w_out"][which])
                mlp_loads(a["mlp_w_up"][layer], a["mlp_w_down"][layer])
            for layer in range(DEPTH_2):
                w_in = a["w_in_2"][layer]
                for n, w in W_IN_2_BLOCKS:
                    load(tiles(w_in[:, n:n + w]), KT, w)
                for n in range(2):
                    load(tiles(a["w_uq_2"][layer][:, n * 384:(n + 1) * 384]), 6, 384)
                for n in range(2):
                    load(tiles(a["w_ukv_2"][layer][:, n * BANK:(n + 1) * BANK]), 2, BANK)
                load(tiles(a["conv_pw_w_2"][layer]), 2, CW)
                out_loads(a["w_out_2"][layer])
            for p in (2, 3):
                sp.wait_ge(sems[f"emptied{p}"], emptied_by_layer[-1][p])
            sp.dma_start(out[0].rearrange("(t p) n -> p t n", p=P), h[:, :, :]).then_inc(*t["stored"].one(16))
            sp.wait_ge(*t["stored"].now())

        @block.gpsimd
        def _(pool):
            t = tallies()
            pool.dma_start(pos_i[:, :], a["positions"][0].rearrange("(t p) -> p t", p=P),
                           allow_slow_non_contiguous=True).then_inc(*t["params_loaded"].one(16))
            pool.dma_start(inv[:, :], a["inv_freq"].partition_broadcast(P)).then_inc(*t["params_loaded"].one(16))
            for n, key in enumerate(LAMBDAS):
                pool.dma_start(lamv[:, n, :], a[key].rearrange("s d -> (s d)").partition_broadcast(P))\
                    .then_inc(*t["params_loaded"].one(16))
            pool.dma_start(sinks[:, :], a["swa_sinks"][0].partition_broadcast(P)).then_inc(*t["params_loaded"].one(16))
            pool.dma_start(swab[:, :], a["swa_b_in"][0].partition_broadcast(P)).then_inc(*t["params_loaded"].one(16))
            for layer in range(DEPTH_2):
                pool.dma_start(wsg[:, layer, :, :], a["sg_w_2"][layer].rearrange("g t s -> t g s"))\
                    .then_inc(*t["mixing_loaded"].one(16))
            for n, key in enumerate(["cos_2", "sin_2"]):
                pool.dma_start(cs2[:, n, :, :], a[key].rearrange("(t p) n -> p t n", p=P)).then_inc(*t["params_loaded"].one(16))
            pool.memset(ident[:, :], 0.0).then_inc(*t["pool_step"].one())
            pool.memset(causal[:, :], 0.0).then_inc(*t["pool_step"].one())
            pool.memset(band[:, :], 0.0).then_inc(*t["pool_step"].one())
            pool.wait_ge(*t["pool_step"].now())
            pool.affine_select(out=ident[:, :], in_=ident[:, :], compare_op=ALU.not_equal, fill=1.0, base=0,
                               pattern=[[-1, P]], channel_multiplier=1).then_inc(*t["consts_made"].one())
            for m in (causal, band):
                for at in (0, 2 * P):
                    pool.affine_select(out=m[:, at:at + P], in_=m[:, at:at + P], compare_op=ALU.is_ge, fill=NEG, base=0,
                                       pattern=[[-1, P]], channel_multiplier=1).then_inc(*t["consts_made"].one())
            pool.affine_select(out=band[:, P:2 * P], in_=band[:, P:2 * P], compare_op=ALU.is_gt, fill=NEG, base=0,
                               pattern=[[1, P]], channel_multiplier=-1).then_inc(*t["consts_made"].one())
            pool.wait_ge(*t["mixing_loaded"].now())
            pool.affine_select(out=wsg[:, :, :, :].rearrange("p l g s -> p (l g) s"),
                               in_=wsg[:, :, :, :].rearrange("p l g s -> p (l g) s"), compare_op=ALU.is_ge, fill=0.0, base=0,
                               pattern=[[0, DEPTH_2 * 4], [-1, P]], channel_multiplier=1).then_inc(*t["mixing_masked"].one())
            pool.wait_ge(sems["block_used"], sum(len(in_blocks(m)) + 2 + 2 * (FF // BANK) for m in MIXERS[:3]))
            pool.dma_start(fing, a["final_norm_g"].partition_broadcast(P)).then_inc(*t["gains_loaded"].one(16))
            for layer in range(DEPTH_2):
                if layer == 0:
                    pool.wait_ge(sems["h_ready"], 1)
                else:
                    for p in (2, 3):
                        pool.wait_ge(sems[f"emptied{p}"], emptied_by_layer[layer - 1][p])
                for name, _ in SPREAD_2:
                    pool.dma_start(param2(name), a[name][layer].partition_broadcast(P)).then_inc(*t["spread_loaded"].one(16))


_INS = ["x", "positions", "attn_norm_g", "mlp_norm_g", "diff_w_in", "diff_w_out", "diff_lam_q1", "diff_lam_k1", "diff_lam_q2",
        "diff_lam_k2", "diff_subln_g", "moba_w_in", "moba_w_out", "swa_w_in", "swa_b_in", "swa_sinks", "swa_w_out",
        "mlp_w_up", "mlp_w_down", "final_norm_g", "norm_g_2", "w_in_2", "conv_w_2", "conv_b_2", "conv_ln_g_2", "conv_ln_b_2",
        "conv_pw_w_2", "conv_pw_b_2", "q_norm_g_2", "w_uq_2", "kv_norm_g_2", "w_ukv_2", "qk_q_g_2", "qk_k_g_2", "sg_ln_g_2",
        "sg_ln_b_2", "sg_w_2", "sg_b_2", "branch_norm_g_2", "w_out_2"]


def _tables():
    f = np.float32
    inv1 = f(ROPE_THETA) ** (-np.arange(0, 2 * HALF, 2, dtype=f) / f(2 * HALF))
    inv2 = f(10000.0) ** (-np.arange(HALF2, dtype=f) / f(HALF2))
    angle = np.arange(SEQ, dtype=f)[:, None] * inv2[None, :].astype(f)
    return {"inv_freq": inv1.astype(f), "cos_2": np.cos(angle).astype(f), "sin_2": np.sin(angle).astype(f)}


def kernel(**inputs):
    import concourse.bacc as _bacc
    from concourse.bass_utils import run_bass_kernel_spmd as _run

    nc = _bacc.Bacc("TRN2", target_bir_lowering=False, num_devices=1)
    arrays, args = {}, {}
    for name, v in [(n, inputs[n]) for n in _INS] + list(_tables().items()):
        v = np.ascontiguousarray(v)
        arrays[f"in_{name}"] = v
        args[name] = nc.dram_tensor(f"in_{name}", v.shape, mybir.dt.from_np(v.dtype), kind="ExternalInput").ap()
    result = nc.dram_tensor("result", (1, SEQ, D), FP32, kind="ExternalOutput").ap()
    build(nc, args, result)
    r = _run(nc, [arrays], core_ids=[0])
    return r.results[0]["result"]
```

```python
import math
from contextlib import ExitStack

import concourse.bass as bass
import numpy as np
from concourse import mybir

FP32 = mybir.dt.float32
FP32R = mybir.dt.float32r
INT32 = mybir.dt.int32
BF16 = mybir.dt.bfloat16
ALU = mybir.AluOpType
ACT = mybir.ActivationFunctionType
AXIS = mybir.AxisListType

P = 128
SEQ, D = 256, 1024
TT = SEQ // P
KT = D // P
FF = 4 * D
DEPTH, DEPTH_2 = 4, 2
HEAD = 64
EPS = 1e-6
HALF = 8
ROPE_THETA = 500000.0
NEG = -1.0e30
BANK = 512
SLOT = 4096
CONV_K = 31
ROUND = 1.5 * 2.0 ** 23
TURN_PARTS = [6.28125, 0.0019350051879882812, 3.019916050e-07]
PI_BELOW = 3.1415925
PARAMS = 10
CW, SGW, MLAW = 256, 256, 512
NOPE, ROPE2, QK2, V2, H2 = 64, 32, 96, 64, 8
HALF2 = ROPE2 // 2
QL, KVL = 768, 256
IN_COLS = 3104
A0, GLU0, ZC0, CQ0, CKV0, KR0, ZM0, U0, V0, ZS0 = 0, 256, 512, 768, 1536, 1792, 1824, 2336, 2592, 2848
W_IN_2_BLOCKS = [(0, 512), (2336, 512), (512, 512), (1024, 512), (1536, 288), (1824, 512), (2848, 256)]
MIXERS = ["diff", "moba", "swa", "diff"]
QKV_COLS = {"diff": 3072, "moba": 3072, "swa": 1280}
LAMBDAS = ["diff_lam_q1", "diff_lam_k1", "diff_lam_q2", "diff_lam_k2"]
LAMBDA_INIT = {0: 0.8 - 0.6 * math.exp(-0.3 * 0), 3: 0.8 - 0.6 * math.exp(-0.3 * 3)}

ROWS_A = [("conv_w_2", DEPTH_2 * CONV_K * 2), ("conv_b_2", DEPTH_2 * 2)]
ROWS_B = [("attn_norm_g", DEPTH * KT), ("mlp_norm_g", DEPTH * KT), ("diff_subln_g", 2), ("norm_g_2", DEPTH_2 * KT),
          ("q_norm_g_2", DEPTH_2 * 6), ("kv_norm_g_2", DEPTH_2 * 2), ("branch_norm_g_2", DEPTH_2 * KT),
          ("sg_b_2", DEPTH_2 * 4)]
N_ROWS_A = sum(n for _, n in ROWS_A)
N_ROWS_B = sum(n for _, n in ROWS_B)
ROW_AT = {}
for _rows in (ROWS_A, ROWS_B):
    _at = 0
    for _name, _n in _rows:
        ROW_AT[_name] = _at
        _at += _n
SPREAD_2 = [("conv_ln_g_2", CW), ("conv_ln_b_2", CW), ("conv_pw_b_2", CW), ("sg_ln_g_2", SGW), ("sg_ln_b_2", SGW),
            ("qk_q_g_2", QK2), ("qk_k_g_2", QK2)]
SPREAD_AT = {}
_at = 0
for _name, _n in SPREAD_2:
    SPREAD_AT[_name] = (_at, _n)
    _at += _n
SPREAD_COLS = _at


class Tally:

    def __init__(self, sem):
        self.sem, self.n, self.turn = sem, 0, 0

    def one(self, k=1):
        self.n += k
        return self.sem, k

    def after(self, k=1):
        self.n += k
        return self.sem, self.n + self.turn

    def now(self, back=0):
        return self.sem, self.n - back + self.turn


class Tallies:

    def __init__(self, sems):
        self.of = {name: Tally(s) for name, s in sems.items()}
        self.loaded = [self.of[f"raw_loaded{s}"] for s in range(2)]
        self.filled = [self.of[f"filled{p}"] for p in range(8)]
        self.emptied = [self.of[f"emptied{p}"] for p in range(8)]
        self.block = 0
        self.lam = 0

    def __getitem__(self, name):
        return self.of[name]


def build(nc, a, out):
    ctx = ExitStack()
    with ctx:
        def sb(name, shape, dt=FP32):
            return ctx.enter_context(nc.sbuf_tensor(name, shape, dt))

        raw = sb("raw", [P, 2, SLOT])
        whi = sb("whi", [P, 2, SLOT], FP32R)
        wlo = sb("wlo", [P, 2, SLOT], FP32R)
        h = sb("h", [P, TT, D])
        xhi = sb("xhi", [P, KT, SEQ], FP32R)
        xlo = sb("xlo", [P, KT, SEQ], FP32R)
        qkv = sb("qkv", [P, TT, IN_COLS])
        qT = sb("qT", [P, 8, SEQ])
        kT = sb("kT", [P, 8, SEQ])
        sm = sb("sm", [P, 2, 2, 384])
        pT = sb("pT", [P, 2, 2, 384])
        ident = sb("ident", [P, P])
        ident_b = sb("ident_b", [P, P], BF16)
        causal = sb("causal", [P, 384], BF16)
        band = sb("band", [P, 384], BF16)
        colsA = sb("colsA", [P, N_ROWS_A])
        colsB = sb("colsB", [P, N_ROWS_B])
        subg = sb("subg", [P, 2])
        sinks = sb("sinks", [P, 16])
        sinks8 = sb("sinks8", [P, 16])
        wsg = sb("wsg", [P, DEPTH_2, 4, P])
        pos_i = sb("pos_i", [P, TT], INT32)
        pos = sb("pos", [P, TT])
        inv = sb("inv", [P, HALF])
        cos1 = sb("cos1", [P, TT, HALF])
        sin1 = sb("sin1", [P, TT, HALF])
        cs2 = sb("cs2", [P, 2, TT, HALF2])
        ang = sb("ang", [P, TT, HALF])
        turns_of = sb("turns_of", [P, TT, HALF])
        rope_tmp = sb("rope_tmp", [P, 4 * TT * 8 * HALF])
        lams = sb("lams", [P, 4])
        neglam = sb("neglam", [P, 2])
        ss = sb("ss", [P, 8])
        var = sb("var", [P, 8])
        std = sb("std", [P, 8])
        rstd = sb("rstd", [P, 8])
        ss16 = sb("ss16", [P, 32])
        std16 = sb("std16", [P, 32])
        rstd16 = sb("rstd16", [P, 32])
        mx = sb("mx", [P, 2, 2, 2])
        negm = sb("negm", [P, 2, 2, 2])
        snk = sb("snk", [P, 8, 2, 2])
        sums = sb("sums", [P, 8, 2, 2])
        rinv = sb("rinv", [P, 8, 2, 2])
        bn6 = sb("bn6", [P, TT, 6])
        bn2 = sb("bn2", [P, TT, 2])

        first = ExitStack()
        ahi = first.enter_context(nc.sbuf_tensor("ahi", [P, 2, 4, SEQ], FP32R))
        alo = first.enter_context(nc.sbuf_tensor("alo", [P, 2, 4, SEQ], FP32R))
        swab = first.enter_context(nc.sbuf_tensor("swab", [P, QKV_COLS["swa"]], FP32))
        fing = swab[:, 0:D]
        first.close()
        qbuf = sb("qbuf", [P, TT, H2 * QK2])
        kfull = sb("kfull", [P, TT, H2 * QK2])
        kvbuf = qkv[:, :, CQ0:CQ0 + H2 * (NOPE + V2)]
        ypad = sb("ypad", [P, 2, CONV_K - 1 + SEQ])
        yacc = sb("yacc", [P, 2, SEQ])
        spread = sb("spread", [P, SPREAD_COLS])

        relu_at = [qkv[:, 0, j * 1024:(j + 1) * 1024] for j in range(2)]
        square_at = qkv[:, 1, 0:1024]
        lamv = qT[:, 0:2, :].rearrange("p a (b n) -> p (a b) n", b=2)

        pair = [ctx.enter_context(nc.psum_tensor(f"pair{i}", [P, 2, BANK], FP32)) for i in range(4)]

        sem_names = ["raw_loaded0", "raw_loaded1", "hi_split", "lo_split", "block_used",
                     "filled0", "filled1", "filled2", "filled3", "filled4", "filled5", "filled6", "filled7",
                     "emptied0", "emptied1", "emptied2", "emptied3", "emptied4", "emptied5", "emptied6", "emptied7",
                     "x_loaded", "params_loaded", "rows_loaded", "mixing_loaded", "gains_loaded", "spread_loaded",
                     "pool_step", "consts_made", "mixing_masked", "dve_step", "angles_ready", "sines_ready", "params_ready",
                     "xhi_written", "squares_summed", "var_ready", "std_ready", "rstd_ready", "sum16_ready", "std16_ready",
                     "ahi_written", "alo_written", "roped", "shift_ready", "sink_ready", "p_ready", "o_normed", "h_ready",
                     "sig_ready", "glu_ready", "conv_ready", "ln_ready", "silu_ready", "zsilu_ready", "qk_ready", "gelu_ready",
                     "vln_ready", "branches_ready", "y_ready", "stored"]
        sems = {n: ctx.enter_context(nc.semaphore(n)) for n in sem_names}

        def tallies():
            return Tallies(sems)

        def turns(t, i, per):
            for name, k in per.items():
                t[name].turn = i * k

        def after_turns(t, per, count, blocks):
            for name, k in per.items():
                t[name].turn = 0
                t[name].n += (count - 1) * k
            t.block += (count - 1) * blocks

        MLP_TURN = {"raw_loaded0": 32, "raw_loaded1": 32, "hi_split": 8, "lo_split": 8, "block_used": 8,
                    "emptied0": 1, "emptied1": 1, "ahi_written": 2, "alo_written": 2}

        def slot(buf, s, T, w):
            return buf[:, s, 0:T * w].rearrange("p (t n) -> p t n", t=T)

        def halves(n):
            return [slice(0, n // 2), slice(n // 2, n)]

        def block_plan():
            full, plan = KT * BANK, []
            for mixer in MIXERS:
                plan += [KT * w for _, w in in_blocks(mixer)] + [full] * (2 + 2 * (FF // BANK))
            for _ in range(DEPTH_2):
                plan += [KT * w for _, w in W_IN_2_BLOCKS] + [6 * 384] * 2 + [2 * BANK] * 2 + [2 * CW] + [full] * 2
            return plan

        def gain(name, layer, n=KT):
            at = ROW_AT[name] + layer * n
            return lambda kt: colsB[:, at + kt:at + kt + 1]

        def gain_latent(layer):
            q, kv = gain("q_norm_g_2", layer, 6), gain("kv_norm_g_2", layer, 2)
            return lambda kt: q(kt) if kt < 6 else kv(kt - 6)

        def gain_sub(which):
            return lambda kt: subg[:, which:which + 1]

        def param2(name):
            at, n = SPREAD_AT[name]
            return spread[:, at:at + n]

        def lanes(ap, shape):
            return ap.to_broadcast(shape)

        def in_blocks(mixer):
            if mixer == "swa":
                return [(1024, 256), (0, BANK), (BANK, BANK)]
            return [(part * D + g * BANK, BANK) for g in range(2) for part in range(3)]

        EIGHTHS = 8

        def mixer_steps(mixer):
            def eighths(what, b):
                return [[(what, b, e)] + ([(what + "_results", b)] if e == EIGHTHS - 1 else []) for e in range(EIGHTHS)]

            def take(fill, n):
                return sum([fill.pop(0) for _ in range(n)], [])

            def head_pair(h, fill, before, after, half=None):
                split = [] if half is None else [("split", half)]
                return ([("scores", h)] + take(fill, before) + [("turn", h)] + split + take(fill, after) + [("mix", h)]
                        + ([("outputs", h // 2)] if h % 2 else []))

            def norm(q):
                return [("o_norm", q)] if mixer == "diff" else []

            both = [("split", 0), ("split", 1)]
            ins = [eighths("in", b) for b in range(len(in_blocks(mixer)))]
            out0, out1 = eighths("out", 0), eighths("out", 1)
            steps = take(ins[0], 8) + both + take(ins[1], 8) + [("rope", 0)]
            if mixer == "swa":
                steps += [("split", 0)] + take(ins[2], 4) + [("heads", 0)] + head_pair(0, ins[2], 2, 0, 1)
                steps += head_pair(1, ins[2], 2, 0) + [("rope", 1), ("features", 0)]
                steps += head_pair(2, out0, 2, 0, 0) + head_pair(3, out0, 2, 0, 1)
                steps += [("heads", 1), ("features", 1)] + head_pair(4, out0, 2, 0) + head_pair(5, out0, 2, 0, 0)
                steps += [("features", 2)] + head_pair(6, out1, 2, 0, 1) + head_pair(7, out1, 2, 0)
            else:
                steps += both + take(ins[2], 8) + [("heads", 0)]
                fill = ins[3] + ins[4]
                for h in range(3):
                    steps += head_pair(h, fill, 3, 1, h % 2)
                steps += norm(0) + head_pair(3, fill, 3, 1, 1) + [("rope", 1)]
                steps += take(ins[5], 4) + [("heads", 1)] + head_pair(4, ins[5], 3, 1, 0) + norm(1) + [("split", 1)]
                steps += [("features", 0), ("features", 1)] + head_pair(5, out0, 3, 0, 0) + head_pair(6, out0, 3, 0, 1)
                steps += norm(2) + [("features", 2)] + head_pair(7, out0, 2, 0, 0) + take(out1, 4)
            steps += norm(3) + [("features", 3)] + ([] if mixer == "swa" else [("split", 1)]) + take(out1, len(out1))
            return steps

        MLA_STEPS = [("heads", 0), ("heads", 1), ("scores", 0), ("scores", 1), ("turn", 0), ("mix", 0), ("scores", 2), ("turn", 1),
                     ("mix", 1), ("outputs", 0), ("scores", 3), ("turn", 2), ("mix", 2), ("turn", 3), ("mix", 3), ("outputs", 1)]

        HALF_PAIRS = {4: (1, 0), 5: (1, 1), 6: (2, 0), 7: (2, 1)}
        SHARED_WITH = {0: (), 1: (4, 5), 2: (6, 7), 3: (), 4: (1,), 5: (1,), 6: (2,), 7: (2,)}

        def outputs_at(q):
            return 4 + q % 2

        def features_at(mixer, q):
            return 6 + q if mixer != "swa" and q < 2 else 4 + q % 2

        def score_pair(mixer, hp):
            return (0, 2)[hp % 2] if mixer == "mla" else 0

        def head_pairs_of_banks(mixer, g):
            return ((2, 3) if mixer == "mla" else (0, 2)) if g else (0, 1)

        def turned_keys(mixer, g):
            if mixer == "swa":
                return [] if g else [0, 1]
            return list(range(4 * g, 4 * g + 4))

        PBLOCKS = [(0, 0, 0), (P, 1, 0), (2 * P, 1, 1)]
        SCALE = {"diff": HEAD ** -0.5, "moba": HEAD ** -0.5, "swa": HEAD ** -0.5, "mla": QK2 ** -0.5}

        def heads(mixer, hp, c):
            if mixer == "mla":
                return qT[0:QK2, 2 * hp + c, :], kT[0:QK2, 2 * hp + c, :]
            rows = slice(c * HEAD, (c + 1) * HEAD)
            return qT[rows, hp, :], kT[rows, hp // 4 if mixer == "swa" else hp, :]

        def values(mixer, hp, c, kt):
            if mixer == "diff":
                return qkv[:, kt, 2048 + hp * P:2048 + (hp + 1) * P]
            if mixer == "moba":
                return qkv[:, kt, 2048 + (2 * hp + c) * HEAD:2048 + (2 * hp + c + 1) * HEAD]
            if mixer == "swa":
                return qkv[:, kt, 1152 + (hp // 4) * HEAD:1152 + (hp // 4 + 1) * HEAD]
            v = (2 * hp + c) * (NOPE + V2) + NOPE
            return kvbuf[:, kt, v:v + V2]

        def q_tile(mixer, n, tt):
            return qbuf[:, tt, n * QK2:(n + 1) * QK2] if mixer == "mla" else qkv[:, tt, n * P:(n + 1) * P]

        def k_tile(mixer, n, tt):
            if mixer == "mla":
                return kfull[:, tt, n * QK2:(n + 1) * QK2]
            at = (1280 if mixer == "swa" else 1024) + n * P
            return qkv[:, tt, at:at + P]

        def o_at(mixer, q):
            return (qbuf if mixer == "mla" else qkv)[:, :, q * 256:(q + 1) * 256]

        def y_tile(kt):
            if kt < 2:
                return lambda tt: qkv[:, tt, ZC0 + kt * P:ZC0 + (kt + 1) * P]
            if kt < 6:
                return lambda tt: qbuf[:, tt, (kt - 2) * P:(kt - 1) * P]
            return lambda tt: qkv[:, tt, U0 + (kt - 6) * P:U0 + (kt - 5) * P]

        def branch(n):
            return [qkv[:, :, ZC0:ZC0 + CW], qbuf[:, :, 0:MLAW], qkv[:, :, U0:U0 + SGW]][n]

        def h_tile(kt):
            return lambda tt: h[:, tt, kt * P:(kt + 1) * P]

        def o_tile(kt):
            return lambda tt: qkv[:, tt, kt * P:(kt + 1) * P]

        def latent_tile(kt):
            return lambda tt: qkv[:, tt, CQ0 + kt * P:CQ0 + (kt + 1) * P]

        def conv_tile(kt):
            return lambda tt: qkv[:, tt, kt * P:(kt + 1) * P]

        def pair_tile(p, j):
            if p in HALF_PAIRS:
                p, half = HALF_PAIRS[p]
                return pair[p][:, half, j * SEQ:(j + 1) * SEQ]
            return pair[p][:, j // 2, (j % 2) * SEQ:(j % 2 + 1) * SEQ]

        block = ctx.enter_context(nc.Block())
        emptied_by_layer = []

        @block.scalar
        def _(act):
            t = tallies()

            plan = block_plan()

            def split(some=(0, 1)):
                if not plan:
                    return
                s = t.block % 2
                if 0 in some:
                    act.wait_ge(*t.loaded[s].after(16))
                for half in some:
                    cols = halves(plan[0])[half]
                    act.activation(whi[:, s, cols], raw[:, s, cols], ACT.Copy).then_inc(*t["hi_split"].one())
                if 1 in some:
                    plan.pop(0)
                    t.block += 1

            def used(halves_done=2):
                act.wait_ge(*t["block_used"].after(halves_done))

            def turn_split(kts, p, scale_of):
                act.wait_ge(*t.filled[p].after())
                for j, kt in enumerate(kts):
                    g = scale_of(kt) if scale_of else 1.0
                    act.activation(xhi[:, kt, :], pair_tile(p, j), ACT.Copy, scale=g).then_inc(*t["xhi_written"].one())
                t.emptied[p].n += 1

            def sum_squares(parts):
                for n, src in enumerate(parts):
                    w = src.shape[-1]
                    junk = kT[:, :, :].rearrange("p a b -> p (a b)")[:, (n % 2) * 1024:(n % 2) * 1024 + w]
                    if n >= 2:
                        act.wait_ge(*t["squares_summed"].now())
                    act.activation(junk, src, ACT.Square, accum_out=ss[:, n:n + 1]).then_inc(*t["squares_summed"].one())

            def roots(n, at=0):
                act.wait_ge(*t["var_ready"].after())
                act.activation(std[:, at:at + n], var[:, at:at + n], ACT.Sqrt).then_inc(*t["std_ready"].one())

            def norm(g, root=True, fresh=False):
                turn_split(range(0, 4), 0, g)
                turn_split(range(4, 8), 1, g)
                if not fresh:
                    used()
                    t.emptied[2].n += 1
                    t.emptied[3].n += 1
                    split()
                sum_squares([h[:, tt, :] for tt in range(TT)])
                if root:
                    roots(TT)

            def results(p, dst, w, scale):
                if p == 2:
                    for tt in range(TT):
                        used(1)
                        m = act.activation(dst(tt), pair[p][:, tt, 0:w], ACT.Copy, scale=scale(tt))
                    m.then_inc(*t.emptied[p].one())
                else:
                    used()
                    t.emptied[p].n += 1

            def queries_out(mixer, g):
                rows = QK2 if mixer == "mla" else P
                p, pk = head_pairs_of_banks(mixer, g)
                act.wait_ge(*t.filled[p].after())
                act.activation(qT[0:rows, 4 * g:4 * g + 4, :], pair[p][0:rows, :, :].rearrange("p b (j n) -> p (b j) n", j=2),
                               ACT.Copy).then_inc(*t.emptied[p].one())
                if turned_keys(mixer, g):
                    t.filled[pk].n += 1
                    t.emptied[pk].n += 1

            def exps(mixer, hp):
                b, p = hp % 2, score_pair(mixer, hp)
                act.wait_ge(*t["shift_ready"].after())
                t.filled[p].n += 1
                for c in range(2):
                    for tt, cols in ((0, slice(0, P)), (1, slice(P, 3 * P))):
                        m = act.activation(sm[:, b, c, cols], pair[p][:, c, cols], ACT.Exp, scale=SCALE[mixer],
                                           bias=negm[:, b, c, tt:tt + 1], accum_out=sums[:, hp, c, tt:tt + 1])
                m.then_inc(*t.emptied[p].one())

            def probs_out(mixer, hp):
                p = score_pair(mixer, hp)
                if mixer == "diff":
                    act.wait_ge(*t.filled[p].after())
                    act.activation(pT[:, hp % 2, 0, :], pair[p][:, 0, 0:384], ACT.Copy).then_inc(*t.emptied[p].one())
                else:
                    t.filled[p].n += 1
                    t.emptied[p].n += 1

            def outputs(mixer, q):
                p = outputs_at(q)
                if mixer == "diff":
                    act.wait_ge(*t.filled[p].after())
                    src = pair[1][:, q % 2, :].rearrange("p (j t e) -> p j t e", j=2, t=TT)
                    act.activation(o_at(mixer, q).rearrange("p t (j e) -> p j t e", j=2), src, ACT.Copy)\
                        .then_inc(*t.emptied[p].one())
                    return
                t.filled[p].n += 1
                t.emptied[p].n += 1
                if mixer == "swa":
                    sink = snk[:, 2 * q:2 * q + 2, :, :]
                    act.activation(sink, sink, ACT.Exp).then_inc(*t["sink_ready"].one())

            def mix_tokens(mixer, steps, g_o=None):
                for what, n, *_ in steps:
                    if what == "in_results":
                        c0, w = in_blocks(mixer)[n]
                        if mixer == "swa":
                            used()
                            t.emptied[2 + n % 2].n += 1
                        else:
                            if n == 0:
                                act.wait_ge(*t["rstd_ready"].after())
                            results(2 + n % 2, lambda tt: qkv[:, tt, c0:c0 + w], w, lambda tt: rstd[:, tt:tt + 1])
                    elif what == "heads":
                        queries_out(mixer, n)
                    elif what == "scores":
                        exps(mixer, n)
                    elif what == "turn":
                        probs_out(mixer, n)
                    elif what == "outputs":
                        outputs(mixer, n)
                    elif what == "o_norm":
                        roots16(4, 4 * n)
                    elif what == "features":
                        turn_split(range(2 * n, 2 * n + 2), features_at(mixer, n), g_o)
                    elif what == "out_results" and n == 0:
                        used()
                    elif what == "split":
                        split((n,))

            def roots16(n, at=0):
                act.wait_ge(*t["sum16_ready"].after())
                act.activation(std16[:, at:at + n], ss16[:, at:at + n], ACT.Sqrt).then_inc(*t["std16_ready"].one())

            def mlp():
                def up(j):
                    b = j % 2
                    used()
                    act.activation(relu_at[b], pair[b][:, :, :].rearrange("p b n -> p (b n)"), ACT.Relu)\
                        .then_inc(*t.emptied[b].one())
                    act.wait_ge(*t.emptied[b].now())
                    act.activation(ahi[:, b, :, :].rearrange("p f n -> p (f n)"), relu_at[b], ACT.Square)\
                        .then_inc(*t["ahi_written"].one())
                    split()

                def down():
                    used()
                    split()

                up(0)
                up(1)
                down()
                with act.Fori(0, 3) as i:
                    turns(t, i, MLP_TURN)
                    up(0)
                    down()
                    up(1)
                    down()
                after_turns(t, MLP_TURN, 3, 4)
                del plan[:8]

            def second(layer):
                norm(gain("norm_g_2", layer), fresh=layer == 0)
                act.wait_ge(*t["rstd_ready"].after())
                for n, (c0, w) in enumerate(W_IN_2_BLOCKS):
                    results(2 + n % 2, lambda tt: qkv[:, tt, c0:c0 + w], w, lambda tt: rstd[:, tt:tt + 1])
                    split()
                    if n == 0:
                        act.wait_ge(*t.emptied[2].now())
                        act.activation(qkv[:, :, GLU0:GLU0 + CW], qkv[:, :, GLU0:GLU0 + CW], ACT.Sigmoid)\
                            .then_inc(*t["sig_ready"].one())
                    elif n == 1:
                        act.wait_ge(*t.filled[0].after())
                        act.activation(ypad[:, :, CONV_K - 1:], pair[0][:, 0, :].rearrange("p (c n) -> p c n", c=2), ACT.Copy)\
                            .then_inc(*t.emptied[0].one())
                        act.wait_ge(*t.emptied[3].now())
                        for c in (V0, U0):
                            act.activation(qkv[:, :, c:c + SGW], qkv[:, :, c:c + SGW], ACT.Gelu_apprx_tanh)\
                                .then_inc(*t["gelu_ready"].one())
                    elif n == 3:
                        roots(TT, 6)
                act.wait_ge(*t.emptied[2].now())
                act.wait_ge(*t.emptied[3].now())
                for c, w in ((ZC0, CW), (ZM0, MLAW), (ZS0, SGW)):
                    act.activation(qkv[:, :, c:c + w], qkv[:, :, c:c + w], ACT.Silu).then_inc(*t["zsilu_ready"].one())
                turn_split(range(0, 4), 0, gain_latent(layer))
                turn_split(range(4, 8), 1, gain_latent(layer))
                sum_squares([qkv[:, tt, c:c + w] for c, w in ((CQ0, QL), (CKV0, KVL)) for tt in range(TT)])
                roots(4)
                act.wait_ge(*t["rstd_ready"].after())
                results(2, lambda tt: qbuf[:, tt, 0:384], 384, lambda tt: rstd[:, tt:tt + 1])
                split()
                t.filled[1].n += 1
                t.emptied[1].n += 1
                roots(TT, 6)
                act.wait_ge(*t["ln_ready"].after())
                act.activation(qkv[:, :, 0:CW], qkv[:, :, 0:CW], ACT.Silu).then_inc(*t["silu_ready"].one())
                t.filled[0].n += 1
                t.emptied[0].n += 1
                results(3, None, 384, None)
                split()
                results(2, lambda tt: kvbuf[:, tt, 0:BANK], BANK, lambda tt: rstd[:, 2 + tt:3 + tt])
                split()
                results(3, None, BANK, None)
                split()
                turn_split(range(2), 0, None)
                used()
                t.emptied[2].n += 1
                split()
                roots16(32)
                mix_tokens("mla", MLA_STEPS)
                act.wait_ge(*t["branches_ready"].after())
                sum_squares([branch(n)[:, tt, :] for n in range(3) for tt in range(TT)])
                roots(6)
                t["rstd_ready"].n += 1
                turn_split(range(0, 4), 0, gain("branch_norm_g_2", layer))
                turn_split(range(4, 8), 1, gain("branch_norm_g_2", layer))
                used()
                split()

            rows_a = sm[:, 0, 0, 0:P]
            rows_b = sm[0:N_ROWS_B, 0, 1, 0:P]
            for tile_at, rows in ((rows_a, ROWS_A), (rows_b, ROWS_B)):
                for name, n in rows:
                    v = a[name]
                    flat = v.rearrange("a b c -> (a b c)") if len(v.shape) == 3 else v.rearrange("a b -> (a b)")
                    act.dma_start(tile_at[ROW_AT[name]:ROW_AT[name] + n, :], flat.rearrange("(r p) -> r p", p=P))\
                        .then_inc(*t["rows_loaded"].one(16))
            split()
            split()
            act.wait_ge(*t.filled[2].after())
            act.activation(colsA[:, :], pair[2][:, 0, 0:N_ROWS_A], ACT.Copy)
            act.activation(colsB[:, :], pair[2][:, 1, 0:N_ROWS_B], ACT.Copy).then_inc(*t.emptied[2].one())
            act.wait_ge(*t.filled[3].after())
            act.activation(wsg[:, :, :, :].rearrange("p l g t -> p l (g t)"), pair[3][:, :, :], ACT.Copy)\
                .then_inc(*t.emptied[3].one())
            act.wait_ge(*t.emptied[2].now())
            act.wait_ge(*t["angles_ready"].after())
            act.activation(sin1[:, :, :], sin1[:, :, :], ACT.Sin).then_inc(*t["sines_ready"].one())
            act.activation(cos1[:, :, :], cos1[:, :, :], ACT.Sin).then_inc(*t["sines_ready"].one())
            act.activation(lams[:, :], lams[:, :], ACT.Exp).then_inc(*t["sines_ready"].one())

            for layer, mixer in enumerate(MIXERS):
                norm(gain("attn_norm_g", layer), fresh=layer == 0)
                if mixer == "swa":
                    t["rstd_ready"].n += 1
                mix_tokens(mixer, mixer_steps(mixer), gain_sub(layer // 3) if mixer == "diff" else None)
                norm(gain("mlp_norm_g", layer), root=False)
                mlp()
            used()
            t.emptied[2].n += 1
            t.emptied[3].n += 1
            split()
            act.wait_ge(*t.emptied[2].now())
            act.wait_ge(*t.emptied[3].now())
            sum_squares([h[:, tt, :] for tt in range(TT)])
            roots(TT)
            t["rstd_ready"].n += 1
            for layer in range(DEPTH_2):
                second(layer)

        @block.tensor
        def _(pe):
            t = tallies()

            def free(p):
                for q in (p,) + SHARED_WITH[p]:
                    if t.emptied[q].n:
                        pe.wait_ge(*t.emptied[q].now())
                t.emptied[p].n += 1

            def products(dst, x, w, first, last):
                (x_hi, x_lo), (w_hi, w_lo) = x, w
                pe.matmul(dst, x_hi, w_hi, start=first, stop=False)
                pe.matmul(dst, x_hi, w_lo, start=False, stop=False)
                return pe.matmul(dst, x_lo, w_hi, start=False, stop=last)

            def token_major(p, T, w, k0=0, eighth=None, opening=False):
                units = [(tt, k) for tt in range(TT) for k in range(T)]
                if opening:
                    units.sort(key=lambda u: u[1] // (KT // 2))
                n = len(units)
                some = range(n) if eighth is None else range(eighth * n // EIGHTHS, (eighth + 1) * n // EIGHTHS)
                s = t.block % 2
                w_hi, w_lo = slot(whi, s, T, w), slot(wlo, s, T, w)
                for u in some:
                    if u == 0:
                        pe.wait_ge(*t["lo_split"].after(2))
                        free(p)
                    if opening:
                        open_layer(u)
                    tt, k = units[u]
                    tok = slice(tt * P, (tt + 1) * P)
                    m = products(pair[p][:, tt, 0:w], (xhi[:, k0 + k, tok], xlo[:, k0 + k, tok]),
                                 (w_hi[:, k, :], w_lo[:, k, :]), k == 0, k == T - 1)
                    if k == T - 1:
                        m.then_inc(*t["block_used"].one())
                if some[-1] == n - 1:
                    t.block += 1

            def open_layer(u):
                if u == 0:
                    turned(0)
                elif u == 4:
                    turn_stream(1)
                elif u == 8:
                    turned(1)

            def turn_stream(half, fresh=False):
                if not fresh:
                    pe.wait_ge(*t.emptied[2 + half].now())
                turn(range(4 * half, 4 * half + 4), half, h_tile)

            BY_COLUMNS = [(n, tt, f) for n in range(2) for tt in range(TT) for f in range(4)]
            BY_FEATURES = sorted(BY_COLUMNS, key=lambda u: u[2] // 2)

            def accumulate(x_hi, x_lo, first, last, order, eighth=None, closing=False, operand=None):
                n_units = len(order)
                some = range(n_units) if eighth is None else range(eighth * n_units // EIGHTHS, (eighth + 1) * n_units // EIGHTHS)
                s = t.block % 2
                w_hi, w_lo = slot(whi, s, 4, D), slot(wlo, s, 4, D)
                for u in some:
                    n, tt, f = order[u]
                    if u == 0:
                        pe.wait_ge(*t["lo_split"].after(2))
                        if first:
                            free(2)
                            free(3)
                    if operand:
                        operand(u)
                    if closing and u == n_units - (4 if order is BY_COLUMNS else 2):
                        turn_stream(0)
                    cols, tok = slice(n * BANK, (n + 1) * BANK), slice(tt * P, (tt + 1) * P)
                    m = products(pair[2 + n][:, tt, :], (x_hi[:, f, tok], x_lo[:, f, tok]),
                                 (w_hi[:, f, cols], w_lo[:, f, cols]), first and f == 0, last and f == 3)
                    if (tt, f) == (TT - 1, 3):
                        m.then_inc(*t["block_used"].one())
                if some[-1] == n_units - 1:
                    t.block += 1

            def out_part(g, operand, eighth=None, closing=True):
                rows = slice(4 * g, 4 * g + 4)
                accumulate(xhi[:, rows, :], xlo[:, rows, :], g == 0, g == 1, BY_FEATURES, eighth, closing and g == 1, operand)

            def turn(kts, p, tile):
                free(p)
                for j, kt in enumerate(kts):
                    for tt in range(TT):
                        m = pe.transpose(pair_tile(p, j)[:, tt * P:(tt + 1) * P], tile(kt)(tt), ident[:, :])
                m.then_inc(*t.filled[p].one())

            def turned(*pairs):
                for p in pairs:
                    pe.wait_ge(*t.emptied[p].now())

            def turn_heads(mixer, g):
                if mixer != "mla":
                    pe.wait_ge(*t["roped"].after())
                if mixer in ("diff", "moba") and g == 0:
                    pe.wait_ge(*t.emptied[2].now())
                rows = QK2 if mixer == "mla" else P
                for p, tiles, tile in zip(head_pairs_of_banks(mixer, g), (range(4 * g, 4 * g + 4), turned_keys(mixer, g)),
                                          (q_tile, k_tile)):
                    if not tiles:
                        continue
                    free(p)
                    for j, n in enumerate(tiles):
                        for tt in range(TT):
                            m = pe.transpose(pair_tile(p, j)[0:rows, tt * P:(tt + 1) * P], tile(mixer, n, tt), ident[:, :])
                    m.then_inc(*t.filled[p].one())

            def scores(mixer, hp):
                p = score_pair(mixer, hp)
                free(p)
                if hp in (0, 4):
                    for q in (1, 2, 3) if mixer == "mla" else head_pairs_of_banks(mixer, hp // 4)[1:]:
                        if q != p and turned_keys(mixer, hp // 4):
                            pe.wait_ge(*t.emptied[q].now())
                mask = band if mixer == "swa" else causal
                masked = P if mixer == "swa" else 2 * P
                for c in range(2):
                    q, k = heads(mixer, hp, c)
                    pe.matmul(pair[p][:, c, 0:P], q[:, 0:P], k[:, 0:P], start=True, stop=False)
                    pe.matmul(pair[p][:, c, 0:P], ident_b[:, :], mask[:, 0:P], start=False, stop=True)
                    pe.matmul(pair[p][:, c, P:3 * P], q[:, P:2 * P], k[:, :], start=True, stop=False)
                    m = pe.matmul(pair[p][:, c, masked:3 * P], ident_b[:, :], mask[:, masked:3 * P], start=False, stop=True)
                m.then_inc(*t.filled[p].one())

            def turn_probs(mixer, hp):
                p = score_pair(mixer, hp)
                if mixer == "diff":
                    pe.wait_ge(*t["p_ready"].after())
                free(p)
                for c in range(1 if mixer == "diff" else 2):
                    for at, _, _ in PBLOCKS:
                        m = pe.transpose(pair[p][:, c, at:at + P], sm[:, hp % 2, c, at:at + P], ident[:, :])
                m.then_inc(*t.filled[p].one())

            def mix_values(mixer, hp):
                pe.wait_ge(*t.emptied[score_pair(mixer, hp)].now())
                j, b = hp % 4, hp % 2
                if b == 0:
                    free(outputs_at(hp // 2))
                if hp == 4 and mixer in ("diff", "moba"):
                    pe.wait_ge(*t.emptied[3].now())
                w = P if mixer == "diff" else V2
                for c in range(1 if mixer == "diff" else 2):
                    for qt in range(TT):
                        at = (j % 2) * SEQ + qt * P + c * V2
                        for col, _, kt in [x for x in PBLOCKS if x[1] == qt]:
                            m = pe.matmul(pair[1][:, j // 2, at:at + w], pT[:, b, c, col:col + P], values(mixer, hp, c, kt),
                                          start=kt == 0, stop=kt == qt)
                if b == 1:
                    m.then_inc(*t.filled[outputs_at(hp // 2)].one())

            def mix_tokens(mixer, steps):
                for what, n, *eighth in steps:
                    if what == "in":
                        token_major(2 + n % 2, KT, in_blocks(mixer)[n][1], 0, eighth[0], opening=n == 0)
                    elif what == "heads":
                        turn_heads(mixer, n)
                    elif what == "scores":
                        scores(mixer, n)
                    elif what == "turn":
                        turn_probs(mixer, n)
                    elif what == "mix":
                        mix_values(mixer, n)
                    elif what == "features":
                        if mixer == "diff":
                            pe.wait_ge(*t["o_normed"].after())
                        else:
                            pe.wait_ge(*t.emptied[outputs_at(n)].now(1 if mixer == "moba" and n == 0 else 0))
                        turn(range(2 * n, 2 * n + 2), features_at(mixer, n), o_tile)
                    elif what == "out":
                        out_part(n, lambda u: turned(features_at(mixer, 2 * n + u // 8)) if u % 8 == 0 else None, eighth[0])

            def mlp(closing):
                def up(j, opening=False):
                    pe.wait_ge(*t["lo_split"].after(2))
                    free(j % 2)
                    s = t.block % 2
                    w_hi, w_lo = slot(whi, s, KT, BANK), slot(wlo, s, KT, BANK)
                    units = [(f, k) for f in (0, 2, 1, 3) for k in range(KT)]
                    if opening:
                        units.sort(key=lambda u: (u[0] % 2, u[1] // (KT // 2) if u[0] % 2 == 0 else 0))
                    for u, (f, k) in enumerate(units):
                        if opening and u:
                            open_layer(u)
                        cols = slice(f * P, (f + 1) * P)
                        m = products(pair_tile(j % 2, f), (w_hi[:, k, cols], w_lo[:, k, cols]),
                                     (xhi[:, k, :], xlo[:, k, :]), k == 0, k == KT - 1)
                        if f % 2 and k == KT - 1:
                            m.then_inc(*t["block_used"].one())
                    t.block += 1

                def down(j, first=False, last=False, closing=False):
                    pe.wait_ge(*t["alo_written"].after())
                    accumulate(ahi[:, j % 2, :, :], alo[:, j % 2, :, :], first, last, BY_COLUMNS, closing=closing)

                up(0, opening=True)
                up(1)
                down(0, first=True)
                with pe.Fori(0, 3) as i:
                    turns(t, i, MLP_TURN)
                    up(0)
                    down(1)
                    up(1)
                    down(0)
                after_turns(t, MLP_TURN, 3, 4)
                down(1, last=True, closing=closing)

            def second(layer):
                for n, (_, w) in enumerate(W_IN_2_BLOCKS):
                    token_major(2 + n % 2, KT, w, opening=n == 0)
                    if n == 1:
                        pe.wait_ge(*t["glu_ready"].after())
                        free(0)
                        for ct in range(2):
                            for tt in range(TT):
                                m = pe.transpose(pair[0][:, 0, ct * SEQ + tt * P:ct * SEQ + (tt + 1) * P], conv_tile(ct)(tt),
                                                 ident[:, :])
                        m.then_inc(*t.filled[0].one())
                pe.wait_ge(*t.emptied[2].now())
                pe.wait_ge(*t.emptied[3].now())
                turn(range(0, 4), 0, latent_tile)
                turn(range(4, 8), 1, latent_tile)
                turned(0, 1)
                token_major(2, 6, 384)
                pe.wait_ge(*t["conv_ready"].after())
                free(1)
                for ct in range(2):
                    for tt in range(TT):
                        m = pe.transpose(pair[1][:, 0, tt * CW + ct * P:tt * CW + (ct + 1) * P],
                                         yacc[:, ct, tt * P:(tt + 1) * P], ident[:, :])
                m.then_inc(*t.filled[1].one())
                pe.wait_ge(*t["vln_ready"].after())
                free(0)
                for tt in range(TT):
                    for g in range(4):
                        m = pe.matmul(pair[0][:, tt, g * 64:(g + 1) * 64], wsg[:, layer, g, :],
                                      qkv[:, tt, V0 + g * 64:V0 + (g + 1) * 64], start=True, stop=True)
                m.then_inc(*t.filled[0].one())
                token_major(3, 6, 384)
                for n in range(2):
                    token_major(2 + n, 2, BANK, 6)
                pe.wait_ge(*t["silu_ready"].after())
                turn(range(2), 0, conv_tile)
                turned(0)
                token_major(2, 2, CW)
                pe.wait_ge(*t["qk_ready"].after())
                mix_tokens("mla", MLA_STEPS)
                pe.wait_ge(*t["y_ready"].after())
                turn(range(0, 4), 0, y_tile)
                turn(range(4, 8), 1, y_tile)
                turned(0, 1)
                for g in range(2):
                    out_part(g, None, closing=layer < DEPTH_2 - 1)

            pe.wait_ge(sems["consts_made"], 7)
            pe.wait_ge(sems["rows_loaded"], 16 * (len(ROWS_A) + len(ROWS_B)))
            free(2)
            pe.transpose(pair[2][:, 0, 0:N_ROWS_A], sm[:, 0, 0, 0:P], ident[:, :])
            pe.transpose(pair[2][:, 1, 0:N_ROWS_B], sm[0:N_ROWS_B, 0, 1, 0:P], ident[0:N_ROWS_B, 0:N_ROWS_B])\
                .then_inc(*t.filled[2].one())
            pe.wait_ge(sems["mixing_masked"], 1)
            free(3)
            for layer in range(DEPTH_2):
                for g in range(4):
                    m = pe.transpose(pair[3][:, layer, g * P:(g + 1) * P], wsg[:, layer, g, :], ident[:, :])
            m.then_inc(*t.filled[3].one())
            pe.wait_ge(sems["x_loaded"], 16)
            turn_stream(0, fresh=True)
            for layer, mixer in enumerate(MIXERS):
                mix_tokens(mixer, mixer_steps(mixer))
                mlp(closing=layer < DEPTH - 1)
            pe.wait_ge(sems["h_ready"], 1)
            turn_stream(0, fresh=True)
            for layer in range(DEPTH_2):
                second(layer)
                emptied_by_layer.append({p: t.emptied[p].n for p in (2, 3)})

        @block.vector
        def _(dve):
            t = tallies()
            plan = block_plan()

            def step():
                dve.wait_ge(*t["dve_step"].now())

            def chain(m):
                m.then_inc(*t["dve_step"].one())
                step()

            def split(some=(0, 1)):
                if not plan:
                    return
                s = t.block % 2
                for half in some:
                    cols = halves(plan[0])[half]
                    dve.wait_ge(*t["hi_split"].after())
                    dve.tensor_tensor(wlo[:, s, cols], raw[:, s, cols], whi[:, s, cols].bitcast(FP32), ALU.subtract)\
                        .then_inc(*t["lo_split"].one())
                if 1 in some:
                    plan.pop(0)
                    t.block += 1

            def used(halves_done=2):
                dve.wait_ge(*t["block_used"].after(halves_done))

            def turn_split(kts, p, scale_of):
                t.filled[p].n += 1
                for j, kt in enumerate(kts):
                    if j % 2 == 0:
                        dve.wait_ge(*t["xhi_written"].after(2))
                    g = scale_of(kt) if scale_of else 1.0
                    m = dve.scalar_tensor_tensor(out=xlo[:, kt, :], in0=pair_tile(p, j), scalar=g,
                                                 in1=xhi[:, kt, :].bitcast(FP32), op0=ALU.mult, op1=ALU.subtract)
                m.then_inc(*t.emptied[p].one())

            def variances(parts, widths, root=True):
                dve.wait_ge(*t["squares_summed"].after(parts))
                at = 0
                for n, w in widths:
                    m = dve.tensor_scalar(var[:, at:at + n], ss[:, at:at + n], 1.0 / w, EPS, ALU.mult, ALU.add)
                    at += n
                if root:
                    m.then_inc(*t["var_ready"].one())
                    dve.wait_ge(*t["std_ready"].after())
                    dve.reciprocal(rstd[:, 0:at], std[:, 0:at]).then_inc(*t["rstd_ready"].one())
                    dve.wait_ge(*t["rstd_ready"].now())
                else:
                    m.then_inc(*t["dve_step"].one())
                    step()
                    dve.reciprocal(rstd[:, 0:at], var[:, 0:at]).then_inc(*t["dve_step"].one())
                    step()

            def norm(g, add, root=True):
                for n in range(2):
                    if add:
                        used(1)
                        add(n)
                    turn_split(range(4 * n, 4 * n + 4), n, g)
                if add:
                    split()
                variances(TT, [(TT, D)], root)

            def results(p, dst, w, scale):
                if p == 3:
                    for tt in range(TT):
                        used(1)
                        m = dve.tensor_scalar(dst(tt), pair[p][:, tt, 0:w], scale(tt), None, ALU.mult)
                    m.then_inc(*t.emptied[p].one())
                else:
                    used()
                    t.emptied[p].n += 1

            def biased_results(n):
                c0, w = in_blocks("swa")[n]
                p = 2 + n % 2
                for tt in range(TT):
                    used(1)
                    m = dve.scalar_tensor_tensor(out=qkv[:, tt, c0:c0 + w], in0=pair[p][:, tt, 0:w], scalar=rstd[:, tt:tt + 1],
                                                 in1=swab[:, c0:c0 + w], op0=ALU.mult, op1=ALU.add)
                m.then_inc(*t.emptied[p].one())

            def rope(view, n, half, cos, sin, place):
                shape = [P, TT, n, half]
                x1, x2 = view(0, half), view(half, 2 * half)
                c = lanes(cos.unsqueeze(2), shape)
                s = lanes(sin.unsqueeze(2), shape)
                size = TT * n * half
                tmp = [place[:, k * size:(k + 1) * size].rearrange("p (t n f) -> p t n f", t=TT, n=n) for k in range(4)]
                for dst, x, y in ((tmp[0], x1, c), (tmp[1], x2, s), (tmp[2], x2, c), (tmp[3], x1, s)):
                    dve.tensor_tensor(dst, x, y, ALU.mult).then_inc(*t["dve_step"].one())
                step()
                dve.tensor_tensor(x1, tmp[0], tmp[1], ALU.subtract).then_inc(*t["dve_step"].one())
                return dve.tensor_tensor(x2, tmp[2], tmp[3], ALU.add)

            def rotate(mixer, g):
                dve.wait_ge(*t.emptied[2].now())
                dve.wait_ge(*t.emptied[3].now())
                parts = [(g * BANK, 8)]
                if mixer != "swa":
                    parts.append((D + g * BANK, 8))
                elif g == 0:
                    parts.append((D, 2))
                for c0, n in parts:
                    x = qkv[:, :, c0:c0 + n * HEAD].rearrange("p t (h d) -> p t h d", d=HEAD)
                    m = rope(lambda lo, hi: x[:, :, :, lo:hi], n, HALF, cos1[:, :, :], sin1[:, :, :], rope_tmp[:, :])
                    if (c0, n) != parts[-1]:
                        chain(m)
                if mixer == "swa" and g == 0:
                    chain(m)
                    k = qkv[:, :, 1024:1152].rearrange("p t (g d) -> p t g d", g=2)
                    both = qkv[:, :, 1280:1536].rearrange("p t (g r d) -> p t g r d", g=2, r=2)
                    for r in range(2):
                        m = dve.tensor_copy(both[:, :, :, r, :], k)
                m.then_inc(*t["roped"].one())
                dve.wait_ge(*t["roped"].now())

            def keys_out(mixer, g):
                rows = QK2 if mixer == "mla" else P
                p, pk = head_pairs_of_banks(mixer, g)
                t.filled[p].n += 1
                t.emptied[p].n += 1
                keys = turned_keys(mixer, g)
                if keys:
                    n = len(keys)
                    dve.wait_ge(*t.filled[pk].after())
                    dve.tensor_copy(kT[0:rows, keys[0]:keys[0] + n, :].rearrange("p j n -> p (j n)"),
                                    pair[pk][0:rows, :, :].rearrange("p b n -> p (b n)")[:, 0:n * SEQ])\
                        .then_inc(*t.emptied[pk].one())

            def shifts(mixer, hp):
                b, p = hp % 2, score_pair(mixer, hp)
                dve.wait_ge(*t.filled[p].after())
                t.emptied[p].n += 1
                for tt, cols in ((0, slice(0, P)), (1, slice(P, 3 * P))):
                    dve.tensor_reduce(mx[:, b, :, tt], pair[p][:, :, cols], AXIS.X, ALU.max).then_inc(*t["dve_step"].one())
                step()
                m = mx[:, b, :, :]
                if mixer == "swa":
                    dve.tensor_tensor(m, m, lanes(sinks8[:, 2 * hp:2 * hp + 2].unsqueeze(2), [P, 2, 2]), ALU.max)\
                        .then_inc(*t["dve_step"].one())
                    step()
                ins = dve.tensor_scalar(negm[:, b, :, :], m, -SCALE[mixer], None, ALU.mult)
                if mixer == "swa":
                    ins.then_inc(*t["dve_step"].one())
                    step()
                    ins = dve.tensor_tensor(snk[:, hp, :, :], negm[:, b, :, :],
                                            lanes(sinks[:, 2 * hp:2 * hp + 2].unsqueeze(2), [P, 2, 2]), ALU.add)
                ins.then_inc(*t["shift_ready"].one())

            def probs(hp):
                b = hp % 2
                dve.wait_ge(*t.emptied[0].now())
                chain(dve.reciprocal(rinv[:, hp, :, :], sums[:, hp, :, :]))
                chain(dve.tensor_scalar(rinv[:, hp, 1, :], rinv[:, hp, 1, :], neglam[:, t.lam:t.lam + 1], None, ALU.mult))
                for tt, cols in ((0, slice(0, P)), (1, slice(P, 3 * P))):
                    m = dve.tensor_scalar(pT[:, b, 1, cols], sm[:, b, 1, cols], rinv[:, hp, 1, tt:tt + 1], None, ALU.mult)
                chain(m)
                for tt, cols in ((0, slice(0, P)), (1, slice(P, 3 * P))):
                    m = dve.scalar_tensor_tensor(out=sm[:, b, 0, cols], in0=sm[:, b, 0, cols], scalar=rinv[:, hp, 0, tt:tt + 1],
                                                 in1=pT[:, b, 1, cols], op0=ALU.mult, op1=ALU.add)
                m.then_inc(*t["p_ready"].one())
                dve.wait_ge(*t["p_ready"].now())

            def probs_out(mixer, hp):
                p = score_pair(mixer, hp)
                if mixer == "diff":
                    probs(hp)
                    t.filled[p].n += 1
                    t.emptied[p].n += 1
                else:
                    dve.wait_ge(*t.filled[p].after())
                    dve.tensor_copy(pT[:, hp % 2, :, :], pair[p][:, :, 0:384]).then_inc(*t.emptied[p].one())

            def outputs(mixer, q):
                p = outputs_at(q)
                if mixer == "diff":
                    t.filled[p].n += 1
                    t.emptied[p].n += 1
                    return
                pairs = slice(2 * q, 2 * q + 2)
                if mixer == "swa":
                    dve.wait_ge(*t["sink_ready"].after())
                    chain(dve.tensor_tensor(sums[:, pairs, :, :], sums[:, pairs, :, :], snk[:, pairs, :, :], ALU.add))
                chain(dve.reciprocal(rinv[:, pairs, :, :], sums[:, pairs, :, :]))
                dve.wait_ge(*t.filled[p].after())
                for tt in range(TT):
                    src = pair[1][:, q % 2, :].rearrange("p (j t c d) -> p j t c d", j=2, t=TT, c=2)[:, :, tt]
                    m = dve.tensor_tensor(o_at(mixer, q)[:, tt, :].rearrange("p (j c d) -> p j c d", j=2, c=2), src,
                                          lanes(rinv[:, pairs, :, tt].unsqueeze(3), [P, 2, 2, V2]), ALU.mult)
                m.then_inc(*t.emptied[p].one())

            def mix_tokens(mixer, steps, g_o=None):
                for what, n, *_ in steps:
                    if what == "in_results":
                        c0, w = in_blocks(mixer)[n]
                        if mixer == "swa":
                            biased_results(n)
                        else:
                            results(2 + n % 2, lambda tt: qkv[:, tt, c0:c0 + w], w, lambda tt: rstd[:, tt:tt + 1])
                    elif what == "rope":
                        rotate(mixer, n)
                    elif what == "heads":
                        keys_out(mixer, n)
                    elif what == "scores":
                        shifts(mixer, n)
                    elif what == "turn":
                        probs_out(mixer, n)
                    elif what == "outputs":
                        outputs(mixer, n)
                    elif what == "o_norm":
                        head_norm(n)
                    elif what == "features":
                        turn_split(range(2 * n, 2 * n + 2), features_at(mixer, n), g_o)
                    elif what == "out_results" and n == 0:
                        used()
                    elif what == "split":
                        split((n,))

            def roots16(n, w, at=0):
                some = slice(at, at + n)
                dve.tensor_scalar(ss16[:, some], ss16[:, some], 1.0 / w, EPS, ALU.mult, ALU.add).then_inc(*t["sum16_ready"].one())
                dve.wait_ge(*t["std16_ready"].after())
                chain(dve.reciprocal(rstd16[:, some], std16[:, some]))

            def head_norm(q):
                dve.wait_ge(*t.emptied[outputs_at(q)].now())
                o = o_at("diff", q)
                squares = qkv[:, :, D + q * 256:D + (q + 1) * 256]
                chain(dve.tensor_tensor(squares, o, o, ALU.mult))
                chain(dve.tensor_reduce(ss16[:, 4 * q:4 * q + 4].rearrange("p (t h) -> p t h", t=TT),
                                        squares.rearrange("p t (h e) -> p t h e", e=P), AXIS.X, ALU.add))
                roots16(4, P, 4 * q)
                ov = o.rearrange("p t (h e) -> p t h e", e=P)
                r = rstd16[:, 4 * q:4 * q + 4].rearrange("p (t h) -> p t h", t=TT).unsqueeze(3)
                dve.tensor_tensor(ov, ov, lanes(r, [P, TT, 2, P]), ALU.mult).then_inc(*t["o_normed"].one())

            def add_out(n):
                cols = slice(n * BANK, (n + 1) * BANK)
                dve.tensor_tensor(h[:, :, cols], pair[2 + n][:, :, :], h[:, :, cols], ALU.add).then_inc(*t.emptied[2 + n].one())

            def add_mlp(n):
                cols = slice(n * BANK, (n + 1) * BANK)
                for tt in range(TT):
                    m = dve.scalar_tensor_tensor(out=h[:, tt, cols], in0=pair[2 + n][:, tt, :], scalar=rstd[:, tt:tt + 1],
                                                 in1=h[:, tt, cols], op0=ALU.mult, op1=ALU.add)
                m.then_inc(*t.emptied[2 + n].one())

            def mlp():
                def up(j):
                    b = j % 2
                    used()
                    dve.wait_ge(*t.emptied[b].after())
                    if t["alo_written"].n:
                        dve.wait_ge(*t["alo_written"].now())
                    dve.tensor_tensor(square_at, relu_at[b], relu_at[b], ALU.mult).then_inc(*t["dve_step"].one())
                    dve.wait_ge(*t["ahi_written"].after())
                    step()
                    dve.tensor_tensor(alo[:, b, :, :].rearrange("p f n -> p (f n)"), square_at,
                                      ahi[:, b, :, :].rearrange("p f n -> p (f n)").bitcast(FP32), ALU.subtract)\
                        .then_inc(*t["alo_written"].one())
                    split()

                def down():
                    used()
                    split()

                up(0)
                up(1)
                down()
                per = dict(MLP_TURN, dve_step=2)
                with dve.Fori(0, 3) as i:
                    turns(t, i, per)
                    up(0)
                    down()
                    up(1)
                    down()
                after_turns(t, per, 3, 4)
                del plan[:8]

            def layer_norm(src, dst, g, b, centred):
                for tt in range(TT):
                    m = dve.bn_stats(bn6[:, tt, :], src(tt))
                chain(m)
                for tt in range(TT):
                    m = dve.bn_aggr(bn2[:, tt, :], bn6[:, tt, :])
                chain(m)
                dve.tensor_scalar(var[:, 6:6 + TT], bn2[:, :, 1], EPS, None, ALU.add).then_inc(*t["var_ready"].one())
                dve.wait_ge(*t["std_ready"].after())
                chain(dve.reciprocal(rstd[:, 6:6 + TT], std[:, 6:6 + TT]))
                for tt in range(TT):
                    m = dve.tensor_scalar(dst[:, tt, :], src(tt), bn2[:, tt, 0:1], rstd[:, 6 + tt:7 + tt], ALU.subtract, ALU.mult)
                m.then_inc(*centred.one())
                dve.wait_ge(*centred.now())
                chain(dve.tensor_tensor(dst, dst, lanes(g.unsqueeze(1), [P, TT, 256]), ALU.mult))
                return dve.tensor_tensor(dst, dst, lanes(b.unsqueeze(1), [P, TT, 256]), ALU.add)

            def convolve(layer, taps):
                at = layer * CONV_K * 2
                step()
                for k in taps:
                    for ct in range(2):
                        w = colsA[:, at + 2 * k + ct:at + 2 * k + ct + 1]
                        y = ypad[:, ct, k:k + SEQ]
                        if k == 0:
                            bias = colsA[:, ROW_AT["conv_b_2"] + 2 * layer + ct:ROW_AT["conv_b_2"] + 2 * layer + ct + 1]
                            m = dve.tensor_scalar(yacc[:, ct, :], y, w, bias, ALU.mult, ALU.add)
                        else:
                            dve.wait_ge(*t["dve_step"].now(1))
                            m = dve.scalar_tensor_tensor(out=yacc[:, ct, :], in0=y, scalar=w, in1=yacc[:, ct, :],
                                                         op0=ALU.mult, op1=ALU.add)
                        if (k, ct) != (CONV_K - 1, 1):
                            m.then_inc(*t["dve_step"].one())
                if taps[-1] == CONV_K - 1:
                    m.then_inc(*t["conv_ready"].one())

            def second(layer):
                norm(gain("norm_g_2", layer), add_out if layer else None)
                dve.wait_ge(*t["spread_loaded"].after(16 * len(SPREAD_2)))
                if layer == 0:
                    chain(dve.memset(ypad[:, :, 0:CONV_K - 1], 0.0))
                taps = {2: range(0, 8), 3: range(8, 15), 4: range(15, 24), 5: range(24, CONV_K)}
                for n, (c0, w) in enumerate(W_IN_2_BLOCKS):
                    results(2 + n % 2, lambda tt: qkv[:, tt, c0:c0 + w], w, lambda tt: rstd[:, tt:tt + 1])
                    split()
                    if n == 0:
                        dve.wait_ge(*t["sig_ready"].after())
                        dve.tensor_tensor(qkv[:, :, A0:A0 + CW], qkv[:, :, A0:A0 + CW], qkv[:, :, GLU0:GLU0 + CW], ALU.mult)\
                            .then_inc(*t["glu_ready"].one())
                    elif n == 1:
                        t.filled[0].n += 1
                        dve.wait_ge(*t.emptied[0].after())
                    if n in taps:
                        convolve(layer, taps[n])
                    if n == 3:
                        v = qkv[:, :, V0:V0 + SGW]
                        dve.wait_ge(*t["gelu_ready"].after())
                        layer_norm(lambda tt: v[:, tt, :], v, param2("sg_ln_g_2"), param2("sg_ln_b_2"), t["dve_step"])\
                            .then_inc(*t["vln_ready"].one())
                turn_split(range(0, 4), 0, gain_latent(layer))
                turn_split(range(4, 8), 1, gain_latent(layer))
                variances(4, [(2, QL), (2, KVL)])
                results(2, None, 384, None)
                split()
                dve.wait_ge(*t.filled[1].after())
                layer_norm(lambda tt: pair[1][:, 0, tt * CW:(tt + 1) * CW], qkv[:, :, 0:CW], param2("conv_ln_g_2"),
                           param2("conv_ln_b_2"), t.emptied[1]).then_inc(*t["ln_ready"].one())
                dve.wait_ge(*t["gelu_ready"].after())
                dve.wait_ge(*t.filled[0].after())
                for g in range(4):
                    u = qkv[:, :, U0 + g * 64:U0 + (g + 1) * 64]
                    at = ROW_AT["sg_b_2"] + layer * 4 + g
                    m = dve.scalar_tensor_tensor(out=u, in0=pair[0][:, :, g * 64:(g + 1) * 64], scalar=colsB[:, at:at + 1], in1=u,
                                                 op0=ALU.add, op1=ALU.mult)
                m.then_inc(*t.emptied[0].one())
                results(3, lambda tt: qbuf[:, tt, 384:768], 384, lambda tt: rstd[:, tt:tt + 1])
                split()
                dve.wait_ge(*t.emptied[0].now())
                dve.wait_ge(*t["zsilu_ready"].after(3))
                chain(dve.tensor_tensor(qkv[:, :, U0:U0 + SGW], qkv[:, :, U0:U0 + SGW], qkv[:, :, ZS0:ZS0 + SGW], ALU.mult))
                q = qbuf[:, :, :].rearrange("p t (h d) -> p t h d", d=QK2)
                k = kfull[:, :, :].rearrange("p t (h d) -> p t h d", d=QK2)
                kv = kvbuf[:, :, :].rearrange("p t (h d) -> p t h d", d=NOPE + V2)
                squares = kT[:, :, :].rearrange("p a b -> p (a b)")[:, 0:TT * H2 * QK2].rearrange("p (t h d) -> p t h d", t=TT, d=QK2)

                def head_squares(n, x):
                    chain(dve.tensor_tensor(squares, x, x, ALU.mult))
                    chain(dve.tensor_reduce(ss16[:, 16 * n:16 * n + 16].rearrange("p (t h) -> p t h", t=TT), squares,
                                            AXIS.X, ALU.add))

                results(2, None, BANK, None)
                split()
                results(3, lambda tt: kvbuf[:, tt, BANK:2 * BANK], BANK, lambda tt: rstd[:, 2 + tt:3 + tt])
                split()
                dve.wait_ge(*t.emptied[2].now())
                dve.wait_ge(*t.emptied[3].now())
                turn_split(range(2), 0, None)
                dve.tensor_copy(k[:, :, :, 0:NOPE], kv[:, :, :, 0:NOPE]).then_inc(*t["dve_step"].one())
                kr = qkv[:, :, KR0:KR0 + ROPE2].unsqueeze(2)
                chain(dve.tensor_copy(k[:, :, :, NOPE:QK2], lanes(kr, [P, TT, H2, ROPE2])))
                head_squares(0, q)
                head_squares(1, k)
                used()
                for tt in range(TT):
                    m = dve.tensor_tensor(yacc[:, tt, :], pair[2][:, tt, 0:CW], param2("conv_pw_b_2"), ALU.add)
                m.then_inc(*t.emptied[2].one())
                dve.wait_ge(*t.emptied[2].now())
                split()
                roots16(32, QK2)
                for n, (x, g) in enumerate(((q, "qk_q_g_2"), (k, "qk_k_g_2"))):
                    r = rstd16[:, 16 * n:16 * n + 16].rearrange("p (t h) -> p t h", t=TT).unsqueeze(3)
                    chain(dve.tensor_tensor(x, x, lanes(r, [P, TT, H2, QK2]), ALU.mult))
                    for tt in range(TT):
                        m = dve.tensor_tensor(x[:, tt], x[:, tt], lanes(param2(g).unsqueeze(1), [P, H2, QK2]), ALU.mult)
                    chain(m)
                    m = rope(lambda lo, hi: x[:, :, :, NOPE + lo:NOPE + hi], H2, HALF2, cs2[:, 0, :, :], cs2[:, 1, :, :],
                             qT[:, :, :].rearrange("p a b -> p (a b)"))
                    if n == 0:
                        chain(m)
                m.then_inc(*t["qk_ready"].one())
                dve.wait_ge(*t["qk_ready"].now())
                chain(dve.tensor_tensor(qkv[:, :, ZC0:ZC0 + CW], qkv[:, :, ZC0:ZC0 + CW], yacc[:, :, :], ALU.mult))
                mix_tokens("mla", MLA_STEPS)
                for q in range(2):
                    dve.wait_ge(*t.emptied[outputs_at(q)].now())
                dve.tensor_tensor(qbuf[:, :, 0:MLAW], qbuf[:, :, 0:MLAW], qkv[:, :, ZM0:ZM0 + MLAW], ALU.mult)\
                    .then_inc(*t["branches_ready"].one())
                variances(6, [(2, CW), (2, MLAW), (2, SGW)])
                for n in range(3):
                    for tt in range(TT):
                        m = dve.tensor_scalar(branch(n)[:, tt, :], branch(n)[:, tt, :], rstd[:, 2 * n + tt:2 * n + tt + 1], None,
                                              ALU.mult)
                m.then_inc(*t["y_ready"].one())
                turn_split(range(0, 4), 0, gain("branch_norm_g_2", layer))
                turn_split(range(4, 8), 1, gain("branch_norm_g_2", layer))
                used()
                split()

            dve.wait_ge(sems["params_loaded"], 16 * PARAMS)
            for n in range(2):
                m = dve.tensor_tensor(lamv[:, 2 * n, :], lamv[:, 2 * n, :], lamv[:, 2 * n + 1, :], ALU.mult)
            chain(m)
            for n in range(2):
                m = dve.tensor_reduce(lams[:, 2 * n:2 * n + 2], lamv[:, 2 * n, :].rearrange("p (s d) -> p s d", d=HEAD),
                                      AXIS.X, ALU.add)
            chain(m)
            chain(dve.tensor_copy(pos[:, :], pos_i[:, :]))
            for tt in range(TT):
                m = dve.tensor_scalar(ang[:, tt, :], inv[:, :], pos[:, tt:tt + 1], None, ALU.mult)
            chain(m)
            chain(dve.tensor_scalar(turns_of[:, :, :], ang[:, :, :], 1.0 / (2 * math.pi), ROUND, ALU.mult, ALU.add))
            chain(dve.tensor_scalar(turns_of[:, :, :], turns_of[:, :, :], -ROUND, None, ALU.add))
            for part in TURN_PARTS:
                chain(dve.scalar_tensor_tensor(out=ang[:, :, :], in0=turns_of[:, :, :], scalar=-part, in1=ang[:, :, :],
                                               op0=ALU.mult, op1=ALU.add))
            chain(dve.tensor_scalar(cos1[:, :, :], ang[:, :, :], math.pi / 2, None, ALU.add))
            chain(dve.tensor_scalar(turns_of[:, :, :], cos1[:, :, :], math.pi, -2 * math.pi, ALU.is_gt, ALU.mult))
            chain(dve.tensor_tensor(cos1[:, :, :], cos1[:, :, :], turns_of[:, :, :], ALU.add))
            dve.tensor_scalar(sin1[:, :, :], ang[:, :, :], PI_BELOW, -PI_BELOW, ALU.min, ALU.max).then_inc(*t["dve_step"].one())
            dve.tensor_scalar(cos1[:, :, :], cos1[:, :, :], PI_BELOW, -PI_BELOW, ALU.min, ALU.max).then_inc(*t["angles_ready"].one())
            dve.tensor_scalar(sinks8[:, :], sinks[:, :], 1.0 / SCALE["swa"], None, ALU.mult).then_inc(*t["dve_step"].one())
            split()
            split()
            t.filled[2].n += 1
            t.filled[3].n += 1
            dve.wait_ge(*t.emptied[2].after())
            dve.wait_ge(*t.emptied[3].after())
            dve.wait_ge(*t["sines_ready"].after(3))
            chain(dve.tensor_tensor(neglam[:, :], lams[:, 2:4], lams[:, 0:2], ALU.subtract))
            for n, layer in enumerate(LAMBDA_INIT):
                at = ROW_AT["diff_subln_g"] + n
                dve.tensor_scalar(neglam[:, n:n + 1], neglam[:, n:n + 1], -LAMBDA_INIT[layer], None, ALU.add)\
                    .then_inc(*t["dve_step"].one())
                dve.tensor_scalar(subg[:, n:n + 1], colsB[:, at:at + 1], 1.0 - LAMBDA_INIT[layer], None, ALU.mult)\
                    .then_inc(*t["params_ready"].one())
            step()

            for layer, mixer in enumerate(MIXERS):
                t.lam = layer // 3
                norm(gain("attn_norm_g", layer), add_mlp if layer else None)
                mix_tokens(mixer, mixer_steps(mixer), gain_sub(t.lam) if mixer == "diff" else None)
                norm(gain("mlp_norm_g", layer), add_out, root=False)
                mlp()
            for n in range(2):
                used(1)
                add_mlp(n)
            split()
            variances(TT, [(TT, D)])
            dve.wait_ge(sems["gains_loaded"], 16)
            for tt in range(TT):
                m = dve.scalar_tensor_tensor(out=h[:, tt, :], in0=h[:, tt, :], scalar=rstd[:, tt:tt + 1], in1=fing,
                                             op0=ALU.mult, op1=ALU.mult)
            m.then_inc(*t["h_ready"].one())
            dve.wait_ge(*t["h_ready"].now())
            for layer in range(DEPTH_2):
                second(layer)
            for n in range(2):
                used(1)
                add_out(n)

        @block.sync
        def _(sp):
            t = tallies()

            def load(src, T, w):
                s = t.block % 2
                if t.block >= 2:
                    sp.wait_ge(*t["lo_split"].now(2))
                sp.dma_start(slot(raw, s, T, w), src).then_inc(*t.loaded[s].one(16))
                t["lo_split"].n += 2
                t.block += 1

            def tiles(w):
                return w.rearrange("(t p) n -> p t n", p=P)

            def loads(mixer, w_in, w_out):
                for n, w in in_blocks(mixer):
                    load(tiles(w_in[:, n:n + w]), KT, w)
                out_loads(w_out)

            def out_loads(w_out):
                for g in range(2):
                    load(tiles(w_out[g * BANK:(g + 1) * BANK, :]), 4, D)

            def mlp_loads(w_up, w_down):
                def up(j):
                    load(tiles(w_up[:, bass.ds(j * BANK, BANK)]), KT, BANK)

                def down(j):
                    load(tiles(w_down[bass.ds(j * BANK, BANK), :]), 4, D)

                up(0)
                up(1)
                down(0)
                with sp.Fori(0, 3) as i:
                    turns(t, i, MLP_TURN)
                    for b in range(2):
                        up(2 * i + 2 + b)
                        down(2 * i + 1 + b)
                after_turns(t, MLP_TURN, 3, 4)
                down(7)

            sp.dma_start(h[:, :, :], a["x"][0].rearrange("(t p) n -> p t n", p=P)).then_inc(*t["x_loaded"].one(16))
            for layer, mixer in enumerate(MIXERS):
                which = layer // 3
                name = {"diff": "diff", "moba": "moba", "swa": "swa"}[mixer]
                loads(mixer, a[f"{name}_w_in"][which], a[f"{name}_w_out"][which])
                mlp_loads(a["mlp_w_up"][layer], a["mlp_w_down"][layer])
            for layer in range(DEPTH_2):
                w_in = a["w_in_2"][layer]
                for n, w in W_IN_2_BLOCKS:
                    load(tiles(w_in[:, n:n + w]), KT, w)
                for n in range(2):
                    load(tiles(a["w_uq_2"][layer][:, n * 384:(n + 1) * 384]), 6, 384)
                for n in range(2):
                    load(tiles(a["w_ukv_2"][layer][:, n * BANK:(n + 1) * BANK]), 2, BANK)
                load(tiles(a["conv_pw_w_2"][layer]), 2, CW)
                out_loads(a["w_out_2"][layer])
            for p in (2, 3):
                sp.wait_ge(sems[f"emptied{p}"], emptied_by_layer[-1][p])
            sp.dma_start(out[0].rearrange("(t p) n -> p t n", p=P), h[:, :, :]).then_inc(*t["stored"].one(16))
            sp.wait_ge(*t["stored"].now())

        @block.gpsimd
        def _(pool):
            t = tallies()
            pool.dma_start(pos_i[:, :], a["positions"][0].rearrange("(t p) -> p t", p=P),
                           allow_slow_non_contiguous=True).then_inc(*t["params_loaded"].one(16))
            pool.dma_start(inv[:, :], a["inv_freq"].partition_broadcast(P)).then_inc(*t["params_loaded"].one(16))
            for n, key in enumerate(LAMBDAS):
                pool.dma_start(lamv[:, n, :], a[key].rearrange("s d -> (s d)").partition_broadcast(P))\
                    .then_inc(*t["params_loaded"].one(16))
            pool.dma_start(sinks[:, :], a["swa_sinks"][0].partition_broadcast(P)).then_inc(*t["params_loaded"].one(16))
            pool.dma_start(swab[:, :], a["swa_b_in"][0].partition_broadcast(P)).then_inc(*t["params_loaded"].one(16))
            for layer in range(DEPTH_2):
                pool.dma_start(wsg[:, layer, :, :], a["sg_w_2"][layer].rearrange("g t s -> t g s"))\
                    .then_inc(*t["mixing_loaded"].one(16))
            for n, key in enumerate(["cos_2", "sin_2"]):
                pool.dma_start(cs2[:, n, :, :], a[key].rearrange("(t p) n -> p t n", p=P)).then_inc(*t["params_loaded"].one(16))
            pool.memset(ident[:, :], 0.0).then_inc(*t["pool_step"].one())
            pool.memset(ident_b[:, :], 0.0).then_inc(*t["pool_step"].one())
            pool.memset(causal[:, :], 0.0).then_inc(*t["pool_step"].one())
            pool.memset(band[:, :], 0.0).then_inc(*t["pool_step"].one())
            pool.wait_ge(*t["pool_step"].now())
            pool.affine_select(out=ident[:, :], in_=ident[:, :], compare_op=ALU.not_equal, fill=1.0, base=0,
                               pattern=[[-1, P]], channel_multiplier=1).then_inc(*t["consts_made"].one())
            pool.affine_select(out=ident_b[:, :], in_=ident_b[:, :], compare_op=ALU.not_equal, fill=1.0, base=0,
                               pattern=[[-1, P]], channel_multiplier=1).then_inc(*t["consts_made"].one())
            for m in (causal, band):
                for at in (0, 2 * P):
                    pool.affine_select(out=m[:, at:at + P], in_=m[:, at:at + P], compare_op=ALU.is_ge, fill=NEG, base=0,
                                       pattern=[[-1, P]], channel_multiplier=1).then_inc(*t["consts_made"].one())
            pool.affine_select(out=band[:, P:2 * P], in_=band[:, P:2 * P], compare_op=ALU.is_gt, fill=NEG, base=0,
                               pattern=[[1, P]], channel_multiplier=-1).then_inc(*t["consts_made"].one())
            pool.wait_ge(*t["mixing_loaded"].now())
            pool.affine_select(out=wsg[:, :, :, :].rearrange("p l g s -> p (l g) s"),
                               in_=wsg[:, :, :, :].rearrange("p l g s -> p (l g) s"), compare_op=ALU.is_ge, fill=0.0, base=0,
                               pattern=[[0, DEPTH_2 * 4], [-1, P]], channel_multiplier=1).then_inc(*t["mixing_masked"].one())
            pool.wait_ge(sems["block_used"], 2 * sum(len(in_blocks(m)) + 2 + 2 * (FF // BANK) for m in MIXERS[:3]))
            pool.dma_start(fing, a["final_norm_g"].partition_broadcast(P)).then_inc(*t["gains_loaded"].one(16))
            for layer in range(DEPTH_2):
                if layer == 0:
                    pool.wait_ge(sems["h_ready"], 1)
                else:
                    for p in (2, 3):
                        pool.wait_ge(sems[f"emptied{p}"], emptied_by_layer[layer - 1][p])
                for name, _ in SPREAD_2:
                    pool.dma_start(param2(name), a[name][layer].partition_broadcast(P)).then_inc(*t["spread_loaded"].one(16))


_INS = ["x", "positions", "attn_norm_g", "mlp_norm_g", "diff_w_in", "diff_w_out", "diff_lam_q1", "diff_lam_k1", "diff_lam_q2",
        "diff_lam_k2", "diff_subln_g", "moba_w_in", "moba_w_out", "swa_w_in", "swa_b_in", "swa_sinks", "swa_w_out",
        "mlp_w_up", "mlp_w_down", "final_norm_g", "norm_g_2", "w_in_2", "conv_w_2", "conv_b_2", "conv_ln_g_2", "conv_ln_b_2",
        "conv_pw_w_2", "conv_pw_b_2", "q_norm_g_2", "w_uq_2", "kv_norm_g_2", "w_ukv_2", "qk_q_g_2", "qk_k_g_2", "sg_ln_g_2",
        "sg_ln_b_2", "sg_w_2", "sg_b_2", "branch_norm_g_2", "w_out_2"]


def _tables():
    f = np.float32
    inv1 = f(ROPE_THETA) ** (-np.arange(0, 2 * HALF, 2, dtype=f) / f(2 * HALF))
    inv2 = f(10000.0) ** (-np.arange(HALF2, dtype=f) / f(HALF2))
    angle = np.arange(SEQ, dtype=f)[:, None] * inv2[None, :].astype(f)
    return {"inv_freq": inv1.astype(f), "cos_2": np.cos(angle).astype(f), "sin_2": np.sin(angle).astype(f)}


def kernel(**inputs):
    import concourse.bacc as _bacc
    from concourse.bass_utils import run_bass_kernel_spmd as _run

    nc = _bacc.Bacc("TRN2", target_bir_lowering=False, num_devices=1)
    arrays, args = {}, {}
    for name, v in [(n, inputs[n]) for n in _INS] + list(_tables().items()):
        v = np.ascontiguousarray(v)
        arrays[f"in_{name}"] = v
        args[name] = nc.dram_tensor(f"in_{name}", v.shape, mybir.dt.from_np(v.dtype), kind="ExternalInput").ap()
    result = nc.dram_tensor("result", (1, SEQ, D), FP32, kind="ExternalOutput").ap()
    build(nc, args, result)
    r = _run(nc, [arrays], core_ids=[0])
    return r.results[0]["result"]
```

```python
import math
from contextlib import ExitStack

import concourse.bass as bass
import numpy as np
from concourse import mybir

FP32 = mybir.dt.float32
FP32R = mybir.dt.float32r
INT32 = mybir.dt.int32
BF16 = mybir.dt.bfloat16
ALU = mybir.AluOpType
ACT = mybir.ActivationFunctionType
AXIS = mybir.AxisListType

P = 128
SEQ, D = 256, 1024
TT = SEQ // P
KT = D // P
FF = 4 * D
DEPTH, DEPTH_2 = 4, 2
HEAD = 64
EPS = 1e-6
HALF = 8
ROPE_THETA = 500000.0
NEG = -1.0e30
BANK = 512
SLOT = 4096
CONV_K = 31
ROUND = 1.5 * 2.0 ** 23
TURN_PARTS = [6.28125, 0.0019350051879882812, 3.019916050e-07]
PI_BELOW = 3.1415925
PARAMS = 10
CW, SGW, MLAW = 256, 256, 512
NOPE, ROPE2, QK2, V2, H2 = 64, 32, 96, 64, 8
HALF2 = ROPE2 // 2
QL, KVL = 768, 256
IN_COLS = 3104
A0, GLU0, ZC0, CQ0, CKV0, KR0, ZM0, U0, V0, ZS0 = 0, 256, 512, 768, 1536, 1792, 1824, 2336, 2592, 2848
BLOCKS_2 = [("w_in_2", GLU0 - CW, KT, 512), ("w_in_2", CQ0 + 256, KT, 512), ("w_in_2", CKV0, KT, KVL + ROPE2),
            ("w_in_2", ZC0, KT, 512), ("w_in_2", U0, KT, 512), ("w_uq_2", 0, QL // P, 384), ("w_ukv_2", 0, KVL // P, 512),
            ("w_uq_2", 384, QL // P, 384), ("w_in_2", ZM0, KT, MLAW), ("w_ukv_2", 512, KVL // P, 512), ("w_in_2", ZS0, KT, SGW),
            ("conv_pw_w_2", 0, CW // P, CW)]
UQ_BLOCK, PW_BLOCK = 5, 11
OUT_ORDER_2 = (0, 1, 6, 7, 2, 3, 4, 5)
MIXERS = ["diff", "moba", "swa", "diff"]
QKV_COLS = {"diff": 3072, "moba": 3072, "swa": 1280}
LAMBDAS = ["diff_lam_q1", "diff_lam_k1", "diff_lam_q2", "diff_lam_k2"]
LAMBDA_INIT = {0: 0.8 - 0.6 * math.exp(-0.3 * 0), 3: 0.8 - 0.6 * math.exp(-0.3 * 3)}

ROWS_A = [("conv_w_2", DEPTH_2 * CONV_K * 2), ("conv_b_2", DEPTH_2 * 2)]
ROWS_B = [("attn_norm_g", DEPTH * KT), ("mlp_norm_g", DEPTH * KT), ("diff_subln_g", 2), ("norm_g_2", DEPTH_2 * KT),
          ("q_norm_g_2", DEPTH_2 * 6), ("kv_norm_g_2", DEPTH_2 * 2), ("branch_norm_g_2", DEPTH_2 * KT),
          ("sg_b_2", DEPTH_2 * 4)]
N_ROWS_A = sum(n for _, n in ROWS_A)
N_ROWS_B = sum(n for _, n in ROWS_B)
ROW_AT = {}
for _rows in (ROWS_A, ROWS_B):
    _at = 0
    for _name, _n in _rows:
        ROW_AT[_name] = _at
        _at += _n
SPREAD_2 = [("conv_ln_g_2", CW), ("conv_ln_b_2", CW), ("conv_pw_b_2", CW), ("sg_ln_g_2", SGW), ("sg_ln_b_2", SGW),
            ("qk_q_g_2", QK2), ("qk_k_g_2", QK2)]
SPREAD_AT = {}
_at = 0
for _name, _n in SPREAD_2:
    SPREAD_AT[_name] = (_at, _n)
    _at += _n
SPREAD_COLS = _at


class Tally:

    def __init__(self, sem):
        self.sem, self.n, self.turn = sem, 0, 0

    def one(self, k=1):
        self.n += k
        return self.sem, k

    def after(self, k=1):
        self.n += k
        return self.sem, self.n + self.turn

    def now(self, back=0):
        return self.sem, self.n - back + self.turn


class Tallies:

    def __init__(self, sems):
        self.of = {name: Tally(s) for name, s in sems.items()}
        self.loaded = [self.of[f"raw_loaded{s}"] for s in range(2)]
        self.filled = [self.of[f"filled{p}"] for p in range(10)]
        self.emptied = [self.of[f"emptied{p}"] for p in range(10)]
        self.block = 0
        self.lam = 0

    def __getitem__(self, name):
        return self.of[name]


def build(nc, a, out):
    ctx = ExitStack()
    with ctx:
        def sb(name, shape, dt=FP32):
            return ctx.enter_context(nc.sbuf_tensor(name, shape, dt))

        raw = sb("raw", [P, 2, SLOT])
        whi = sb("whi", [P, 2, SLOT], FP32R)
        wlo = sb("wlo", [P, 2, SLOT], FP32R)
        h = sb("h", [P, TT, D])
        xhi = sb("xhi", [P, KT, SEQ], FP32R)
        xlo = sb("xlo", [P, KT, SEQ], FP32R)
        qkv = sb("qkv", [P, TT, IN_COLS])
        latents = ExitStack()
        lhi = latents.enter_context(nc.sbuf_tensor("lhi", [P, KT, SEQ], FP32R))
        llo = latents.enter_context(nc.sbuf_tensor("llo", [P, KT, SEQ], FP32R))
        latents.close()
        qT = sb("qT", [P, 8, SEQ])
        kT = sb("kT", [P, 8, SEQ])
        sm = sb("sm", [P, 2, 2, 384])
        pT = sb("pT", [P, 2, 2, 384])
        ident = sb("ident", [P, P])
        ident_b = sb("ident_b", [P, P], BF16)
        causal = sb("causal", [P, 384], BF16)
        band = sb("band", [P, 384], BF16)
        colsA = sb("colsA", [P, N_ROWS_A])
        colsB = sb("colsB", [P, N_ROWS_B])
        subg = sb("subg", [P, 2])
        sinks = sb("sinks", [P, 16])
        sinks8 = sb("sinks8", [P, 16])
        wsg = sb("wsg", [P, DEPTH_2, 4, P])
        pos_i = sb("pos_i", [P, TT], INT32)
        pos = sb("pos", [P, TT])
        inv = sb("inv", [P, HALF])
        cos1 = sb("cos1", [P, TT, HALF])
        sin1 = sb("sin1", [P, TT, HALF])
        cs2 = sb("cs2", [P, 2, TT, HALF2])
        ang = sb("ang", [P, TT, HALF])
        turns_of = sb("turns_of", [P, TT, HALF])
        rope_tmp = sb("rope_tmp", [P, 4 * TT * 8 * HALF])
        lams = sb("lams", [P, 4])
        neglam = sb("neglam", [P, 2])
        ss = sb("ss", [P, 12])
        var = sb("var", [P, 12])
        std = sb("std", [P, 12])
        rstd = sb("rstd", [P, 12])
        ss16 = sb("ss16", [P, 32])
        std16 = sb("std16", [P, 32])
        rstd16 = sb("rstd16", [P, 32])
        mx = sb("mx", [P, 2, 2, 2])
        negm = sb("negm", [P, 2, 2, 2])
        snk = sb("snk", [P, 8, 2, 2])
        sums = sb("sums", [P, 8, 2, 2])
        rinv = sb("rinv", [P, 8, 2, 2])
        bn6 = sb("bn6", [P, TT, 6])
        bn2 = sb("bn2", [P, TT, 2])

        first = ExitStack()
        ahi = first.enter_context(nc.sbuf_tensor("ahi", [P, 2, 4, SEQ], FP32R))
        alo = first.enter_context(nc.sbuf_tensor("alo", [P, 2, 4, SEQ], FP32R))
        swab = first.enter_context(nc.sbuf_tensor("swab", [P, QKV_COLS["swa"]], FP32))
        fing = swab[:, 0:D]
        first.close()
        qbuf = sb("qbuf", [P, TT, H2 * QK2])
        kfull = sb("kfull", [P, TT, H2 * QK2])
        kvbuf = qkv[:, :, CQ0:CQ0 + H2 * (NOPE + V2)]
        ypad = sb("ypad", [P, 2, CONV_K - 1 + SEQ])
        yacc = sb("yacc", [P, 2, SEQ])
        tap = sb("tap", [P, SEQ])
        spread = sb("spread", [P, SPREAD_COLS])

        flat_sm, flat_pT = (x[:, :, :, :].rearrange("p a b c -> p (a b c)") for x in (sm, pT))

        relu_at = [qkv[:, 0, j * 1024:(j + 1) * 1024] for j in range(2)]
        square_at = qkv[:, 1, 0:1024]
        lamv = qT[:, 0:2, :].rearrange("p a (b n) -> p (a b) n", b=2)

        pair = [ctx.enter_context(nc.psum_tensor(f"pair{i}", [P, 2, BANK], FP32)) for i in range(4)]

        sem_names = ["raw_loaded0", "raw_loaded1", "hi_split", "lo_split", "block_used",
                     "filled0", "filled1", "filled2", "filled3", "filled4", "filled5", "filled6", "filled7", "filled8",
                     "filled9",
                     "emptied0", "emptied1", "emptied2", "emptied3", "emptied4", "emptied5", "emptied6", "emptied7", "emptied8",
                     "emptied9",
                     "x_loaded", "params_loaded", "rows_loaded", "mixing_loaded", "gains_loaded", "spread_loaded",
                     "pool_step", "consts_made", "mixing_masked", "dve_step", "angles_ready", "sines_ready", "params_ready",
                     "xhi_written", "bank_split", "squares_summed", "var_ready", "std_ready", "rstd_ready", "sum16_ready", "std16_ready",
                     "ahi_written", "alo_written", "roped", "shift_ready", "sink_ready", "p_ready", "rstd16_ready", "h_ready",
                     "sig_ready", "glu_ready", "channels_ready", "conv_ready", "pool_conv_ready", "shared_key_copied", "heads_squared", "ln_ready", "silu_ready", "zsilu_ready", "qk_ready", "gelu_ready",
                     "vln_ready", "branches_ready", "y_ready", "stored"]
        sems = {n: ctx.enter_context(nc.semaphore(n)) for n in sem_names}

        def tallies():
            return Tallies(sems)

        def turns(t, i, per):
            for name, k in per.items():
                t[name].turn = i * k

        def after_turns(t, per, count, blocks):
            for name, k in per.items():
                t[name].turn = 0
                t[name].n += (count - 1) * k
            t.block += (count - 1) * blocks

        MLP_TURN = {"raw_loaded0": 32, "raw_loaded1": 32, "hi_split": 8, "lo_split": 8, "block_used": 8,
                    "emptied0": 1, "emptied1": 1, "ahi_written": 2, "alo_written": 2}

        def slot(buf, s, T, w):
            return buf[:, s, 0:T * w].rearrange("p (t n) -> p t n", t=T)

        def halves(n):
            return [slice(0, n // 2), slice(n // 2, n)]

        def block_plan():
            full, plan = KT * BANK, []
            for mixer in MIXERS:
                plan += [KT * w for _, w in in_blocks(mixer)] + [full] * (2 + 2 * (FF // BANK))
            plan = [(cols, 1) for cols in plan]
            for _ in range(DEPTH_2):
                plan += [(T * w, 1) for _, _, T, w in BLOCKS_2] + [(full, 2), (full, 1)]
            return plan

        def gain(name, layer, n=KT):
            at = ROW_AT[name] + layer * n
            return lambda kt: colsB[:, at + kt:at + kt + 1]

        def gain_latent(layer):
            q, kv = gain("q_norm_g_2", layer, 6), gain("kv_norm_g_2", layer, 2)
            return lambda kt: q(kt) if kt < 6 else kv(kt - 6)

        def gain_branch(layer):
            g = gain("branch_norm_g_2", layer)
            return lambda kt: g(OUT_ORDER_2[kt])

        def gain_sub(which):
            return lambda kt: subg[:, which:which + 1]

        def param2(name):
            at, n = SPREAD_AT[name]
            return spread[:, at:at + n]

        def lanes(ap, shape):
            return ap.to_broadcast(shape)

        def in_blocks(mixer):
            if mixer == "swa":
                return [(1024, 256), (0, BANK), (BANK, BANK)]
            return [(part * D + g * BANK, BANK) for g in range(2) for part in range(3)]

        EIGHTHS = 8

        def mixer_steps(mixer):
            def eighths(what, b):
                return [[(what, b, e)] + ([(what + "_results", b)] if e == EIGHTHS - 1 else []) for e in range(EIGHTHS)]

            def take(fill, n):
                return sum([fill.pop(0) for _ in range(n)], [])

            def head_pair(h, fill, before, after, half=None, late=()):
                split = list(late) + ([] if half is None else [("split", half)])
                done = [("outputs", h // 2)] if h % 2 and (mixer != "diff" or h == 7) else []
                return ([("scores", h)] + take(fill, before) + [("turn", h)] + split + take(fill, after) + [("mix", h)] + done)

            def normed(q):
                return [("outputs", q)] if mixer == "diff" else []

            both = [("split", 0), ("split", 1)]
            ins = [eighths("in", b) for b in range(len(in_blocks(mixer)))]
            out0, out1 = eighths("out", 0), eighths("out", 1)
            steps = take(ins[0], 8) + both + take(ins[1], 8) + [("rope", 0)]
            if mixer == "swa":
                steps += [("split", 0)] + take(ins[2], 4) + [("heads", 0)] + head_pair(0, ins[2], 2, 0, 1)
                steps += head_pair(1, ins[2], 2, 0) + [("rope", 1), ("features", 0)]
                steps += head_pair(2, out0, 2, 0, 0) + head_pair(3, out0, 2, 0, 1)
                steps += [("heads", 1), ("features", 1)] + head_pair(4, out0, 2, 0) + head_pair(5, out0, 2, 0, 0)
                steps += [("features", 2)] + head_pair(6, out1, 2, 0, 1) + head_pair(7, out1, 2, 0)
            else:
                steps += both + take(ins[2], 8) + [("heads", 0)]
                fill = ins[3] + ins[4]
                for h in range(4):
                    steps += head_pair(h, fill, 3, 1, h % 2)
                steps += [("rope", 1), ("split", 0)] + normed(0) + take(ins[5], 4) + [("heads", 1)] + head_pair(4, ins[5], 3, 1)
                steps += [("features", 0), ("split", 1)]
                if mixer == "diff":
                    steps += head_pair(5, out0, 3, 0, 0, normed(1)) + [("features", 1)] + head_pair(6, out0, 3, 0, 1, normed(2))
                    steps += [("features", 2)] + head_pair(7, out0, 2, 0, 0) + take(out1, 4)
                else:
                    steps += head_pair(5, out0, 3, 1, 0) + [("features", 1)] + head_pair(6, out0, 3, 1, 1)
                    steps += [("features", 2)] + head_pair(7, out1, 2, 0, 0) + take(out1, 2)
            steps += [("features", 3)] + ([] if mixer == "swa" else [("split", 1)]) + take(out1, len(out1))
            return steps

        def second_steps():
            ins = [[[("in", b, e)] + ([("in_results", b)] if e == EIGHTHS - 1 else []) for e in range(EIGHTHS)]
                   for b in range(PW_BLOCK)]

            def take(b, n):
                return sum([ins[b].pop(0) for _ in range(n)], [])

            both = [("split", 0), ("split", 1)]
            steps = take(0, 8) + [("glu", 0)] + both + take(1, 4) + [("conv_in", 0)] + take(1, 4) + both + [("taps", range(0, 8))]
            steps += take(2, 8) + both + [("taps", range(8, 12))] + take(3, 8) + both + [("taps", range(12, 25))]
            steps += take(4, 4) + [("latents", 0), ("taps", range(25, CONV_K))] + take(4, 4) + both + [("gelu", 0)]
            steps += take(5, 8) + both + [("v_norm", 0)] + take(6, 8) + both + take(7, 8) + both + [("prep", 0)]
            steps += take(8, 4) + [("sgu_mix", 0), ("sgu_gate", 0), ("conv_norm", 0)] + take(8, 4) + both + [("gates", 0)]
            steps += take(9, 8) + both + [("prep", 1), ("conv_operand", 0)] + take(10, 8) + [("gates", 1), ("pw", 0)]
            steps += [("heads", 0), ("heads", 1), ("scores", 0), ("scores", 1), ("branch_gates", 0), ("turn", 0), ("turn", 1)]
            steps += [("split", 0), ("branches", 0), ("mix", 0), ("scores", 2), ("mix", 1), ("outputs", 0), ("scores", 3), ("y", 0)]
            steps += [("turn", 2), ("turn", 3), ("split", 1), ("mix", 2), ("mix", 3), ("outputs", 1)]
            steps += [("out", 0, e) for e in range(6)] + [("branches", 1)] + both + [("y", 1)]
            steps += [("out", 0, e) for e in range(6, 8)] + [("out_results", 0)] + both
            return steps + [("out", 1, e) for e in range(EIGHTHS)]

        HALF_PAIRS = {4: (1, 0), 5: (1, 1), 6: (2, 0), 7: (2, 1), 8: (3, 0), 9: (3, 1)}
        SHARED_WITH = {0: (), 1: (4, 5), 2: (6, 7), 3: (8, 9), 4: (1,), 5: (1,), 6: (2,), 7: (2,), 8: (3,), 9: (3,)}

        def outputs_at(q):
            return 4 + q % 2

        def features_at(mixer, q):
            return 6 if mixer != "swa" and q == 0 else 4 + q % 2

        def score_pair(mixer, hp):
            return (0, 2)[hp % 2] if mixer == "mla" else 0

        def head_pairs_of_banks(mixer, g):
            return ((2, 3) if mixer == "mla" else (0, 2)) if g else (0, 1)

        def turned_keys(mixer, g):
            if mixer == "swa":
                return [] if g else [0, 1]
            return list(range(4 * g, 4 * g + 4))

        PBLOCKS = [(0, 0, 0), (P, 1, 0), (2 * P, 1, 1)]
        SCALE = {"diff": HEAD ** -0.5, "moba": HEAD ** -0.5, "swa": HEAD ** -0.5, "mla": QK2 ** -0.5}

        def heads(mixer, hp, c):
            if mixer == "mla":
                return qT[0:QK2, 2 * hp + c, :], kT[0:QK2, 2 * hp + c, :]
            rows = slice(c * HEAD, (c + 1) * HEAD)
            return qT[rows, hp, :], kT[rows, hp // 4 if mixer == "swa" else hp, :]

        def values(mixer, hp, c, kt):
            if mixer == "diff":
                return qkv[:, kt, 2048 + hp * P:2048 + (hp + 1) * P]
            if mixer == "moba":
                return qkv[:, kt, 2048 + (2 * hp + c) * HEAD:2048 + (2 * hp + c + 1) * HEAD]
            if mixer == "swa":
                return qkv[:, kt, 1152 + (hp // 4) * HEAD:1152 + (hp // 4 + 1) * HEAD]
            v = (2 * hp + c) * (NOPE + V2) + NOPE
            return kvbuf[:, kt, v:v + V2]

        def q_tile(mixer, n, tt):
            return qbuf[:, tt, n * QK2:(n + 1) * QK2] if mixer == "mla" else qkv[:, tt, n * P:(n + 1) * P]

        def k_tile(mixer, n, tt):
            if mixer == "mla":
                return kfull[:, tt, n * QK2:(n + 1) * QK2]
            at = (1280 if mixer == "swa" else 1024) + n * P
            return qkv[:, tt, at:at + P]

        def o_at(mixer, q):
            return (qbuf if mixer == "mla" else qkv)[:, :, q * 256:(q + 1) * 256]

        def y_tile(kt):
            kt = OUT_ORDER_2[kt]
            if kt < 2:
                return lambda tt: qkv[:, tt, ZC0 + kt * P:ZC0 + (kt + 1) * P]
            if kt < 6:
                return lambda tt: qbuf[:, tt, (kt - 2) * P:(kt - 1) * P]
            return lambda tt: qkv[:, tt, U0 + (kt - 6) * P:U0 + (kt - 5) * P]

        def branch(n):
            return [qkv[:, :, ZC0:ZC0 + CW], qbuf[:, :, 0:MLAW], qkv[:, :, U0:U0 + SGW]][n]

        def block_results(b, tt):
            weights, c0, _, w = BLOCKS_2[b]
            bank = pair[2 + b % 2][:, tt, 0:w]
            if weights == "w_uq_2":
                return [(qbuf[:, tt, c0:c0 + w], bank)], rstd[:, 2 + tt:3 + tt]
            if weights == "w_ukv_2":
                heads_here, n = bank.rearrange("p (h d) -> p h d", d=NOPE + V2), c0 // (NOPE + V2)
                k = kfull[:, tt, :].rearrange("p (h d) -> p h d", d=QK2)[:, n:n + w // (NOPE + V2), 0:NOPE]
                v = kvbuf[:, tt, c0:c0 + w].rearrange("p (h d) -> p h d", d=NOPE + V2)[:, :, NOPE:]
                return [(k, heads_here[:, :, 0:NOPE]), (v, heads_here[:, :, NOPE:])], rstd[:, 4 + tt:5 + tt]
            return [(qkv[:, tt, c0:c0 + w], bank)], rstd[:, tt:tt + 1]

        def h_tile(kt):
            return lambda tt: h[:, tt, kt * P:(kt + 1) * P]

        def o_tile(kt):
            return lambda tt: qkv[:, tt, kt * P:(kt + 1) * P]

        def latent_tile(kt):
            return lambda tt: qkv[:, tt, CQ0 + kt * P:CQ0 + (kt + 1) * P]

        def conv_tile(kt):
            return lambda tt: qkv[:, tt, kt * P:(kt + 1) * P]

        def pair_tile(p, j):
            if p in HALF_PAIRS:
                p, half = HALF_PAIRS[p]
                return pair[p][:, half, j * SEQ:(j + 1) * SEQ]
            return pair[p][:, j // 2, (j % 2) * SEQ:(j % 2 + 1) * SEQ]

        block = ctx.enter_context(nc.Block())
        emptied_by_layer = []

        @block.scalar
        def _(act):
            t = tallies()

            plan = block_plan()

            def split(some=(0, 1)):
                if not plan:
                    return
                s = t.block % 2
                cols_of, transfers = plan[0]
                if 0 in some:
                    act.wait_ge(*t.loaded[s].after(16 * transfers))
                for half in some:
                    cols = halves(cols_of)[half]
                    act.activation(whi[:, s, cols], raw[:, s, cols], ACT.Copy).then_inc(*t["hi_split"].one())
                if 1 in some:
                    plan.pop(0)
                    t.block += 1

            def used(halves_done=2):
                act.wait_ge(*t["block_used"].after(halves_done))

            def turn_split(kts, p, scale_of, x_hi=xhi):
                act.wait_ge(*t.filled[p].after())
                for j, kt in enumerate(kts):
                    g = scale_of(kt) if scale_of else 1.0
                    act.activation(x_hi[:, kt, :], pair_tile(p, j), ACT.Copy, scale=g).then_inc(*t["xhi_written"].one())
                t.emptied[p].n += 1

            def sum_squares(parts, at=0, junk=(flat_sm, flat_pT)):
                for n, src in enumerate(parts):
                    if n >= len(junk):
                        act.wait_ge(*t["squares_summed"].now())
                    act.activation(junk[n % len(junk)][:, 0:src.shape[-1]], src, ACT.Square, accum_out=ss[:, at + n:at + n + 1])\
                        .then_inc(*t["squares_summed"].one())

            def roots(n, at=0):
                act.wait_ge(*t["var_ready"].after())
                act.activation(std[:, at:at + n], var[:, at:at + n], ACT.Sqrt).then_inc(*t["std_ready"].one())

            def norm(g, root=True, fresh=False, waiting=1):
                turn_split(range(0, 4), 0, g)
                turn_split(range(4, 8), 1, g)
                if not fresh:
                    used()
                    t.emptied[2].n += 1
                    t.emptied[3].n += 1
                for _ in range(waiting):
                    split()
                sum_squares([h[:, tt, :] for tt in range(TT)])
                if root:
                    roots(TT)

            def results(p, dst, w, scale):
                if p == 2:
                    for tt in range(TT):
                        used(1)
                        m = act.activation(dst(tt), pair[p][:, tt, 0:w], ACT.Copy, scale=scale(tt))
                    m.then_inc(*t.emptied[p].one())
                else:
                    used()
                    t.emptied[p].n += 1

            def queries_out(mixer, g):
                rows = QK2 if mixer == "mla" else P
                p, pk = head_pairs_of_banks(mixer, g)
                act.wait_ge(*t.filled[p].after())
                act.activation(qT[0:rows, 4 * g:4 * g + 4, :], pair[p][0:rows, :, :].rearrange("p b (j n) -> p (b j) n", j=2),
                               ACT.Copy).then_inc(*t.emptied[p].one())
                if turned_keys(mixer, g):
                    t.filled[pk].n += 1
                    t.emptied[pk].n += 1

            def exps(mixer, hp):
                b, p = hp % 2, score_pair(mixer, hp)
                act.wait_ge(*t["shift_ready"].after())
                t.filled[p].n += 1
                for c in range(2):
                    for tt, cols in ((0, slice(0, P)), (1, slice(P, 3 * P))):
                        m = act.activation(sm[:, b, c, cols], pair[p][:, c, cols], ACT.Exp, scale=SCALE[mixer],
                                           bias=negm[:, b, c, tt:tt + 1], accum_out=sums[:, hp, c, tt:tt + 1])
                m.then_inc(*t.emptied[p].one())

            def probs_out(mixer, hp):
                p = score_pair(mixer, hp)
                if mixer == "diff":
                    act.wait_ge(*t.filled[p].after())
                    act.activation(pT[:, hp % 2, 0, :], pair[p][:, 0, 0:384], ACT.Copy).then_inc(*t.emptied[p].one())
                else:
                    t.filled[p].n += 1
                    t.emptied[p].n += 1

            def outputs(mixer, q):
                p = outputs_at(q)
                if mixer == "diff":
                    act.wait_ge(*t.filled[p].after())
                    parts = [(tt, j) for tt in range(TT) for j in range(2)]

                    def columns(tt, j):
                        return pair[1][:, q % 2, (j * TT + tt) * P:(j * TT + tt + 1) * P]

                    for i, (tt, j) in enumerate(parts):
                        at = D + (2 * q + j) * P
                        m = act.activation(qkv[:, tt, at:at + P], columns(tt, j), ACT.Square,
                                           accum_out=ss16[:, 4 * q + i:4 * q + i + 1])
                    m.then_inc(*t["heads_squared"].one())
                    roots16(4, 4 * q)
                    act.wait_ge(*t["rstd16_ready"].after())
                    for i, (tt, j) in enumerate(parts):
                        m = act.activation(o_at(mixer, q)[:, tt, j * P:(j + 1) * P], columns(tt, j), ACT.Copy,
                                           scale=rstd16[:, 4 * q + i:4 * q + i + 1])
                    m.then_inc(*t.emptied[p].one())
                    return
                t.filled[p].n += 1
                t.emptied[p].n += 1
                if mixer == "swa":
                    sink = snk[:, 2 * q:2 * q + 2, :, :]
                    act.activation(sink, sink, ACT.Exp).then_inc(*t["sink_ready"].one())

            def mix_tokens(mixer, steps, g_o=None):
                for what, n, *_ in steps:
                    if what == "in_results":
                        c0, w = in_blocks(mixer)[n]
                        if mixer == "swa":
                            used()
                            t.emptied[2 + n % 2].n += 1
                        else:
                            if n == 0:
                                act.wait_ge(*t["rstd_ready"].after())
                            results(2 + n % 2, lambda tt: qkv[:, tt, c0:c0 + w], w, lambda tt: rstd[:, tt:tt + 1])
                    elif what == "heads":
                        queries_out(mixer, n)
                    elif what == "scores":
                        exps(mixer, n)
                    elif what == "turn":
                        probs_out(mixer, n)
                    elif what == "outputs":
                        outputs(mixer, n)
                    elif what == "features":
                        turn_split(range(2 * n, 2 * n + 2), features_at(mixer, n), g_o)
                    elif what == "out_results" and n == 0:
                        used()
                    elif what == "split":
                        split((n,))

            def roots16(n, at=0):
                act.wait_ge(*t["sum16_ready"].after())
                act.activation(std16[:, at:at + n], ss16[:, at:at + n], ACT.Sqrt).then_inc(*t["std16_ready"].one())

            def mlp():
                def up(j):
                    b = j % 2
                    used()
                    act.activation(relu_at[b], pair[b][:, :, :].rearrange("p b n -> p (b n)"), ACT.Relu)\
                        .then_inc(*t.emptied[b].one())
                    act.wait_ge(*t.emptied[b].now())
                    act.activation(ahi[:, b, :, :].rearrange("p f n -> p (f n)"), relu_at[b], ACT.Square)\
                        .then_inc(*t["ahi_written"].one())
                    split()

                def down():
                    used()
                    split()

                up(0)
                up(1)
                down()
                with act.Fori(0, 3) as i:
                    turns(t, i, MLP_TURN)
                    up(0)
                    down()
                    up(1)
                    down()
                after_turns(t, MLP_TURN, 3, 4)
                del plan[:8]

            def block_out(b):
                for tt in range(TT):
                    used(1)
                    places, scale = block_results(b, tt)
                    for dst, src in places:
                        m = act.activation(dst, src, ACT.Copy, scale=scale)
                m.then_inc(*t.emptied[2 + b % 2].one())

            def second(layer):
                norm(gain("norm_g_2", layer), fresh=layer == 0, waiting=1 if layer else 0)
                act.wait_ge(*t["rstd_ready"].after())
                for step in second_steps():
                    what, n = step[0], step[1]
                    if what == "in_results":
                        block_out(n)
                    elif what == "glu":
                        act.wait_ge(*t.emptied[2].now())
                        act.activation(qkv[:, :, GLU0:GLU0 + CW], qkv[:, :, GLU0:GLU0 + CW], ACT.Sigmoid)\
                            .then_inc(*t["sig_ready"].one())
                    elif what == "conv_in":
                        act.wait_ge(*t.filled[0].after())
                        act.activation(ypad[:, 1, CONV_K - 1:], pair[0][:, 0, SEQ:], ACT.Copy).then_inc(*t["channels_ready"].one())
                        act.activation(ypad[:, 0, CONV_K - 1:], pair[0][:, 0, 0:SEQ], ACT.Copy).then_inc(*t.emptied[0].one())
                    elif what == "latents":
                        turn_split(range(0, 4), 0, gain_latent(layer), lhi)
                        turn_split(range(4, 8), 1, gain_latent(layer), lhi)
                        sum_squares([qkv[:, tt, c:c + w] for c, w in ((CQ0, QL), (CKV0, KVL)) for tt in range(TT)], 2)
                        roots(4, 2)
                        act.wait_ge(*t["rstd_ready"].after())
                        kr = qkv[:, :, KR0:KR0 + ROPE2].unsqueeze(2)
                        act.activation(kfull[:, :, :].rearrange("p t (h d) -> p t h d", d=QK2)[:, :, :, NOPE:QK2],
                                       lanes(kr, [P, TT, H2, ROPE2]), ACT.Copy).then_inc(*t["shared_key_copied"].one())
                    elif what == "conv_norm":
                        t.filled[4].n += 1
                        t.emptied[4].n += 1
                        roots(TT, 6)
                        act.wait_ge(*t["ln_ready"].after())
                        act.activation(qkv[:, :, 0:CW], qkv[:, :, 0:CW], ACT.Silu).then_inc(*t["silu_ready"].one())
                    elif what == "prep":
                        for p in (2, 3):
                            act.wait_ge(*t.emptied[p].now())
                        if n == 1:
                            act.wait_ge(*t["shared_key_copied"].now())
                        x, squares = ((qbuf, flat_sm), (kfull, flat_pT))[n]
                        act.activation(squares, x[:, :, :].rearrange("p t n -> p (t n)"), ACT.Square)\
                            .then_inc(*t["heads_squared"].one())
                        roots16(16, 16 * n)
                    elif what == "gelu":
                        act.wait_ge(*t.emptied[2].now())
                        for c in (V0, U0):
                            act.activation(qkv[:, :, c:c + SGW], qkv[:, :, c:c + SGW], ACT.Gelu_apprx_tanh)\
                                .then_inc(*t["gelu_ready"].one())
                    elif what == "conv_operand":
                        turn_split(range(2), 5, None, lhi)
                    elif what == "gates":
                        act.wait_ge(*t.emptied[2].now())
                        for c, w in ((ZS0, SGW),) if n else ((ZC0, CW), (ZM0, MLAW)):
                            act.activation(qkv[:, :, c:c + w], qkv[:, :, c:c + w], ACT.Silu).then_inc(*t["zsilu_ready"].one())
                    elif what == "pw":
                        used()
                        t.emptied[3].n += 1
                    elif what == "v_norm":
                        roots(TT, 6)
                    elif what == "sgu_mix":
                        t.filled[8].n += 1
                        t.emptied[8].n += 1
                    elif what == "branches":
                        act.wait_ge(*t["branches_ready"].after())
                        if n == 0:
                            sum_squares([branch(x)[:, tt, :] for x in (0, 2) for tt in range(TT)], 8,
                                        [ypad[:, ct, CONV_K - 1:] for ct in range(2)])
                            roots(4, 8)
                        else:
                            sum_squares([branch(1)[:, tt, :] for tt in range(TT)], 2, [yacc[:, :, :].rearrange("p a b -> p (a b)")])
                            roots(TT, 2)
                        t["rstd_ready"].n += 1
                    elif what == "y":
                        g = gain_branch(layer)
                        if n == 0:
                            turn_split(range(0, 2), 8, g)
                            turn_split(range(2, 4), 9, g)
                        else:
                            turn_split(range(4, 8), 0, g)
                    elif what == "out_results":
                        used()
                    elif what == "split":
                        split((n,))
                    else:
                        mix_tokens("mla", [step])
                if layer == DEPTH_2 - 1:
                    used()

            rows_a = sm[:, 0, 0, 0:P]
            rows_b = sm[0:N_ROWS_B, 0, 1, 0:P]
            for tile_at, rows in ((rows_a, ROWS_A), (rows_b, ROWS_B)):
                for name, n in rows:
                    v = a[name]
                    flat = v.rearrange("a b c -> (a b c)") if len(v.shape) == 3 else v.rearrange("a b -> (a b)")
                    act.dma_start(tile_at[ROW_AT[name]:ROW_AT[name] + n, :], flat.rearrange("(r p) -> r p", p=P))\
                        .then_inc(*t["rows_loaded"].one(16))
            act.wait_ge(*t.filled[2].after())
            act.activation(colsA[:, :], pair[2][:, 0, 0:N_ROWS_A], ACT.Copy)
            act.activation(colsB[:, :], pair[2][:, 1, 0:N_ROWS_B], ACT.Copy).then_inc(*t.emptied[2].one())
            act.wait_ge(*t.emptied[2].now())
            for layer, mixer in enumerate(MIXERS):
                norm(gain("attn_norm_g", layer), fresh=layer == 0, waiting=1 if layer else 2)
                if layer == 0:
                    act.wait_ge(*t.filled[3].after())
                    act.activation(wsg[:, :, :, :].rearrange("p l g t -> p l (g t)"), pair[3][:, :, :], ACT.Copy)\
                        .then_inc(*t.emptied[3].one())
                    act.wait_ge(*t["angles_ready"].after())
                    act.activation(sin1[:, :, :], sin1[:, :, :], ACT.Sin).then_inc(*t["sines_ready"].one())
                    act.activation(cos1[:, :, :], cos1[:, :, :], ACT.Sin).then_inc(*t["sines_ready"].one())
                    act.activation(lams[:, :], lams[:, :], ACT.Exp).then_inc(*t["sines_ready"].one())
                if mixer == "swa":
                    t["rstd_ready"].n += 1
                mix_tokens(mixer, mixer_steps(mixer), gain_sub(layer // 3) if mixer == "diff" else None)
                norm(gain("mlp_norm_g", layer), root=False)
                mlp()
            used()
            t.emptied[2].n += 1
            t.emptied[3].n += 1
            act.wait_ge(*t.emptied[2].now())
            act.wait_ge(*t.emptied[3].now())
            sum_squares([h[:, tt, :] for tt in range(TT)])
            roots(TT)
            t["rstd_ready"].n += 1
            split()
            for layer in range(DEPTH_2):
                second(layer)

        @block.tensor
        def _(pe):
            t = tallies()

            def free(p):
                for q in (p,) + SHARED_WITH[p]:
                    if t.emptied[q].n:
                        pe.wait_ge(*t.emptied[q].now())
                t.emptied[p].n += 1

            def products(dst, x, w, first, last):
                (x_hi, x_lo), (w_hi, w_lo) = x, w
                pe.matmul(dst, x_hi, w_hi, start=first, stop=False)
                pe.matmul(dst, x_hi, w_lo, start=False, stop=False)
                return pe.matmul(dst, x_lo, w_hi, start=False, stop=last)

            def token_major(p, T, w, k0=0, eighth=None, opening=False, x=(xhi, xlo)):
                units = [(tt, k) for tt in range(TT) for k in range(T)]
                if opening:
                    units.sort(key=lambda u: u[1] // (KT // 2))
                n = len(units)
                some = range(n) if eighth is None else range(eighth * n // EIGHTHS, (eighth + 1) * n // EIGHTHS)
                s = t.block % 2
                w_hi, w_lo = slot(whi, s, T, w), slot(wlo, s, T, w)
                for u in some:
                    if u == 0:
                        pe.wait_ge(*t["lo_split"].after(2))
                        free(p)
                    if opening:
                        open_layer(u)
                    tt, k = units[u]
                    tok = slice(tt * P, (tt + 1) * P)
                    m = products(pair[p][:, tt, 0:w], (x[0][:, k0 + k, tok], x[1][:, k0 + k, tok]),
                                 (w_hi[:, k, :], w_lo[:, k, :]), k == 0, k == T - 1)
                    if k == T - 1:
                        m.then_inc(*t["block_used"].one())
                if some[-1] == n - 1:
                    t.block += 1

            def open_layer(u):
                if u in (0, 8):
                    pe.wait_ge(*t["bank_split"].after())
                elif u in (2, 10):
                    turned(u // 8)
                elif u == 4:
                    turn_stream(1)

            def turn_stream(half, fresh=False):
                if not fresh:
                    pe.wait_ge(*t.emptied[2 + half].now())
                turn(range(4 * half, 4 * half + 4), half, h_tile)

            BY_COLUMNS = [(n, tt, f) for n in range(2) for tt in range(TT) for f in range(4)]
            BY_FEATURES = sorted(BY_COLUMNS, key=lambda u: u[2] // 2)

            def accumulate(x_hi, x_lo, first, last, order, eighth=None, closing=False, operand=None, tiles=range(4)):
                n_units = len(order)
                some = range(n_units) if eighth is None else range(eighth * n_units // EIGHTHS, (eighth + 1) * n_units // EIGHTHS)
                s = t.block % 2
                w_hi, w_lo = slot(whi, s, 4, D), slot(wlo, s, 4, D)
                for u in some:
                    n, tt, f = order[u]
                    if u == 0:
                        pe.wait_ge(*t["lo_split"].after(2))
                        if first:
                            free(2)
                            free(3)
                    if operand:
                        operand(u)
                    if closing and u == n_units - (4 if order is BY_COLUMNS else 2):
                        turn_stream(0)
                    cols, tok = slice(n * BANK, (n + 1) * BANK), slice(tt * P, (tt + 1) * P)
                    m = products(pair[2 + n][:, tt, :], (x_hi[:, tiles[f], tok], x_lo[:, tiles[f], tok]),
                                 (w_hi[:, f, cols], w_lo[:, f, cols]), first and f == 0, last and f == 3)
                    if (tt, f) == (TT - 1, 3):
                        m.then_inc(*t["block_used"].one())
                if some[-1] == n_units - 1:
                    t.block += 1

            def out_part(g, operand, eighth=None, closing=True):
                accumulate(xhi, xlo, g == 0, g == 1, BY_FEATURES, eighth, closing and g == 1, operand, range(4 * g, 4 * g + 4))

            def turn(kts, p, tile):
                free(p)
                for j, kt in enumerate(kts):
                    for tt in range(TT):
                        m = pe.transpose(pair_tile(p, j)[:, tt * P:(tt + 1) * P], tile(kt)(tt), ident[:, :])
                m.then_inc(*t.filled[p].one())

            def turned(*pairs):
                for p in pairs:
                    pe.wait_ge(*t.emptied[p].now())

            def turn_heads(mixer, g):
                if mixer != "mla":
                    pe.wait_ge(*t["roped"].after())
                if mixer in ("diff", "moba") and g == 0:
                    pe.wait_ge(*t.emptied[2].now())
                rows = QK2 if mixer == "mla" else P
                for p, tiles, tile in zip(head_pairs_of_banks(mixer, g), (range(4 * g, 4 * g + 4), turned_keys(mixer, g)),
                                          (q_tile, k_tile)):
                    if not tiles:
                        continue
                    free(p)
                    for j, n in enumerate(tiles):
                        for tt in range(TT):
                            m = pe.transpose(pair_tile(p, j)[0:rows, tt * P:(tt + 1) * P], tile(mixer, n, tt), ident[:, :])
                    m.then_inc(*t.filled[p].one())

            def scores(mixer, hp):
                p = score_pair(mixer, hp)
                free(p)
                if hp in (0, 4):
                    for q in (1, 2, 3) if mixer == "mla" else head_pairs_of_banks(mixer, hp // 4)[1:]:
                        if q != p and turned_keys(mixer, hp // 4):
                            pe.wait_ge(*t.emptied[q].now())
                mask = band if mixer == "swa" else causal
                masked = P if mixer == "swa" else 2 * P
                for c in range(2):
                    q, k = heads(mixer, hp, c)
                    pe.matmul(pair[p][:, c, 0:P], q[:, 0:P], k[:, 0:P], start=True, stop=False)
                    pe.matmul(pair[p][:, c, 0:P], ident_b[:, :], mask[:, 0:P], start=False, stop=True)
                    pe.matmul(pair[p][:, c, P:3 * P], q[:, P:2 * P], k[:, :], start=True, stop=False)
                    m = pe.matmul(pair[p][:, c, masked:3 * P], ident_b[:, :], mask[:, masked:3 * P], start=False, stop=True)
                m.then_inc(*t.filled[p].one())

            def turn_probs(mixer, hp):
                p = score_pair(mixer, hp)
                if mixer == "diff":
                    pe.wait_ge(*t["p_ready"].after())
                free(p)
                for c in range(1 if mixer == "diff" else 2):
                    for at, _, _ in PBLOCKS:
                        m = pe.transpose(pair[p][:, c, at:at + P], sm[:, hp % 2, c, at:at + P], ident[:, :])
                m.then_inc(*t.filled[p].one())

            def mix_values(mixer, hp):
                pe.wait_ge(*t.emptied[score_pair(mixer, hp)].now())
                j, b = hp % 4, hp % 2
                if b == 0:
                    free(outputs_at(hp // 2))
                if hp == 4 and mixer in ("diff", "moba"):
                    pe.wait_ge(*t.emptied[3].now())
                w = P if mixer == "diff" else V2
                for c in range(1 if mixer == "diff" else 2):
                    for qt in range(TT):
                        at = (j % 2) * SEQ + qt * P + c * V2
                        for col, _, kt in [x for x in PBLOCKS if x[1] == qt]:
                            m = pe.matmul(pair[1][:, j // 2, at:at + w], pT[:, b, c, col:col + P], values(mixer, hp, c, kt),
                                          start=kt == 0, stop=kt == qt)
                if b == 1:
                    m.then_inc(*t.filled[outputs_at(hp // 2)].one())

            def mix_tokens(mixer, steps, fresh=False):
                for what, n, *eighth in steps:
                    if what == "in":
                        token_major(2 + n % 2, KT, in_blocks(mixer)[n][1], 0, eighth[0], opening=n == 0 and not fresh)
                    elif what == "heads":
                        turn_heads(mixer, n)
                    elif what == "scores":
                        scores(mixer, n)
                    elif what == "turn":
                        turn_probs(mixer, n)
                    elif what == "mix":
                        mix_values(mixer, n)
                    elif what == "features":
                        pe.wait_ge(*t.emptied[outputs_at(n)].now(1 if mixer != "swa" and n == 0 else 0))
                        turn(range(2 * n, 2 * n + 2), features_at(mixer, n), o_tile)
                    elif what == "out":
                        out_part(n, lambda u: turned(features_at(mixer, 2 * n + u // 8)) if u % 8 == 0 else None, eighth[0])

            def mlp(closing):
                def up(j, opening=False):
                    pe.wait_ge(*t["lo_split"].after(2))
                    free(j % 2)
                    s = t.block % 2
                    w_hi, w_lo = slot(whi, s, KT, BANK), slot(wlo, s, KT, BANK)
                    units = [(f, k) for f in (0, 2, 1, 3) for k in range(KT)]
                    if opening:
                        units.sort(key=lambda u: (u[0] % 2, u[1] // (KT // 2) if u[0] % 2 == 0 else 0))
                    for u, (f, k) in enumerate(units):
                        if opening and u == 0:
                            t["bank_split"].n += 1
                        elif opening and u > 2:
                            open_layer(u)
                        cols = slice(f * P, (f + 1) * P)
                        m = products(pair_tile(j % 2, f), (w_hi[:, k, cols], w_lo[:, k, cols]),
                                     (xhi[:, k, :], xlo[:, k, :]), k == 0, k == KT - 1)
                        if f % 2 and k == KT - 1:
                            m.then_inc(*t["block_used"].one())
                    t.block += 1

                def down(j, first=False, last=False, closing=False):
                    pe.wait_ge(*t["alo_written"].after())
                    accumulate(ahi[:, j % 2, :, :], alo[:, j % 2, :, :], first, last, BY_COLUMNS, closing=closing)

                up(0, opening=True)
                up(1)
                down(0, first=True)
                with pe.Fori(0, 3) as i:
                    turns(t, i, MLP_TURN)
                    up(0)
                    down(1)
                    up(1)
                    down(0)
                after_turns(t, MLP_TURN, 3, 4)
                down(1, last=True, closing=closing)

            def block_products(layer, b, eighth):
                weights, _, T, w = BLOCKS_2[b]
                if weights == "w_in_2":
                    token_major(2 + b % 2, T, w, 0, eighth, opening=b == 0)
                elif eighth in (None, 0):
                    k0 = QL // P if weights == "w_ukv_2" else 0
                    if b == UQ_BLOCK:
                        turned(0, 1)
                    token_major(2 + b % 2, T, w, k0, x=(lhi, llo))

            def second(layer):
                for step in second_steps():
                    what, n = step[0], step[1]
                    if what == "in":
                        block_products(layer, n, step[2])
                    elif what == "conv_in":
                        pe.wait_ge(*t["glu_ready"].after())
                        free(0)
                        for ct in range(2):
                            for tt in range(TT):
                                m = pe.transpose(pair[0][:, 0, ct * SEQ + tt * P:ct * SEQ + (tt + 1) * P], conv_tile(ct)(tt),
                                                 ident[:, :])
                        m.then_inc(*t.filled[0].one())
                    elif what == "latents":
                        pe.wait_ge(*t.emptied[2].now(1))
                        pe.wait_ge(*t.emptied[3].now())
                        turn(range(0, 4), 0, latent_tile)
                        turn(range(4, 8), 1, latent_tile)
                    elif what == "conv_norm":
                        pe.wait_ge(*t["conv_ready"].after())
                        pe.wait_ge(*t["pool_conv_ready"].after())
                        free(4)
                        for ct in range(2):
                            for tt in range(TT):
                                m = pe.transpose(pair[1][:, 0, tt * CW + ct * P:tt * CW + (ct + 1) * P],
                                                 yacc[:, ct, tt * P:(tt + 1) * P], ident[:, :])
                        m.then_inc(*t.filled[4].one())
                    elif what == "conv_operand":
                        pe.wait_ge(*t["silu_ready"].after())
                        turn(range(2), 5, conv_tile)
                    elif what == "pw":
                        turned(5)
                        block_products(layer, PW_BLOCK, None)
                    elif what == "sgu_mix":
                        pe.wait_ge(*t["vln_ready"].after())
                        free(8)
                        for tt in range(TT):
                            for g in range(4):
                                m = pe.matmul(pair[3][:, 0, tt * SGW + g * 64:tt * SGW + (g + 1) * 64], wsg[:, layer, g, :],
                                              qkv[:, tt, V0 + g * 64:V0 + (g + 1) * 64], start=True, stop=True)
                        m.then_inc(*t.filled[8].one())
                    elif what == "y":
                        pe.wait_ge(*t["y_ready"].after())
                        if n == 0:
                            turn(range(0, 2), 8, y_tile)
                            turn(range(2, 4), 9, y_tile)
                        else:
                            turn(range(4, 8), 0, y_tile)
                    elif what == "out":
                        if step[2] == 0:
                            turned(*((8, 9) if n == 0 else (0,)))
                        accumulate(xhi, xlo, n == 0, n == 1, BY_COLUMNS, step[2], n == 1 and layer < DEPTH_2 - 1,
                                   tiles=range(4 * n, 4 * n + 4))
                    else:
                        if step == ("heads", 0):
                            pe.wait_ge(*t["qk_ready"].after(2))
                        mix_tokens("mla", [step])

            pe.wait_ge(sems["consts_made"], 7)
            pe.wait_ge(sems["rows_loaded"], 16 * (len(ROWS_A) + len(ROWS_B)))
            free(2)
            pe.transpose(pair[2][:, 0, 0:N_ROWS_A], sm[:, 0, 0, 0:P], ident[:, :])
            pe.transpose(pair[2][:, 1, 0:N_ROWS_B], sm[0:N_ROWS_B, 0, 1, 0:P], ident[0:N_ROWS_B, 0:N_ROWS_B])\
                .then_inc(*t.filled[2].one())
            pe.wait_ge(sems["x_loaded"], 16)
            for half in range(2):
                turn_stream(half, fresh=True)
            pe.wait_ge(sems["mixing_masked"], 1)
            free(3)
            for layer in range(DEPTH_2):
                for g in range(4):
                    m = pe.transpose(pair[3][:, layer, g * P:(g + 1) * P], wsg[:, layer, g, :], ident[:, :])
            m.then_inc(*t.filled[3].one())
            turned(0, 1)
            t["bank_split"].n += 2
            for layer, mixer in enumerate(MIXERS):
                mix_tokens(mixer, mixer_steps(mixer), fresh=layer == 0)
                mlp(closing=layer < DEPTH - 1)
            pe.wait_ge(sems["h_ready"], 1)
            turn_stream(0, fresh=True)
            for layer in range(DEPTH_2):
                second(layer)
                emptied_by_layer.append({p: t.emptied[p].n for p in (2, 3)})

        @block.vector
        def _(dve):
            t = tallies()
            plan = block_plan()

            def step():
                dve.wait_ge(*t["dve_step"].now())

            def chain(m):
                m.then_inc(*t["dve_step"].one())
                step()

            def split(some=(0, 1)):
                if not plan:
                    return
                s = t.block % 2
                for half in some:
                    cols = halves(plan[0][0])[half]
                    dve.wait_ge(*t["hi_split"].after())
                    dve.tensor_tensor(wlo[:, s, cols], raw[:, s, cols], whi[:, s, cols].bitcast(FP32), ALU.subtract)\
                        .then_inc(*t["lo_split"].one())
                if 1 in some:
                    plan.pop(0)
                    t.block += 1

            def used(halves_done=2):
                dve.wait_ge(*t["block_used"].after(halves_done))

            def turn_split(kts, p, scale_of, x=(xhi, xlo), by_bank=False):
                t.filled[p].n += 1
                for j, kt in enumerate(kts):
                    if j % 2 == 0:
                        dve.wait_ge(*t["xhi_written"].after(2))
                    g = scale_of(kt) if scale_of else 1.0
                    m = dve.scalar_tensor_tensor(out=x[1][:, kt, :], in0=pair_tile(p, j), scalar=g,
                                                 in1=x[0][:, kt, :].bitcast(FP32), op0=ALU.mult, op1=ALU.subtract)
                    if by_bank and j == 1:
                        m.then_inc(*t["bank_split"].one())
                m.then_inc(*t.emptied[p].one())

            def variances(widths, root=True, at=0):
                some = slice(at, at + sum(n for n, _ in widths))
                dve.wait_ge(*t["squares_summed"].after(some.stop - some.start))
                for n, w in widths:
                    m = dve.tensor_scalar(var[:, at:at + n], ss[:, at:at + n], 1.0 / w, EPS, ALU.mult, ALU.add)
                    at += n
                if root:
                    m.then_inc(*t["var_ready"].one())
                    dve.wait_ge(*t["std_ready"].after())
                    dve.reciprocal(rstd[:, some], std[:, some]).then_inc(*t["rstd_ready"].one())
                    dve.wait_ge(*t["rstd_ready"].now())
                else:
                    chain(m)
                    chain(dve.reciprocal(rstd[:, some], var[:, some]))

            def norm(g, add, root=True, waiting=1):
                for n in range(2):
                    if add:
                        used(1)
                        add(n)
                    turn_split(range(4 * n, 4 * n + 4), n, g, by_bank=True)
                for _ in range(waiting):
                    split()
                variances([(TT, D)], root)

            def results(p, dst, w, scale):
                if p == 3:
                    for tt in range(TT):
                        used(1)
                        m = dve.tensor_scalar(dst(tt), pair[p][:, tt, 0:w], scale(tt), None, ALU.mult)
                    m.then_inc(*t.emptied[p].one())
                else:
                    used()
                    t.emptied[p].n += 1

            def biased_results(n):
                c0, w = in_blocks("swa")[n]
                p = 2 + n % 2
                for tt in range(TT):
                    used(1)
                    m = dve.scalar_tensor_tensor(out=qkv[:, tt, c0:c0 + w], in0=pair[p][:, tt, 0:w], scalar=rstd[:, tt:tt + 1],
                                                 in1=swab[:, c0:c0 + w], op0=ALU.mult, op1=ALU.add)
                m.then_inc(*t.emptied[p].one())

            def rope(view, n, half, cos, sin, place):
                shape = [P, TT, n, half]
                x1, x2 = view(0, half), view(half, 2 * half)
                c = lanes(cos.unsqueeze(2), shape)
                s = lanes(sin.unsqueeze(2), shape)
                size = TT * n * half
                tmp = [place[:, k * size:(k + 1) * size].rearrange("p (t n f) -> p t n f", t=TT, n=n) for k in range(4)]
                for dst, x, y in ((tmp[0], x1, c), (tmp[1], x2, s), (tmp[2], x2, c), (tmp[3], x1, s)):
                    dve.tensor_tensor(dst, x, y, ALU.mult).then_inc(*t["dve_step"].one())
                step()
                dve.tensor_tensor(x1, tmp[0], tmp[1], ALU.subtract).then_inc(*t["dve_step"].one())
                return dve.tensor_tensor(x2, tmp[2], tmp[3], ALU.add)

            def rotate(mixer, g):
                dve.wait_ge(*t.emptied[2].now())
                dve.wait_ge(*t.emptied[3].now())
                parts = [(g * BANK, 8)]
                if mixer != "swa":
                    parts.append((D + g * BANK, 8))
                elif g == 0:
                    parts.append((D, 2))
                for c0, n in parts:
                    x = qkv[:, :, c0:c0 + n * HEAD].rearrange("p t (h d) -> p t h d", d=HEAD)
                    m = rope(lambda lo, hi: x[:, :, :, lo:hi], n, HALF, cos1[:, :, :], sin1[:, :, :], rope_tmp[:, :])
                    if (c0, n) != parts[-1]:
                        chain(m)
                if mixer == "swa" and g == 0:
                    chain(m)
                    k = qkv[:, :, 1024:1152].rearrange("p t (g d) -> p t g d", g=2)
                    both = qkv[:, :, 1280:1536].rearrange("p t (g r d) -> p t g r d", g=2, r=2)
                    for r in range(2):
                        m = dve.tensor_copy(both[:, :, :, r, :], k)
                m.then_inc(*t["roped"].one())
                dve.wait_ge(*t["roped"].now())

            def keys_out(mixer, g):
                rows = QK2 if mixer == "mla" else P
                p, pk = head_pairs_of_banks(mixer, g)
                t.filled[p].n += 1
                t.emptied[p].n += 1
                keys = turned_keys(mixer, g)
                if keys:
                    n = len(keys)
                    dve.wait_ge(*t.filled[pk].after())
                    dve.tensor_copy(kT[0:rows, keys[0]:keys[0] + n, :].rearrange("p j n -> p (j n)"),
                                    pair[pk][0:rows, :, :].rearrange("p b n -> p (b n)")[:, 0:n * SEQ])\
                        .then_inc(*t.emptied[pk].one())

            def shifts(mixer, hp):
                b, p = hp % 2, score_pair(mixer, hp)
                dve.wait_ge(*t.filled[p].after())
                t.emptied[p].n += 1
                for tt, cols in ((0, slice(0, P)), (1, slice(P, 3 * P))):
                    dve.tensor_reduce(mx[:, b, :, tt], pair[p][:, :, cols], AXIS.X, ALU.max).then_inc(*t["dve_step"].one())
                step()
                m = mx[:, b, :, :]
                if mixer == "swa":
                    dve.tensor_tensor(m, m, lanes(sinks8[:, 2 * hp:2 * hp + 2].unsqueeze(2), [P, 2, 2]), ALU.max)\
                        .then_inc(*t["dve_step"].one())
                    step()
                ins = dve.tensor_scalar(negm[:, b, :, :], m, -SCALE[mixer], None, ALU.mult)
                if mixer == "swa":
                    ins.then_inc(*t["dve_step"].one())
                    step()
                    ins = dve.tensor_tensor(snk[:, hp, :, :], negm[:, b, :, :],
                                            lanes(sinks[:, 2 * hp:2 * hp + 2].unsqueeze(2), [P, 2, 2]), ALU.add)
                ins.then_inc(*t["shift_ready"].one())

            def probs(hp):
                b = hp % 2
                dve.wait_ge(*t.emptied[0].now())
                chain(dve.reciprocal(rinv[:, hp, :, :], sums[:, hp, :, :]))
                chain(dve.tensor_scalar(rinv[:, hp, 1, :], rinv[:, hp, 1, :], neglam[:, t.lam:t.lam + 1], None, ALU.mult))
                for tt, cols in ((0, slice(0, P)), (1, slice(P, 3 * P))):
                    m = dve.tensor_scalar(pT[:, b, 1, cols], sm[:, b, 1, cols], rinv[:, hp, 1, tt:tt + 1], None, ALU.mult)
                chain(m)
                for tt, cols in ((0, slice(0, P)), (1, slice(P, 3 * P))):
                    m = dve.scalar_tensor_tensor(out=sm[:, b, 0, cols], in0=sm[:, b, 0, cols], scalar=rinv[:, hp, 0, tt:tt + 1],
                                                 in1=pT[:, b, 1, cols], op0=ALU.mult, op1=ALU.add)
                m.then_inc(*t["p_ready"].one())
                dve.wait_ge(*t["p_ready"].now())

            def probs_out(mixer, hp):
                p = score_pair(mixer, hp)
                if mixer == "diff":
                    probs(hp)
                    t.filled[p].n += 1
                    t.emptied[p].n += 1
                else:
                    dve.wait_ge(*t.filled[p].after())
                    dve.tensor_copy(pT[:, hp % 2, :, :], pair[p][:, :, 0:384]).then_inc(*t.emptied[p].one())

            def outputs(mixer, q):
                p = outputs_at(q)
                if mixer == "diff":
                    dve.wait_ge(*t["heads_squared"].after())
                    roots16(4, P, 4 * q).then_inc(*t["rstd16_ready"].one())
                    t.filled[p].n += 1
                    t.emptied[p].n += 1
                    return
                pairs = slice(2 * q, 2 * q + 2)
                if mixer == "swa":
                    dve.wait_ge(*t["sink_ready"].after())
                    chain(dve.tensor_tensor(sums[:, pairs, :, :], sums[:, pairs, :, :], snk[:, pairs, :, :], ALU.add))
                chain(dve.reciprocal(rinv[:, pairs, :, :], sums[:, pairs, :, :]))
                dve.wait_ge(*t.filled[p].after())
                for tt in range(TT):
                    src = pair[1][:, q % 2, :].rearrange("p (j t c d) -> p j t c d", j=2, t=TT, c=2)[:, :, tt]
                    m = dve.tensor_tensor(o_at(mixer, q)[:, tt, :].rearrange("p (j c d) -> p j c d", j=2, c=2), src,
                                          lanes(rinv[:, pairs, :, tt].unsqueeze(3), [P, 2, 2, V2]), ALU.mult)
                m.then_inc(*t.emptied[p].one())

            def mix_tokens(mixer, steps, g_o=None):
                for what, n, *_ in steps:
                    if what == "in_results":
                        c0, w = in_blocks(mixer)[n]
                        if mixer == "swa":
                            biased_results(n)
                        else:
                            results(2 + n % 2, lambda tt: qkv[:, tt, c0:c0 + w], w, lambda tt: rstd[:, tt:tt + 1])
                    elif what == "rope":
                        rotate(mixer, n)
                    elif what == "heads":
                        keys_out(mixer, n)
                    elif what == "scores":
                        shifts(mixer, n)
                    elif what == "turn":
                        probs_out(mixer, n)
                    elif what == "outputs":
                        outputs(mixer, n)
                    elif what == "features":
                        turn_split(range(2 * n, 2 * n + 2), features_at(mixer, n), g_o)
                    elif what == "out_results" and n == 0:
                        used()
                    elif what == "split":
                        split((n,))

            def roots16(n, w, at=0):
                some = slice(at, at + n)
                dve.tensor_scalar(ss16[:, some], ss16[:, some], 1.0 / w, EPS, ALU.mult, ALU.add).then_inc(*t["sum16_ready"].one())
                dve.wait_ge(*t["std16_ready"].after())
                return dve.reciprocal(rstd16[:, some], std16[:, some])

            def add_out(n):
                cols = slice(n * BANK, (n + 1) * BANK)
                dve.tensor_tensor(h[:, :, cols], pair[2 + n][:, :, :], h[:, :, cols], ALU.add).then_inc(*t.emptied[2 + n].one())

            def add_mlp(n):
                cols = slice(n * BANK, (n + 1) * BANK)
                for tt in range(TT):
                    m = dve.scalar_tensor_tensor(out=h[:, tt, cols], in0=pair[2 + n][:, tt, :], scalar=rstd[:, tt:tt + 1],
                                                 in1=h[:, tt, cols], op0=ALU.mult, op1=ALU.add)
                m.then_inc(*t.emptied[2 + n].one())

            def mlp():
                def up(j):
                    b = j % 2
                    used()
                    dve.wait_ge(*t.emptied[b].after())
                    if t["alo_written"].n:
                        dve.wait_ge(*t["alo_written"].now())
                    dve.tensor_tensor(square_at, relu_at[b], relu_at[b], ALU.mult).then_inc(*t["dve_step"].one())
                    dve.wait_ge(*t["ahi_written"].after())
                    step()
                    dve.tensor_tensor(alo[:, b, :, :].rearrange("p f n -> p (f n)"), square_at,
                                      ahi[:, b, :, :].rearrange("p f n -> p (f n)").bitcast(FP32), ALU.subtract)\
                        .then_inc(*t["alo_written"].one())
                    split()

                def down():
                    used()
                    split()

                up(0)
                up(1)
                down()
                per = dict(MLP_TURN, dve_step=2)
                with dve.Fori(0, 3) as i:
                    turns(t, i, per)
                    up(0)
                    down()
                    up(1)
                    down()
                after_turns(t, per, 3, 4)
                del plan[:8]

            def layer_norm(src, dst, g, b, centred):
                for tt in range(TT):
                    m = dve.bn_stats(bn6[:, tt, :], src(tt))
                chain(m)
                for tt in range(TT):
                    m = dve.bn_aggr(bn2[:, tt, :], bn6[:, tt, :])
                chain(m)
                dve.tensor_scalar(var[:, 6:6 + TT], bn2[:, :, 1], EPS, None, ALU.add).then_inc(*t["var_ready"].one())
                dve.wait_ge(*t["std_ready"].after())
                chain(dve.reciprocal(rstd[:, 6:6 + TT], std[:, 6:6 + TT]))
                for tt in range(TT):
                    m = dve.tensor_scalar(dst[:, tt, :], src(tt), bn2[:, tt, 0:1], rstd[:, 6 + tt:7 + tt], ALU.subtract, ALU.mult)
                m.then_inc(*centred.one())
                dve.wait_ge(*centred.now())
                chain(dve.tensor_tensor(dst, dst, lanes(g.unsqueeze(1), [P, TT, 256]), ALU.mult))
                return dve.tensor_tensor(dst, dst, lanes(b.unsqueeze(1), [P, TT, 256]), ALU.add)

            def convolve(layer, taps):
                at = layer * CONV_K * 2
                step()
                for k in taps:
                    w, y = colsA[:, at + 2 * k:at + 2 * k + 1], ypad[:, 0, k:k + SEQ]
                    if k == 0:
                        bias = colsA[:, ROW_AT["conv_b_2"] + 2 * layer:ROW_AT["conv_b_2"] + 2 * layer + 1]
                        m = dve.tensor_scalar(yacc[:, 0, :], y, w, bias, ALU.mult, ALU.add)
                    else:
                        step()
                        m = dve.scalar_tensor_tensor(out=yacc[:, 0, :], in0=y, scalar=w, in1=yacc[:, 0, :],
                                                     op0=ALU.mult, op1=ALU.add)
                    m.then_inc(*t["conv_ready" if k == CONV_K - 1 else "dve_step"].one())

            def prepare(n):
                x, gains, place = ((qbuf, "qk_q_g_2", flat_sm), (kfull, "qk_k_g_2", flat_pT))[n]
                x = x[:, :, :].rearrange("p t (h d) -> p t h d", d=QK2)
                squares = place[:, 0:TT * H2 * QK2].rearrange("p (t h d) -> p t h d", t=TT, d=QK2)
                dve.wait_ge(*t["heads_squared"].after())
                chain(dve.tensor_reduce(ss16[:, 16 * n:16 * n + 16].rearrange("p (t h) -> p t h", t=TT), squares, AXIS.X, ALU.add))
                chain(roots16(16, QK2, 16 * n))
                r = rstd16[:, 16 * n:16 * n + 16].rearrange("p (t h) -> p t h", t=TT).unsqueeze(3)
                chain(dve.tensor_tensor(x, x, lanes(r, [P, TT, H2, QK2]), ALU.mult))
                for tt in range(TT):
                    m = dve.tensor_tensor(x[:, tt], x[:, tt], lanes(param2(gains).unsqueeze(1), [P, H2, QK2]), ALU.mult)
                chain(m)
                rope(lambda lo, hi: x[:, :, :, NOPE + lo:NOPE + hi], H2, HALF2, cs2[:, 0, :, :], cs2[:, 1, :, :], place)\
                    .then_inc(*t["qk_ready"].one())

            def second(layer):
                norm(gain("norm_g_2", layer), add_out if layer else None)
                dve.wait_ge(*t["spread_loaded"].after(16 * len(SPREAD_2)))
                if layer == 0:
                    chain(dve.memset(ypad[:, :, 0:CONV_K - 1], 0.0))
                for what, n, *rest in second_steps():
                    if what == "in_results":
                        used()
                        t.emptied[2 + n % 2].n += 1
                    elif what == "glu":
                        dve.wait_ge(*t["sig_ready"].after())
                        dve.tensor_tensor(qkv[:, :, A0:A0 + CW], qkv[:, :, A0:A0 + CW], qkv[:, :, GLU0:GLU0 + CW], ALU.mult)\
                            .then_inc(*t["glu_ready"].one())
                    elif what == "conv_in":
                        t.filled[0].n += 1
                        dve.wait_ge(*t.emptied[0].after())
                    elif what == "taps":
                        convolve(layer, n)
                    elif what == "latents":
                        turn_split(range(0, 4), 0, gain_latent(layer), (lhi, llo))
                        turn_split(range(4, 8), 1, gain_latent(layer), (lhi, llo))
                        variances([(2, QL), (2, KVL)], at=2)
                    elif what == "conv_norm":
                        dve.wait_ge(*t.filled[4].after())
                        layer_norm(lambda tt: pair[1][:, 0, tt * CW:(tt + 1) * CW], qkv[:, :, 0:CW], param2("conv_ln_g_2"),
                                   param2("conv_ln_b_2"), t.emptied[4]).then_inc(*t["ln_ready"].one())
                    elif what == "prep":
                        prepare(n)
                    elif what == "conv_operand":
                        turn_split(range(2), 5, None, (lhi, llo))
                    elif what == "pw":
                        used()
                        for tt in range(TT):
                            m = dve.tensor_tensor(yacc[:, tt, :], pair[3][:, tt, 0:CW], param2("conv_pw_b_2"), ALU.add)
                        m.then_inc(*t.emptied[3].one())
                        pw_done = t.emptied[3].now()
                    elif what == "branch_gates":
                        dve.wait_ge(*pw_done)
                        dve.wait_ge(*t["zsilu_ready"].after(3))
                        chain(dve.tensor_tensor(qkv[:, :, ZC0:ZC0 + CW], qkv[:, :, ZC0:ZC0 + CW], yacc[:, :, :], ALU.mult))
                        dve.tensor_tensor(qkv[:, :, U0:U0 + SGW], qkv[:, :, U0:U0 + SGW], qkv[:, :, ZS0:ZS0 + SGW], ALU.mult)\
                            .then_inc(*t["branches_ready"].one())
                    elif what == "v_norm":
                        v = qkv[:, :, V0:V0 + SGW]
                        dve.wait_ge(*t["gelu_ready"].after(2))
                        layer_norm(lambda tt: v[:, tt, :], v, param2("sg_ln_g_2"), param2("sg_ln_b_2"), t["dve_step"])\
                            .then_inc(*t["vln_ready"].one())
                    elif what == "sgu_gate":
                        dve.wait_ge(*t.filled[8].after())
                        for g in range(4):
                            u = qkv[:, :, U0 + g * 64:U0 + (g + 1) * 64]
                            at = ROW_AT["sg_b_2"] + layer * 4 + g
                            mixed = pair[3][:, 0, :].rearrange("p (t n) -> p t n", t=TT)[:, :, g * 64:(g + 1) * 64]
                            m = dve.scalar_tensor_tensor(out=u, in0=mixed, scalar=colsB[:, at:at + 1], in1=u,
                                                         op0=ALU.add, op1=ALU.mult)
                        m.then_inc(*t.emptied[8].one())
                        dve.wait_ge(*t.emptied[8].now())
                    elif what == "branches":
                        if n == 1:
                            for q in range(2):
                                dve.wait_ge(*t.emptied[outputs_at(q)].now())
                            dve.tensor_tensor(qbuf[:, :, 0:MLAW], qbuf[:, :, 0:MLAW], qkv[:, :, ZM0:ZM0 + MLAW], ALU.mult)\
                                .then_inc(*t["branches_ready"].one())
                        variances([(TT, CW), (TT, SGW)] if n == 0 else [(TT, MLAW)], at=8 if n == 0 else 2)
                        for i, x in enumerate((0, 2) if n == 0 else (1,)):
                            for tt in range(TT):
                                at = (8 if n == 0 else 2) + 2 * i + tt
                                m = dve.tensor_scalar(branch(x)[:, tt, :], branch(x)[:, tt, :], rstd[:, at:at + 1], None, ALU.mult)
                        m.then_inc(*t["y_ready"].one())
                    elif what == "y":
                        g = gain_branch(layer)
                        if n == 0:
                            turn_split(range(0, 2), 8, g)
                            turn_split(range(2, 4), 9, g)
                        else:
                            turn_split(range(4, 8), 0, g)
                    elif what == "out_results":
                        used()
                    elif what == "split":
                        split((n,))
                    else:
                        mix_tokens("mla", [(what, n, *rest)])

            t.filled[2].n += 1
            dve.wait_ge(*t.emptied[2].after())

            def first_parameters():
                t.filled[3].n += 1
                dve.wait_ge(*t.emptied[3].after())
                dve.wait_ge(sems["params_loaded"], 16 * PARAMS)
                for n in range(2):
                    m = dve.tensor_tensor(lamv[:, 2 * n, :], lamv[:, 2 * n, :], lamv[:, 2 * n + 1, :], ALU.mult)
                chain(m)
                for n in range(2):
                    m = dve.tensor_reduce(lams[:, 2 * n:2 * n + 2], lamv[:, 2 * n, :].rearrange("p (s d) -> p s d", d=HEAD),
                                          AXIS.X, ALU.add)
                chain(m)
                chain(dve.tensor_copy(pos[:, :], pos_i[:, :]))
                for tt in range(TT):
                    m = dve.tensor_scalar(ang[:, tt, :], inv[:, :], pos[:, tt:tt + 1], None, ALU.mult)
                chain(m)
                chain(dve.tensor_scalar(turns_of[:, :, :], ang[:, :, :], 1.0 / (2 * math.pi), ROUND, ALU.mult, ALU.add))
                chain(dve.tensor_scalar(turns_of[:, :, :], turns_of[:, :, :], -ROUND, None, ALU.add))
                for part in TURN_PARTS:
                    chain(dve.scalar_tensor_tensor(out=ang[:, :, :], in0=turns_of[:, :, :], scalar=-part, in1=ang[:, :, :],
                                                   op0=ALU.mult, op1=ALU.add))
                chain(dve.tensor_scalar(cos1[:, :, :], ang[:, :, :], math.pi / 2, None, ALU.add))
                chain(dve.tensor_scalar(turns_of[:, :, :], cos1[:, :, :], math.pi, -2 * math.pi, ALU.is_gt, ALU.mult))
                chain(dve.tensor_tensor(cos1[:, :, :], cos1[:, :, :], turns_of[:, :, :], ALU.add))
                dve.tensor_scalar(sin1[:, :, :], ang[:, :, :], PI_BELOW, -PI_BELOW, ALU.min, ALU.max).then_inc(*t["dve_step"].one())
                dve.tensor_scalar(cos1[:, :, :], cos1[:, :, :], PI_BELOW, -PI_BELOW, ALU.min, ALU.max).then_inc(*t["angles_ready"].one())
                dve.tensor_scalar(sinks8[:, :], sinks[:, :], 1.0 / SCALE["swa"], None, ALU.mult).then_inc(*t["dve_step"].one())
                dve.wait_ge(*t["sines_ready"].after(3))
                chain(dve.tensor_tensor(neglam[:, :], lams[:, 2:4], lams[:, 0:2], ALU.subtract))
                for n, layer in enumerate(LAMBDA_INIT):
                    at = ROW_AT["diff_subln_g"] + n
                    dve.tensor_scalar(neglam[:, n:n + 1], neglam[:, n:n + 1], -LAMBDA_INIT[layer], None, ALU.add)\
                        .then_inc(*t["dve_step"].one())
                    dve.tensor_scalar(subg[:, n:n + 1], colsB[:, at:at + 1], 1.0 - LAMBDA_INIT[layer], None, ALU.mult)\
                        .then_inc(*t["params_ready"].one())
                step()

            for layer, mixer in enumerate(MIXERS):
                t.lam = layer // 3
                norm(gain("attn_norm_g", layer), add_mlp if layer else None, waiting=1 if layer else 2)
                if layer == 0:
                    first_parameters()
                mix_tokens(mixer, mixer_steps(mixer), gain_sub(t.lam) if mixer == "diff" else None)
                norm(gain("mlp_norm_g", layer), add_out, root=False)
                mlp()
            for n in range(2):
                used(1)
                add_mlp(n)
            variances([(TT, D)])
            dve.wait_ge(sems["gains_loaded"], 16)
            for tt in range(TT):
                m = dve.scalar_tensor_tensor(out=h[:, tt, :], in0=h[:, tt, :], scalar=rstd[:, tt:tt + 1], in1=fing,
                                             op0=ALU.mult, op1=ALU.mult)
            m.then_inc(*t["h_ready"].one())
            dve.wait_ge(*t["h_ready"].now())
            for layer in range(DEPTH_2):
                second(layer)
            for n in range(2):
                used(1)
                add_out(n)

        @block.sync
        def _(sp):
            t = tallies()

            def load(src, T, w):
                s = t.block % 2
                if t.block == 0:
                    sp.wait_ge(sems["rows_loaded"], 16 * (len(ROWS_A) + len(ROWS_B)))
                if t.block >= 2:
                    sp.wait_ge(*t["lo_split"].now(2))
                parts = src if isinstance(src, list) else [src]
                n = T // len(parts)
                for i, part in enumerate(parts):
                    sp.dma_start(slot(raw, s, T, w)[:, i * n:(i + 1) * n, :], part).then_inc(*t.loaded[s].one(16))
                t["lo_split"].n += 2
                t.block += 1

            def tiles(w):
                return w.rearrange("(t p) n -> p t n", p=P)

            def loads(mixer, w_in, w_out):
                for n, w in in_blocks(mixer):
                    load(tiles(w_in[:, n:n + w]), KT, w)
                out_loads(w_out)

            def out_loads(w_out):
                for g in range(2):
                    load(tiles(w_out[g * BANK:(g + 1) * BANK, :]), 4, D)

            def mlp_loads(w_up, w_down):
                def up(j):
                    load(tiles(w_up[:, bass.ds(j * BANK, BANK)]), KT, BANK)

                def down(j):
                    load(tiles(w_down[bass.ds(j * BANK, BANK), :]), 4, D)

                up(0)
                up(1)
                down(0)
                with sp.Fori(0, 3) as i:
                    turns(t, i, MLP_TURN)
                    for b in range(2):
                        up(2 * i + 2 + b)
                        down(2 * i + 1 + b)
                after_turns(t, MLP_TURN, 3, 4)
                down(7)

            sp.dma_start(h[:, :, :], a["x"][0].rearrange("(t p) n -> p t n", p=P)).then_inc(*t["x_loaded"].one(16))
            for layer, mixer in enumerate(MIXERS):
                which = layer // 3
                name = {"diff": "diff", "moba": "moba", "swa": "swa"}[mixer]
                loads(mixer, a[f"{name}_w_in"][which], a[f"{name}_w_out"][which])
                mlp_loads(a["mlp_w_up"][layer], a["mlp_w_down"][layer])
            for layer in range(DEPTH_2):
                for weights, c0, T, w in BLOCKS_2:
                    load(tiles(a[weights][layer][:, c0:c0 + w]), T, w)
                w_out = a["w_out_2"][layer]
                load([tiles(w_out[0:CW, :]), tiles(w_out[CW + MLAW:D, :])], 4, D)
                load(tiles(w_out[CW:CW + MLAW, :]), 4, D)
            for n in range(2):
                cols = slice(n * BANK, (n + 1) * BANK)
                sp.wait_ge(sems[f"emptied{2 + n}"], emptied_by_layer[-1][2 + n])
                sp.dma_start(out[0][:, cols].rearrange("(t p) n -> p t n", p=P), h[:, :, cols]).then_inc(*t["stored"].one(16))
            sp.wait_ge(*t["stored"].now())

        @block.gpsimd
        def _(pool):
            t = tallies()
            pool.memset(ident[:, :], 0.0).then_inc(*t["pool_step"].one())
            pool.memset(ident_b[:, :], 0.0).then_inc(*t["pool_step"].one())
            pool.memset(causal[:, :], 0.0).then_inc(*t["pool_step"].one())
            pool.memset(band[:, :], 0.0).then_inc(*t["pool_step"].one())
            pool.wait_ge(*t["pool_step"].now())
            pool.affine_select(out=ident[:, :], in_=ident[:, :], compare_op=ALU.not_equal, fill=1.0, base=0,
                               pattern=[[-1, P]], channel_multiplier=1).then_inc(*t["consts_made"].one())
            pool.affine_select(out=ident_b[:, :], in_=ident_b[:, :], compare_op=ALU.not_equal, fill=1.0, base=0,
                               pattern=[[-1, P]], channel_multiplier=1).then_inc(*t["consts_made"].one())
            for m in (causal, band):
                for at in (0, 2 * P):
                    pool.affine_select(out=m[:, at:at + P], in_=m[:, at:at + P], compare_op=ALU.is_ge, fill=NEG, base=0,
                                       pattern=[[-1, P]], channel_multiplier=1).then_inc(*t["consts_made"].one())
            pool.affine_select(out=band[:, P:2 * P], in_=band[:, P:2 * P], compare_op=ALU.is_gt, fill=NEG, base=0,
                               pattern=[[1, P]], channel_multiplier=-1).then_inc(*t["consts_made"].one())
            for layer in range(DEPTH_2):
                pool.dma_start(wsg[:, layer, :, :], a["sg_w_2"][layer].rearrange("g t s -> t g s"))\
                    .then_inc(*t["mixing_loaded"].one(16))
            pool.dma_start(pos_i[:, :], a["positions"][0].rearrange("(t p) -> p t", p=P),
                           allow_slow_non_contiguous=True).then_inc(*t["params_loaded"].one(16))
            pool.dma_start(inv[:, :], a["inv_freq"].partition_broadcast(P)).then_inc(*t["params_loaded"].one(16))
            for n, key in enumerate(LAMBDAS):
                pool.dma_start(lamv[:, n, :], a[key].rearrange("s d -> (s d)").partition_broadcast(P))\
                    .then_inc(*t["params_loaded"].one(16))
            pool.dma_start(sinks[:, :], a["swa_sinks"][0].partition_broadcast(P)).then_inc(*t["params_loaded"].one(16))
            pool.dma_start(swab[:, :], a["swa_b_in"][0].partition_broadcast(P)).then_inc(*t["params_loaded"].one(16))
            for n, key in enumerate(["cos_2", "sin_2"]):
                pool.dma_start(cs2[:, n, :, :], a[key].rearrange("(t p) n -> p t n", p=P)).then_inc(*t["params_loaded"].one(16))
            pool.wait_ge(*t["mixing_loaded"].now())
            pool.affine_select(out=wsg[:, :, :, :].rearrange("p l g s -> p (l g) s"),
                               in_=wsg[:, :, :, :].rearrange("p l g s -> p (l g) s"), compare_op=ALU.is_ge, fill=0.0, base=0,
                               pattern=[[0, DEPTH_2 * 4], [-1, P]], channel_multiplier=1).then_inc(*t["mixing_masked"].one())
            pool.wait_ge(sems["block_used"], 2 * sum(len(in_blocks(m)) + 2 + 2 * (FF // BANK) for m in MIXERS[:3]))
            pool.dma_start(fing, a["final_norm_g"].partition_broadcast(P)).then_inc(*t["gains_loaded"].one(16))
            for layer in range(DEPTH_2):
                if layer == 0:
                    pool.wait_ge(sems["h_ready"], 1)
                else:
                    for p in (2, 3):
                        pool.wait_ge(sems[f"emptied{p}"], emptied_by_layer[layer - 1][p])
                for name, _ in SPREAD_2:
                    pool.dma_start(param2(name), a[name][layer].partition_broadcast(P)).then_inc(*t["spread_loaded"].one(16))
                pool.wait_ge(*t["channels_ready"].after())
                at = layer * CONV_K * 2 + 1
                for k in range(CONV_K):
                    w, y = colsA[:, at + 2 * k:at + 2 * k + 1], ypad[:, 1, k:k + SEQ]
                    if k == 0:
                        bias = colsA[:, ROW_AT["conv_b_2"] + 2 * layer + 1:ROW_AT["conv_b_2"] + 2 * layer + 2]
                        pool.tensor_scalar(yacc[:, 1, :], y, w, bias, ALU.mult, ALU.add).then_inc(*t["pool_step"].one())
                        continue
                    pool.wait_ge(*t["pool_step"].now())
                    pool.tensor_scalar(tap[:, :], y, w, None, ALU.mult).then_inc(*t["pool_step"].one())
                    pool.wait_ge(*t["pool_step"].now())
                    pool.tensor_tensor(yacc[:, 1, :], yacc[:, 1, :], tap[:, :], ALU.add)\
                        .then_inc(*t["pool_conv_ready" if k == CONV_K - 1 else "pool_step"].one())


_INS = ["x", "positions", "attn_norm_g", "mlp_norm_g", "diff_w_in", "diff_w_out", "diff_lam_q1", "diff_lam_k1", "diff_lam_q2",
        "diff_lam_k2", "diff_subln_g", "moba_w_in", "moba_w_out", "swa_w_in", "swa_b_in", "swa_sinks", "swa_w_out",
        "mlp_w_up", "mlp_w_down", "final_norm_g", "norm_g_2", "w_in_2", "conv_w_2", "conv_b_2", "conv_ln_g_2", "conv_ln_b_2",
        "conv_pw_w_2", "conv_pw_b_2", "q_norm_g_2", "w_uq_2", "kv_norm_g_2", "w_ukv_2", "qk_q_g_2", "qk_k_g_2", "sg_ln_g_2",
        "sg_ln_b_2", "sg_w_2", "sg_b_2", "branch_norm_g_2", "w_out_2"]


def _tables():
    f = np.float32
    inv1 = f(ROPE_THETA) ** (-np.arange(0, 2 * HALF, 2, dtype=f) / f(2 * HALF))
    inv2 = f(10000.0) ** (-np.arange(HALF2, dtype=f) / f(HALF2))
    angle = np.arange(SEQ, dtype=f)[:, None] * inv2[None, :].astype(f)
    return {"inv_freq": inv1.astype(f), "cos_2": np.cos(angle).astype(f), "sin_2": np.sin(angle).astype(f)}


def kernel(**inputs):
    import concourse.bacc as _bacc
    from concourse.bass_utils import run_bass_kernel_spmd as _run

    nc = _bacc.Bacc("TRN2", target_bir_lowering=False, num_devices=1)
    arrays, args = {}, {}
    for name, v in [(n, inputs[n]) for n in _INS] + list(_tables().items()):
        v = np.ascontiguousarray(v)
        arrays[f"in_{name}"] = v
        args[name] = nc.dram_tensor(f"in_{name}", v.shape, mybir.dt.from_np(v.dtype), kind="ExternalInput").ap()
    result = nc.dram_tensor("result", (1, SEQ, D), FP32, kind="ExternalOutput").ap()
    build(nc, args, result)
    r = _run(nc, [arrays], core_ids=[0])
    return r.results[0]["result"]
```
